# Optimizing a Trainium2 kernel written in Bass

```python
import math
import jax, jax.numpy as jnp
from jax import lax
import numpy as np

D_MODEL = 1024
BATCH = 1
SEQ = 128
DEPTH = 2
DEC_BATCH = 1
DEC_SEQ = 512
PAST_LEN = 128

GRID_W = 64
ROPE_BASE = 10000.0
EPS = 1e-6
Q_BLOCK = 128
DA_HEADS = 4
DA_DH = 64
DA_OUT = DA_HEADS * 2 * DA_DH
MLA_HEADS = 8
MLA_Q_RANK = 256
MLA_KV_RANK = 128
MLA_NOPE = 64
MLA_ROPE = 32
MLA_V = 64
MLA_OUT = MLA_HEADS * MLA_V
SWA_HEADS = 8
SWA_KV_HEADS = 2
SWA_DH = 64
WINDOW = 128
W_BLOCK = 128
SWA_OUT = SWA_HEADS * SWA_DH
IN_SIZES = (DA_OUT, DA_OUT, DA_OUT, MLA_Q_RANK, MLA_KV_RANK, MLA_ROPE,
            SWA_HEADS * SWA_DH, SWA_KV_HEADS * SWA_DH, SWA_KV_HEADS * SWA_DH)
IN_COLS = 3 * DA_OUT + MLA_Q_RANK + MLA_KV_RANK + MLA_ROPE + SWA_HEADS * SWA_DH + 2 * SWA_KV_HEADS * SWA_DH
N_EXPERTS = 16
EXPERT_FF = 1024
CAPACITY_FACTOR = 2

kernel_name = 'hybrid_flow_prefix_diffmla_swa_ec'

def rms_norm(x, g):
    xf = x.astype(jnp.float32)
    y = xf * lax.rsqrt(jnp.mean(xf * xf, axis=-1, keepdims=True) + EPS)
    return y.astype(x.dtype) * g

def axial_rope(n_tokens, rot_dim):
    rows = n_tokens // GRID_W
    row = jnp.repeat(jnp.arange(rows, dtype=jnp.float32), GRID_W)
    col = jnp.tile(jnp.arange(GRID_W, dtype=jnp.float32), rows)
    n_freq = rot_dim // 4
    inv = ROPE_BASE ** (-jnp.arange(n_freq, dtype=jnp.float32) / n_freq)
    ang = jnp.concatenate([row[:, None] * inv, col[:, None] * inv], axis=-1)
    return jnp.cos(ang), jnp.sin(ang)

def apply_rope(x, cs):
    cos, sin = cs
    xf = x.astype(jnp.float32).reshape(x.shape[:-1] + (x.shape[-1] // 2, 2))
    x1, x2 = xf[..., 0], xf[..., 1]
    c = cos[None, :, None, :]
    s = sin[None, :, None, :]
    out = jnp.stack([x1 * c - x2 * s, x1 * s + x2 * c], axis=-1).reshape(x.shape)
    return out.astype(x.dtype)

def _q_blocks(t):
    B, S = t.shape[0], t.shape[1]
    return t.reshape((B, S // Q_BLOCK, Q_BLOCK) + t.shape[2:]).swapaxes(0, 1)

def _unblock(o):
    o = o.swapaxes(0, 1)
    return o.reshape((o.shape[0], o.shape[1] * o.shape[2]) + o.shape[3:])

def softmax_attention(q, k, v, scale, sink=None):
    def one(qb):
        s = jnp.einsum('bqhd,bkhd->bhqk', qb, k).astype(jnp.float32) * scale
        if sink is None:
            p = jax.nn.softmax(s, axis=-1)
        else:
            sk = jnp.broadcast_to(sink.astype(jnp.float32)[None, :, None, None], s.shape[:-1] + (1,))
            p = jax.nn.softmax(jnp.concatenate([s, sk], axis=-1), axis=-1)[..., :-1]
        return jnp.einsum('bhqk,bkhd->bqhd', p.astype(v.dtype), v)
    return _unblock(lax.map(one, _q_blocks(q)))

def diff_attention(q1, q2, k1, k2, v, lam, scale):
    def one(qs):
        b1, b2 = qs
        a1 = jax.nn.softmax(jnp.einsum('bqhd,bkhd->bhqk', b1, k1).astype(jnp.float32) * scale, axis=-1)
        a2 = jax.nn.softmax(jnp.einsum('bqhd,bkhd->bhqk', b2, k2).astype(jnp.float32) * scale, axis=-1)
        return jnp.einsum('bhqk,bkhd->bqhd', (a1 - lam * a2).astype(v.dtype), v)
    return _unblock(lax.map(one, (_q_blocks(q1), _q_blocks(q2))))

def window_attention(q, k, v, ck, cv, sink, scale):
    B, N, Hq, dh = q.shape
    Hkv = k.shape[2]
    G = Hq // Hkv
    nb = N // W_BLOCK
    qb = q.reshape(B, nb, W_BLOCK, Hkv, G, dh)
    pad = ((0, 0), (W_BLOCK, W_BLOCK), (0, 0), (0, 0))
    kp, vp = jnp.pad(k, pad), jnp.pad(v, pad)
    idx = jnp.arange(nb)[:, None] * W_BLOCK + jnp.arange(3 * W_BLOCK)[None, :]
    kb, vb = kp[:, idx], vp[:, idx]
    qpos = jnp.arange(N).reshape(nb, W_BLOCK)
    kpos = idx - W_BLOCK
    valid = ((jnp.abs(qpos[:, :, None] - kpos[:, None, :]) <= WINDOW)
             & (kpos[:, None, :] >= 0) & (kpos[:, None, :] < N))
    s_loc = jnp.einsum('bnqhgd,bnjhd->bnhgqj', qb, kb).astype(jnp.float32) * scale
    s_loc = jnp.where(valid[None, :, None, None], s_loc, -jnp.inf)
    s_ctx = jnp.einsum('bnqhgd,bchd->bnhgqc', qb, ck).astype(jnp.float32) * scale
    s_sink = jnp.broadcast_to(sink.astype(jnp.float32).reshape(Hkv, G)[None, None, :, :, None, None],
                              s_loc.shape[:-1] + (1,))
    p = jax.nn.softmax(jnp.concatenate([s_loc, s_ctx, s_sink], axis=-1), axis=-1)
    n_loc = s_loc.shape[-1]
    p_loc = p[..., :n_loc].astype(v.dtype)
    p_ctx = p[..., n_loc:-1].astype(v.dtype)
    o = jnp.einsum('bnhgqj,bnjhd->bnqhgd', p_loc, vb) + jnp.einsum('bnhgqc,bchd->bnqhgd', p_ctx, cv)
    return o.reshape(B, N, Hq, dh)

def mixing_sublayer(h, p, layer, ctx, rope):
    B, S, D = h.shape
    latent = ctx is not None
    offs = np.cumsum(IN_SIZES)[:-1].tolist()
    da_q, da_k, da_v, m_q, m_kv, m_kr, s_q, s_k, s_v = jnp.split(h @ p['w_in'], offs, axis=-1)

    q = da_q.reshape(B, S, DA_HEADS, 2, DA_DH)
    q1, q2 = q[..., 0, :], q[..., 1, :]
    k_own = da_k.reshape(B, S, DA_HEADS, 2 * DA_DH)
    v_own = da_v.reshape(B, S, DA_HEADS, 2 * DA_DH)
    if latent:
        rope64, rope32 = rope
        q1, q2 = apply_rope(q1, rope64), apply_rope(q2, rope64)
        k_lat = jnp.concatenate([apply_rope(k_own[..., :DA_DH], rope64),
                                 apply_rope(k_own[..., DA_DH:], rope64)], axis=-1)
        k_all = jnp.concatenate([ctx[0], k_lat], axis=1)
        v_all = jnp.concatenate([ctx[1], v_own], axis=1)
    else:
        k_all, v_all = k_own, v_own
    lam_init = 0.8 - 0.6 * math.exp(-0.3 * layer)
    lam = (jnp.exp(jnp.sum((p['da_lq1'] * p['da_lk1']).astype(jnp.float32)))
           - jnp.exp(jnp.sum((p['da_lq2'] * p['da_lk2']).astype(jnp.float32))) + lam_init)
    o = diff_attention(q1, q2, k_all[..., :DA_DH], k_all[..., DA_DH:], v_all, lam, DA_DH ** -0.5)
    o_da = (rms_norm(o, p['da_subln']) * (1.0 - lam_init)).reshape(B, S, DA_OUT)

    cq = (rms_norm(m_q, p['mla_q_norm']) @ p['mla_w_qb']).reshape(B, S, MLA_HEADS, MLA_NOPE + MLA_ROPE)
    q_nope, q_rope = cq[..., :MLA_NOPE], cq[..., MLA_NOPE:]
    ckv_own = rms_norm(m_kv, p['mla_kv_norm'])
    kr_own = m_kr
    if latent:
        q_rope = apply_rope(q_rope, rope32)
        kr_lat = apply_rope(kr_own[:, :, None, :], rope32)[:, :, 0]
        ckv_all = jnp.concatenate([ctx[2], ckv_own], axis=1)
        kr_all = jnp.concatenate([ctx[3], kr_lat], axis=1)
    else:
        ckv_all, kr_all = ckv_own, kr_own
    Sk = ckv_all.shape[1]
    kv = (ckv_all @ p['mla_w_kvb']).reshape(B, Sk, MLA_HEADS, MLA_NOPE + MLA_V)
    k_m = jnp.concatenate([kv[..., :MLA_NOPE],
                           jnp.broadcast_to(kr_all[:, :, None, :], (B, Sk, MLA_HEADS, MLA_ROPE))], axis=-1)
    q_m = jnp.concatenate([q_nope, q_rope], axis=-1)
    o_mla = softmax_attention(q_m, k_m, kv[..., MLA_NOPE:], (MLA_NOPE + MLA_ROPE) ** -0.5).reshape(B, S, MLA_OUT)

    q_s = s_q.reshape(B, S, SWA_HEADS, SWA_DH)
    k_s = s_k.reshape(B, S, SWA_KV_HEADS, SWA_DH)
    v_s = s_v.reshape(B, S, SWA_KV_HEADS, SWA_DH)
    if latent:
        o = window_attention(apply_rope(q_s, rope64), apply_rope(k_s, rope64), v_s,
                             ctx[4], ctx[5], p['swa_sink'], SWA_DH ** -0.5)
    else:
        G = SWA_HEADS // SWA_KV_HEADS
        o = softmax_attention(q_s, jnp.repeat(k_s, G, axis=2), jnp.repeat(v_s, G, axis=2),
                              SWA_DH ** -0.5, p['swa_sink'])
    o_swa = o.reshape(B, S, SWA_OUT)

    g_da, g_mla, g_swa = jnp.split(jax.nn.sigmoid(h @ p['w_gate']), 3, axis=-1)
    merged = (g_da * (o_da @ p['w_br_da']) + g_mla * (o_mla @ p['w_br_mla'])
              + g_swa * (o_swa @ p['w_br_swa']))
    own = (k_own, v_own, ckv_own, kr_own, k_s, v_s)
    return merged @ p['w_o'], own

def expert_choice_ffn(h, w_router, w1, w3, w2):
    B, S, D = h.shape
    n_tok = B * S
    cap = CAPACITY_FACTOR * n_tok // N_EXPERTS
    xt = h.reshape(n_tok, D)
    aff = jax.nn.softmax((xt @ w_router).astype(jnp.float32), axis=-1)
    g, idx = lax.top_k(aff.T, cap)
    xe = xt[idx]
    hid = jax.nn.silu(jnp.einsum('ecd,edf->ecf', xe, w1)) * jnp.einsum('ecd,edf->ecf', xe, w3)
    ye = jnp.einsum('ecf,efd->ecd', hid, w2) * g[..., None].astype(h.dtype)
    out = jnp.zeros_like(xt).at[idx.reshape(-1)].add(ye.reshape(-1, D))
    return out.reshape(B, S, D)

def trunk_layer(x, mod, p, layer, ctx, rope):
    shift1, scale1, gate1, shift2, scale2, gate2 = jnp.split(mod, 6, axis=-1)
    h = rms_norm(x, p['norm1']) * (1.0 + scale1) + shift1
    mixed, own = mixing_sublayer(h, p, layer, ctx, rope)
    x = x + gate1 * mixed
    h = rms_norm(x, p['norm2']) * (1.0 + scale2) + shift2
    x = x + gate2 * expert_choice_ffn(h, p['w_router'], p['w_ff1'], p['w_ff3'], p['w_ff2'])
    return x, own

def setup_inputs(seed: int = 0) -> dict:
    key = jax.random.key(seed)
    ks = iter(jax.random.split(key, 48))

    def nrm(shape, scale):
        return jax.random.normal(next(ks), shape, jnp.float32) * scale

    def gain(shape):
        return 1.0 + nrm(shape, 0.05)

    D = D_MODEL
    return {
        'x_prompt': nrm((BATCH, SEQ, D), 1.0),
        'x_sample': nrm((DEC_BATCH, DEC_SEQ, D), 1.0),
        'cache_da_k': nrm((DEC_BATCH, DEPTH, PAST_LEN, DA_HEADS, 2 * DA_DH), 1.0),
        'cache_da_v': nrm((DEC_BATCH, DEPTH, PAST_LEN, DA_HEADS, 2 * DA_DH), 1.0),
        'cache_mla_ckv': nrm((DEC_BATCH, DEPTH, PAST_LEN, MLA_KV_RANK), 1.0),
        'cache_mla_krope': nrm((DEC_BATCH, DEPTH, PAST_LEN, MLA_ROPE), 1.0),
        'cache_swa_k': nrm((DEC_BATCH, DEPTH, PAST_LEN, SWA_KV_HEADS, SWA_DH), 1.0),
        'cache_swa_v': nrm((DEC_BATCH, DEPTH, PAST_LEN, SWA_KV_HEADS, SWA_DH), 1.0),
        'c': nrm((DEC_BATCH, D), 1.0),
        'c_ctx': nrm((D,), 1.0),
        'w_ada': nrm((DEPTH, D, 6 * D), 0.5 * D ** -0.5),
        'b_ada': nrm((DEPTH, 6 * D), 0.01),
        'norm1': gain((DEPTH, D)),
        'norm2': gain((DEPTH, D)),
        'w_in': nrm((DEPTH, D, IN_COLS), D ** -0.5),
        'da_lq1': nrm((DEPTH, DA_DH), 0.1),
        'da_lk1': nrm((DEPTH, DA_DH), 0.1),
        'da_lq2': nrm((DEPTH, DA_DH), 0.1),
        'da_lk2': nrm((DEPTH, DA_DH), 0.1),
        'da_subln': gain((DEPTH, 2 * DA_DH)),
        'mla_q_norm': gain((DEPTH, MLA_Q_RANK)),
        'mla_w_qb': nrm((DEPTH, MLA_Q_RANK, MLA_HEADS * (MLA_NOPE + MLA_ROPE)), MLA_Q_RANK ** -0.5),
        'mla_kv_norm': gain((DEPTH, MLA_KV_RANK)),
        'mla_w_kvb': nrm((DEPTH, MLA_KV_RANK, MLA_HEADS * (MLA_NOPE + MLA_V)), MLA_KV_RANK ** -0.5),
        'swa_sink': nrm((DEPTH, SWA_HEADS), 0.5),
        'w_gate': nrm((DEPTH, D, 3 * D), D ** -0.5),
        'w_br_da': nrm((DEPTH, DA_OUT, D), DA_OUT ** -0.5),
        'w_br_mla': nrm((DEPTH, MLA_OUT, D), MLA_OUT ** -0.5),
        'w_br_swa': nrm((DEPTH, SWA_OUT, D), SWA_OUT ** -0.5),
        'w_o': nrm((DEPTH, D, D), D ** -0.5),
        'w_router': nrm((DEPTH, D, N_EXPERTS), D ** -0.5),
        'w_ff1': nrm((DEPTH, N_EXPERTS, D, EXPERT_FF), D ** -0.5),
        'w_ff3': nrm((DEPTH, N_EXPERTS, D, EXPERT_FF), D ** -0.5),
        'w_ff2': nrm((DEPTH, N_EXPERTS, EXPERT_FF, D), EXPERT_FF ** -0.5),
        'final_norm': gain((D,)),
    }

def reference(x_prompt, x_sample, cache_da_k, cache_da_v, cache_mla_ckv, cache_mla_krope,
              cache_swa_k, cache_swa_v, c, c_ctx, w_ada, b_ada, norm1, norm2, w_in,
              da_lq1, da_lk1, da_lq2, da_lk2, da_subln, mla_q_norm, mla_w_qb, mla_kv_norm,
              mla_w_kvb, swa_sink, w_gate, w_br_da, w_br_mla, w_br_swa, w_o, w_router,
              w_ff1, w_ff3, w_ff2, final_norm):
    n_lat = x_sample.shape[1]
    rope = (axial_rope(n_lat, DA_DH), axial_rope(n_lat, MLA_ROPE))
    xp, xs = x_prompt, x_sample
    new = [[], [], [], [], [], []]
    for l in range(DEPTH):
        p = {'norm1': norm1[l], 'norm2': norm2[l], 'w_in': w_in[l],
             'da_lq1': da_lq1[l], 'da_lk1': da_lk1[l], 'da_lq2': da_lq2[l], 'da_lk2': da_lk2[l],
             'da_subln': da_subln[l], 'mla_q_norm': mla_q_norm[l], 'mla_w_qb': mla_w_qb[l],
             'mla_kv_norm': mla_kv_norm[l], 'mla_w_kvb': mla_w_kvb[l], 'swa_sink': swa_sink[l],
             'w_gate': w_gate[l], 'w_br_da': w_br_da[l], 'w_br_mla': w_br_mla[l],
             'w_br_swa': w_br_swa[l], 'w_o': w_o[l], 'w_router': w_router[l],
             'w_ff1': w_ff1[l], 'w_ff3': w_ff3[l], 'w_ff2': w_ff2[l]}
        mod_ctx = (jax.nn.silu(c_ctx) @ w_ada[l] + b_ada[l])[None, None, :]
        xp, own = trunk_layer(xp, mod_ctx, p, l, None, None)
        for i in range(6):
            new[i].append(own[i])
        mod_lat = (jax.nn.silu(c) @ w_ada[l] + b_ada[l])[:, None, :]
        ctx = (cache_da_k[:, l], cache_da_v[:, l], cache_mla_ckv[:, l], cache_mla_krope[:, l],
               cache_swa_k[:, l], cache_swa_v[:, l])
        xs, _ = trunk_layer(xs, mod_lat, p, l, ctx, rope)
    y_prompt = rms_norm(xp, final_norm)
    y_sample = rms_norm(xs, final_norm)
    return (y_prompt, y_sample, jnp.stack(new[0], axis=1), jnp.stack(new[1], axis=1),
            jnp.stack(new[2], axis=1), jnp.stack(new[3], axis=1), jnp.stack(new[4], axis=1),
            jnp.stack(new[5], axis=1))


_drawn_inputs = setup_inputs


def setup_inputs(seed=0):
    import zlib

    import numpy as np

    out = dict(_drawn_inputs(seed))
    spreads = {}
    factors = {'cache_mla_ckv': 6.365,
     'cache_mla_krope': 8.0,
     'cache_swa_k': 4.6,
     'cache_swa_v': 4.112,
     'b_ada': 3.718,
     'norm2': 3.752,
     'da_lq1': 7.302,
     'da_lk1': 8.0,
     'da_lq2': 7.545,
     'da_lk2': 6.676,
     'da_subln': 6.313,
     'mla_q_norm': 8.0,
     'swa_sink': 8.0}
    for name, (base, spread) in spreads.items():
        noise = np.random.default_rng([zlib.crc32(name.encode()), seed]).standard_normal(out[name].shape)
        drawn = base * np.exp(spread * noise) if base else spread * noise
        out[name] = __import__('jax').numpy.asarray(drawn.astype(out[name].dtype))
    for name, factor in factors.items():
        out[name] = (out[name] * factor).astype(out[name].dtype)
    return out
```

```python
import math
from contextlib import ExitStack

import numpy as np

import concourse.bass as bass
from concourse import mybir

FP32 = mybir.dt.float32
ALU = mybir.AluOpType
ACT = mybir.ActivationFunctionType
AX = mybir.AxisListType

P = 128
D = 1024
KT = D // P
DEPTH = 2
NLAT, NPR, NCTX = 512, 128, 128
T = NLAT + NPR
TT = T // P
PRT = TT - 1
LT = NLAT // P
KEYS = NLAT + NCTX + NPR
KEY_TILES = KEYS // P
GRID_W = 64
ROPE_BASE = 10000.0
EPS = 1e-6
DA_H, DH = 4, 64
QR, KVR, MROPE, MNOPE, MV, MH = 256, 128, 32, 64, 64, 8
MQ = MNOPE + MROPE
SW_H, SW_KV = 8, 2
BR = 512
IN_COLS = 3 * BR + QR + KVR + MROPE + SW_H * DH + 2 * SW_KV * DH
MLA_AT = 3 * BR
SWQ_AT = MLA_AT + QR + KVR + MROPE
SWK_AT = SWQ_AT + SW_H * DH
SWV_AT = SWK_AT + SW_KV * DH
NE, FF = 16, 1024
CAP_L, CAP_P = 2 * NLAT // NE, 2 * NPR // NE
CAP = CAP_L + CAP_P
PAIRS = NE // 2
SLOTS_P = NE * CAP_P
NEG = -1.0e30

RING = 8
HALF = 4
CHUNK = HALF * 512


def _layout(parts):
    at, out = 0, {}
    for name, width in parts:
        out[name] = (at, at + width)
        at += width
    return out, at


CONST, CONST_COLS = _layout([
    ("ident", P), ("swap", P), ("swap32", MROPE), ("ones", P), ("mask_before", P), ("mask_after", P),
    ("iota", CAP_L), ("cos64", NLAT), ("sin64", NLAT), ("cos32", NLAT), ("sin32", NLAT)])

ROWS, NROWS = _layout([
    ("b_ada", 48), ("norm1", KT), ("norm2", KT), ("q_norm", 2), ("kv_norm", 1), ("subln", 1),
    ("final", KT), ("c", KT), ("c_ctx", KT)])


def shape_constants():
    t = np.zeros((P, CONST_COLS), np.float32)

    def put(name, rows, value):
        a, b = CONST[name]
        t[rows, a:b] = value

    p = np.arange(P)
    put("ident", slice(0, P), np.eye(P))
    swap = np.zeros((P, P), np.float32)
    swap[p[1::2], p[0::2]] = -1.0
    swap[p[0::2], p[1::2]] = 1.0
    put("swap", slice(0, P), swap)
    put("swap32", slice(MNOPE, MQ), swap[:MROPE, :MROPE])
    put("ones", slice(0, P), 1.0)
    put("mask_before", slice(0, P), np.where(p[None, :] >= p[:, None], 0.0, NEG))
    put("mask_after", slice(0, P), np.where(p[None, :] <= p[:, None], 0.0, NEG))
    put("iota", slice(0, P), np.arange(CAP_L))
    tok = np.arange(NLAT)
    row, col = (tok // GRID_W).astype(np.float32), (tok % GRID_W).astype(np.float32)

    def angles(rot):
        n = rot // 4
        inv = (np.float32(ROPE_BASE) ** (-np.arange(n, dtype=np.float32) / np.float32(n))).astype(np.float32)
        ang = np.concatenate([row[:, None] * inv, col[:, None] * inv], axis=-1)
        return np.repeat(ang, 2, axis=1).T.astype(np.float32)

    a64 = angles(DH)
    a64 = np.concatenate([a64, a64])
    a32 = angles(MROPE)
    put("cos64", slice(0, P), np.cos(a64))
    put("sin64", slice(0, P), np.sin(a64))
    put("cos32", slice(MNOPE, MQ), np.cos(a32))
    put("sin32", slice(MNOPE, MQ), np.sin(a32))
    lam = np.array([[0.8 - 0.6 * math.exp(-0.3 * l) for l in range(DEPTH)]]).T
    lam = np.concatenate([lam, 1.0 - lam], axis=1).astype(np.float32)
    return t, lam


def layer_chunks():
    out = []

    def block(kind, c0, width=512):
        out.append((kind, 0, c0, width))
        out.append((kind, HALF, c0, width))

    def gates(b, branch):
        for mb in range(2):
            block("gate", b * D + mb * 512)
            out.append((branch, 0, mb * 512, 512))

    for b in range(12):
        block("ada", b * 512)
    for b in range(3):
        block("in", b * BR)
    gates(0, "br_da")
    block("in", MLA_AT, QR + KVR + MROPE)
    out.append(("qb", 0, 0, MH * MQ))
    out.append(("kvb", 0, 0, MH * (MNOPE + MV)))
    gates(1, "br_mla")
    block("in", SWQ_AT)
    block("in", SWK_AT, 2 * SW_KV * DH)
    gates(2, "br_swa")
    for b in range(2):
        block("o", b * 512)
    return out


CHUNKS = layer_chunks()
FIRST = {}
for _i, _c in enumerate(CHUNKS):
    FIRST.setdefault(_c[0], _i)
N_DENSE = len(CHUNKS)
PAIR_CHUNKS = 2 * 12
LAYER_CHUNKS = N_DENSE + PAIRS * PAIR_CHUNKS
PAIR_SLOT = N_DENSE % RING
assert PAIR_CHUNKS % RING == 0
assert LAYER_CHUNKS % RING == PAIR_SLOT


def _turns(parts):
    at, out = 0, {}
    for name, n in parts:
        out[name] = at
        at += n
    return out, at


DA_N, SW_N, MLA_N = TT * DA_H, TT * SW_H, TT * MH
PAIR_MM, PAIR_T, PAIR_O = 8, 2, 8
MM, _mm_dense = _turns([
    ("ada", 12), ("norm1", 1), ("da_q", 4), ("da_k", 4), ("da_rot", 8), ("da_v", TT), ("da_s", 2 * DA_N),
    ("da_out", 16), ("mla_in", 4), ("mla_norm", 2), ("kr_rot", 1), ("mla_v", KEY_TILES),
    ("mla_heads", MLA_N + 3 * MH), ("mla_out", 16), ("sw_q", 4), ("sw_k", 1), ("sw_rot", 5), ("sw_v", TT),
    ("sw_s", SW_N), ("sw_out", 16), ("o", 8), ("norm2", 1), ("router", 1), ("gather_p", 2),
    ("pairs", 0)])
MM["combine_p"] = _mm_dense + PAIRS * PAIR_MM
MM_LAYER = MM["combine_p"] + 1
MM_USES = [(MM_LAYER + 1) // 2, MM_LAYER // 2]
T_BEFORE = TT
TR, _t_dense = _turns([
    ("cols", 1), ("da_ctx", 1), ("da_new", 1), ("da", DA_N + TT), ("mla_ctx", 1), ("mla_new", 1),
    ("mla", MLA_N + TT), ("sw_ctx", 1), ("sw_new", 1), ("sw", SW_N + TT), ("h_tok", TT), ("aff", 1),
    ("pos", 1), ("hot_p", 1), ("pairs", 0)])
TR["ye_p"] = _t_dense + PAIRS * PAIR_T
T_LAYER = TR["ye_p"] + 2
OO, _o_dense = _turns([("da", DA_N), ("mla", MLA_N), ("sw", SW_N), ("pairs", 0)])
O_LAYER = _o_dense + PAIRS * PAIR_O
O_USES = [O_LAYER // 2, O_LAYER // 2]
assert O_LAYER % 2 == 0 and _o_dense % 2 == 0


def mla_s(i):
    h, t = divmod(i, TT)
    return MM["mla_heads"] + 3 + h * (TT + 3) + t + (3 if t >= 2 and h < MH - 1 else 0)


def mla_prep(h):
    return MM["mla_heads"] + (0 if h == 0 else 3 + (h - 1) * (TT + 3) + 2)


def t_order(n, per_tile, every):
    p, o, at = {}, {}, 0
    for s in range(n + 2):
        if 1 <= s <= n:
            p[s - 1] = at
            at += 1
        if every and s >= per_tile + 3 and (s - 3) % per_tile == 0:
            o[(s - 3) // per_tile - 1] = at
            at += 1
    for t in range(TT):
        if t not in o:
            o[t] = at
            at += 1
    return p, o


DA_TP, DA_TO = t_order(DA_N, DA_H, True)
SW_TP, SW_TO = t_order(SW_N, SW_H, True)
MLA_TP, MLA_TO = t_order(MLA_N, MH, False)

NEW_STORES = 4
SMALL_LOADS = 15
NM_LAYER = 2 * DA_N + MLA_N + SW_N
PER_LAYER = {
    "sq_ready": 2 * KT + 3, "sq_used": 2 * (KT - 1) + 1, "var_ready": 4, "r0_ready": 4,
    "scaled": 2 * KT, "h_ready": 2,
}


def build(nc, a):
    ctx = ExitStack()
    with ctx:
        def sb(name, shape):
            return ctx.enter_context(nc.sbuf_tensor(name, shape, FP32))

        def sem(name):
            return ctx.enter_context(nc.semaphore(name))

        ring = [sb(f"ring{i}", [P, HALF, 512]) for i in range(RING)]
        x = sb("x", [P, KT, T])
        h = sb("h", [P, KT, T])
        merged = sb("merged", [P, KT, T])
        tok = merged[:, :, :].rearrange("p k t -> p (k t)").rearrange("p (t c) -> p t c", c=D)
        SCRATCH = 12288
        scratch = sb("scratch", [P, SCRATCH])
        pt = sb("pt", [P, 2, T])
        tmp = [sb(f"tmp{i}", [P, T]) for i in range(3)]
        rstd = tmp_r = sb("rstd", [P, T])
        const = sb("const", [P, CONST_COLS])
        rows = sb("rows", [NROWS, P])
        cols = sb("cols", [P, NROWS])
        mod = sb("mod", [P, 48, 2])
        gain = sb("gain", [P, 2, KT, 2])
        silu_c = sb("silu_c", [P, KT, 2])
        silu_t = sb("silu_t", [P, 2 * KT])
        bc = sb("bc", [P, 4 * DH + SW_H + 2])
        lam = sb("lam", [P, 8])
        ctx_in = sb("ctx_in", [P, 352])
        new_out = sb("new_out", [P, 512])
        stat = sb("stat", [P, 64])
        wr = sb("wr", [P, KT, NE])
        pos_t = sb("pos_t", [P, TT, NE])
        aff = sb("aff", [P, TT, NE])

        def c_(name, rows_=slice(0, P)):
            lo, hi = CONST[name]
            return const[rows_, lo:hi]

        def col(name, k=0):
            lo = ROWS[name][0]
            return cols[:, lo + k:lo + k + 1]

        def view(at, *shape):
            n = int(np.prod(shape))
            assert at + n <= SCRATCH, (at, shape)
            v = scratch[:, at:at + n]
            if len(shape) == 1:
                return v
            if len(shape) == 2:
                return v.rearrange("p (a b) -> p a b", b=shape[1])
            return v.rearrange("p (a b c) -> p a b c", b=shape[1], c=shape[2])

        ident = c_("ident")
        ones = c_("ones")

        da_q, da_k = view(0, 4, T), view(2560, 4, KEYS)
        da_v = view(5632, KEY_TILES, 512)
        da_o = view(8704, 2, 512)
        da_p = [[view(9728 + (2 * i + m) * T, T) for m in range(2)] for i in range(2)]
        da_ctx = view(9728, 512)
        cq, ckv = view(0, 2, T), view(1280, KEYS)
        ml_v = view(2048, KEY_TILES, 512)
        ml_q = [view(5120 + i * T, T) for i in range(2)]
        ml_k = [view(6400 + i * KEYS, KEYS) for i in range(2)]
        ml_otok = view(7936, TT, 512)
        ml_p = [view(10496 + i * T, T) for i in range(2)]
        ml_o = view(2048, 4, T)
        sw_q, sw_kraw = view(0, 4, T), view(2560, KEYS)
        sw_k = view(3328, 2, KEYS)
        sw_v = view(4864, KEY_TILES, SW_KV * DH)
        sw_o = view(5632, 2, 512)
        sw_p = [view(6656 + i * 512, 512) for i in range(2)]
        xe_p = view(0, KT, SLOTS_P)
        ye_p = view(2048, KT, SLOTS_P)
        xe = [view(4096 + i * 640, KT, CAP) for i in range(2)]
        hid = [view(5376 + i * 640, KT, CAP) for i in range(2)]
        ye = view(6656, KT, P)
        ye_tok = view(7680, D)
        hot = view(8704, LT, 2, CAP_L)
        hotw = view(9216, LT, 2, CAP_L)
        hotw_t = view(9728, NLAT)
        hot_p = view(10240, NE, CAP_P)
        hotw_p = view(10496, NE, CAP_P)
        hotw_pt = view(10752, 2, P)
        ye_ptok = view(0, 2, D)
        aff_e, work_e, mask_e = view(4096, T), view(4736, T), view(5376, T)
        cum_e = view(6016, T)
        ones_e, top8 = view(6656, T), view(7296, 8)

        mm = [ctx.enter_context(nc.psum_tensor(f"mm{i}", [P, 1024], FP32)) for i in range(2)]
        tp = ctx.enter_context(nc.psum_tensor("tp", [P, 1024], FP32))
        oo = [ctx.enter_context(nc.psum_tensor(f"oo{i}", [P, 512], FP32)) for i in range(2)]

        slot_in = [sem(f"slot{i}_in") for i in range(RING)]
        chunks_free = sem("chunks_free")
        mm_full = [sem(f"mm{i}_full") for i in range(2)]
        mm_empty = [sem(f"mm{i}_empty") for i in range(2)]
        t_full, t_empty = sem("t_full"), sem("t_empty")
        o_full = [sem(f"o{i}_full") for i in range(2)]
        o_empty = [sem(f"o{i}_empty") for i in range(2)]
        const_in, x_in = sem("const_in"), sem("x_in")
        small_in, ctx_kin, ctx_vin, sw_vin, wr_in = (sem("small_in"), sem("ctx_kin"), sem("ctx_vin"),
                                                     sem("sw_vin"), sem("wr_in"))
        small_free, layer_free = sem("small_free"), sem("layer_free")
        cols_ready, silu_e, silu_ready, mod_ready = (sem("cols_ready"), sem("silu_e"), sem("silu_ready"),
                                                     sem("mod_ready"))
        lam_e, lam_e_done = sem("lam_e"), sem("lam_e_done")
        sq_ready, sq_used, var_ready, r0_ready = sem("sq_ready"), sem("sq_used"), sem("var_ready"), sem("r0_ready")
        scaled, h_ready = sem("scaled"), sem("h_ready")
        da_roped, da_kctx_sent, nm_ready, p_mixed = (sem("da_roped"), sem("da_ctx_done"), sem("nm_ready"),
                                                     sem("p_mixed"))
        new_ready, new_sent, v_sent = sem("new_ready"), sem("new_sent"), sem("v_sent")
        ss_ready, o_ready = sem("ss_ready"), sem("o_ready")
        rs_ln, rs_done = sem("rs_ln"), sem("rs_done")
        e_ready, merged_ready = sem("e_ready"), sem("merged_ready")
        c_normed, kr_ready, mq_roped = sem("c_normed"), sem("kr_ready"), sem("mq_roped")
        sw_kready, sw_roped = sem("sw_kready"), sem("sw_roped")
        sink_in, sink_e = sem("sink_in"), sem("sink_e")
        x_ready = sem("x_ready")
        lg_ready, lg_e, aff_ready, pos_ready = sem("lg_ready"), sem("lg_e"), sem("aff_ready"), sem("pos_ready")
        hotp_ready, hot_ready, hotw_ready = sem("hotp_ready"), sem("hot_ready"), sem("hotw_ready")
        xe_ready, g_e, g_ready, ye_ready = sem("xe_ready"), sem("g_e"), sem("g_ready"), sem("ye_ready")
        y_ready, y_sent = sem("y_ready"), sem("y_sent")
        pe_waited = sem("pe_waited")

        def mm_count(l, j, e):
            n = l * MM_USES[j % 2] + j // 2 + 1
            return n if e is None else n + e * (PAIR_MM // 2)

        def t_count(l, j, e):
            n = l * T_LAYER + (T_BEFORE + j + 1)
            return n if e is None else n + e * PAIR_T

        def o_count(l, j, e):
            n = l * O_USES[j % 2] + j // 2 + 1
            return n if e is None else n + e * (PAIR_O // 2)

        def wait_mm_full(eng, l, j, e=None):
            eng.wait_ge(mm_full[j % 2], mm_count(l, j, e))

        def wait_mm_empty(eng, l, j, e=None):
            eng.wait_ge(mm_empty[j % 2], mm_count(l, j, e))

        def wait_mm_read(eng, l, j, e=None):
            eng.wait_ge(mm_empty[j % 2], mm_count(l, j, e) + 1)

        def wait_t_full(eng, l, j, e=None):
            eng.wait_ge(t_full, t_count(l, j, e))

        def wait_t_empty(eng, l, j, e=None):
            eng.wait_ge(t_empty, t_count(l, j, e))

        def wait_t_read(eng, l, j, e=None):
            eng.wait_ge(t_empty, t_count(l, j, e) + 1)

        def wait_o_full(eng, l, j, e=None):
            eng.wait_ge(o_full[j % 2], o_count(l, j, e))

        def wait_o_empty(eng, l, j, e=None):
            eng.wait_ge(o_empty[j % 2], o_count(l, j, e))

        def chunk_use(l, i, e=None):
            before = LAYER_CHUNKS // RING + (1 if i % RING < LAYER_CHUNKS % RING else 0)
            n = l * before + i // RING + 1
            return n if e is None else n + e * (PAIR_CHUNKS // RING)

        block = ctx.enter_context(nc.Block())

        @block.sync
        def _(sp):
            sp.dma_start(const[:, :], a["const"]).then_inc(const_in, 16)
            sp.dma_start(tok[:, 0:LT, :], a["x_sample"][0].rearrange("(t p) c -> p t c", p=P)).then_inc(x_in, 16)
            sp.dma_start(tok[:, PRT, :], a["x_prompt"][0]).then_inc(x_in, 16)

            def chunk_source(l, kind, k0, c0, width):
                r0 = k0 * P
                if kind == "qb":
                    return a["mla_w_qb"][l].rearrange("(k p) c -> p k c", p=P)
                if kind == "kvb":
                    return a["mla_w_kvb"][l]
                w = {"ada": "w_ada", "in": "w_in", "gate": "w_gate", "br_da": "w_br_da",
                     "br_mla": "w_br_mla", "br_swa": "w_br_swa", "o": "w_o"}[kind]
                return a[w][l, r0:r0 + HALF * P, c0:c0 + width].rearrange("(k p) c -> p k c", p=P)

            def chunk_target(kind, slot, width):
                if kind == "qb":
                    return ring[slot][:, :, :].rearrange("p k c -> p (k c)")[:, 0:2 * MH * MQ].rearrange(
                        "p (k c) -> p k c", k=2)
                if kind == "kvb":
                    return ring[slot][:, :, :].rearrange("p k c -> p (k c)")[:, 0:MH * (MNOPE + MV)]
                return ring[slot][:, :, 0:width]

            with sp.Fori(0, DEPTH) as l:
                sp.wait_ge(small_free, l + 1)
                for name, key, per in (("b_ada", "b_ada", 48), ("norm1", "norm1", KT), ("norm2", "norm2", KT),
                                       ("q_norm", "mla_q_norm", 2), ("kv_norm", "mla_kv_norm", 1),
                                       ("subln", "da_subln", 1)):
                    lo, hi = ROWS[name]
                    sp.dma_start(rows[lo:hi, :], a[key][l].rearrange("(r c) -> r c", c=P)).then_inc(small_in, 16)
                for name, src in (("final", a["final_norm"]), ("c", a["c"][0]), ("c_ctx", a["c_ctx"])):
                    lo, hi = ROWS[name]
                    sp.dma_start(rows[lo:hi, :], src.rearrange("(r c) -> r c", c=P)).then_inc(small_in, 16)
                for i, key in enumerate(("da_lq1", "da_lk1", "da_lq2", "da_lk2")):
                    sp.dma_start(bc[:, i * DH:(i + 1) * DH], a[key][l].partition_broadcast(P)).then_inc(small_in, 16)
                sp.dma_start(bc[:, 4 * DH:4 * DH + SW_H], a["swa_sink"][l].partition_broadcast(P)).then_inc(small_in, 16)
                sp.dma_start(bc[:, 4 * DH + SW_H:], a["lam"][l].partition_broadcast(P)).then_inc(small_in, 16)

                def load(i):
                    kind, k0, c0, width = CHUNKS[i]
                    sp.wait_ge(chunks_free, l * LAYER_CHUNKS + (i + 1))
                    sp.dma_start(chunk_target(kind, i % RING, width),
                                 chunk_source(l, kind, k0, c0, width)).then_inc(slot_in[i % RING], 16)

                for i in range(FIRST["in"]):
                    load(i)
                sp.wait_ge(layer_free, l + 1)
                sp.dma_start(da_ctx, a["cache_da_k"][0, l].rearrange("t h d -> t (h d)")).then_inc(ctx_kin, 16)
                sp.dma_start(ctx_in[:, 0:KVR], a["cache_mla_ckv"][0, l]).then_inc(ctx_kin, 16)
                sp.dma_start(ctx_in[:, KVR + MNOPE:KVR + MQ], a["cache_mla_krope"][0, l]).then_inc(ctx_kin, 16)
                sp.dma_start(ctx_in[:, 224:352], a["cache_swa_k"][0, l].rearrange("t h d -> t (h d)")).then_inc(ctx_kin, 16)
                sp.dma_start(da_v[:, LT, :], a["cache_da_v"][0, l].rearrange("t h d -> t (h d)")).then_inc(ctx_vin, 16)
                sp.dma_start(wr[:, :, :], a["w_router"][l].rearrange("(k p) e -> p k e", p=P)).then_inc(wr_in, 16)
                for i in range(FIRST["in"], FIRST["qb"] + 2):
                    load(i)
                for i in range(FIRST["qb"] + 2, N_DENSE):
                    if i == FIRST["br_swa"] - 6:
                        wait_mm_full(sp, l, MM["mla_out"] + 15)
                        sp.dma_start(sw_v[:, LT, :],
                                     a["cache_swa_v"][0, l].rearrange("t h d -> t (h d)")).then_inc(sw_vin, 16)
                    load(i)

                with sp.Fori(0, PAIRS) as e:
                    i = N_DENSE
                    for half in range(2):
                        for w, c0 in (("w_ff1", 0), ("w_ff3", 0), ("w_ff1", 512), ("w_ff3", 512),
                                      ("w_ff2", 0), ("w_ff2", 512)):
                            for k0 in (0, HALF):
                                sp.wait_ge(chunks_free, l * LAYER_CHUNKS + e * PAIR_CHUNKS + (i + 1))
                                sp.dma_start(ring[i % RING][:, :, :],
                                             a[w][l, 2 * e + half, k0 * P:(k0 + HALF) * P, c0:c0 + 512]
                                             .rearrange("(k p) c -> p k c", p=P)).then_inc(slot_in[i % RING], 16)
                                i += 1
            sp.wait_ge(y_ready, 2)
            sp.dma_start(a["y_sample"][0].rearrange("(t p) c -> p t c", p=P), tok[:, 0:LT, :]).then_inc(y_sent, 16)
            sp.dma_start(a["y_prompt"][0], tok[:, PRT, :]).then_inc(y_sent, 16)
            sp.wait_ge(y_sent, 32)
            sp.wait_ge(new_sent, DEPTH * NEW_STORES * 16)
            sp.wait_ge(v_sent, DEPTH * 2 * 16)

        @block.gpsimd
        def _(pool):
            pool.sem_inc(chunks_free, RING)
            pool.sem_inc(small_free, 1)
            for s in (*mm_empty, t_empty, *o_empty):
                pool.sem_inc(s, 1)

            with pool.Fori(0, DEPTH) as l:
                def consumed(turn, n, e=None):
                    wait_mm_full(pool, l, turn, e)
                    pool.sem_inc(chunks_free, n)

                for b in range(12):
                    consumed(MM["ada"] + b, 2)
                consumed(MM["da_q"] + 3, 2)
                consumed(MM["da_k"] + 3, 2)
                consumed(MM["da_v"] + TT - 1, 2)
                consumed(MM["da_out"] + 7, 3)
                consumed(MM["da_out"] + 15, 3)
                consumed(MM["mla_in"] + 3, 2)
                consumed(mla_prep(MH - 1) + 2, 2)
                consumed(MM["mla_out"] + 7, 3)
                consumed(MM["mla_out"] + 15, 3)
                consumed(MM["sw_q"] + 3, 2)
                consumed(MM["sw_v"] + TT - 1, 2)
                consumed(MM["sw_out"] + 7, 3)
                consumed(MM["sw_out"] + 15, 3)
                consumed(MM["o"] + 3, 2)
                consumed(MM["o"] + 7, 2)
                with pool.Fori(0, PAIRS) as e:
                    for half in range(2):
                        for n in range(2):
                            consumed(MM["pairs"] + 2 + 3 * half + n, 4, e)
                        consumed(MM["pairs"] + 2 + 3 * half + 2, 4, e)

        @block.tensor
        def _(pe):
            pe.wait_ge(const_in, 16)
            pe.wait_ge(x_in, 32)
            for t in range(TT):
                pe.wait_ge(t_empty, t + 1)
                for k in range(KT):
                    last = pe.transpose(tp[:, k * P:(k + 1) * P], tok[:, t, k * P:(k + 1) * P], ident)
                last.then_inc(t_full, 1)

            def product(out, lhs, rhs, terms):
                for n in range(terms):
                    for lo, hi in ((0, 512), (512, T)):
                        last = pe.matmul(out[:, lo:hi], lhs(n), rhs(n)[:, lo:hi],
                                         start=(n == 0), stop=(n == terms - 1))
                return last

            def norm_sum(l, turn, sq0, used0, tiles):
                wait_mm_empty(pe, l, turn)
                for k in range(tiles):
                    pe.wait_ge(sq_ready, l * PER_LAYER["sq_ready"] + (sq0 + k + 1))
                    for lo, hi in ((0, 512), (512, T)):
                        last = pe.matmul(mm[turn % 2][:, lo:hi], ones, tmp[k % 2][:, lo:hi],
                                         start=(k == 0), stop=(k == tiles - 1))
                    last.then_inc(sq_used if k < tiles - 1 else mm_full[turn % 2], 1)

            def wait_chunks(l, i, n, e=None):
                for c in range(i, i + n):
                    pe.wait_ge(slot_in[c % RING], 16 * chunk_use(l, c, e))

            def weight(i, k, c0, c1):
                return ring[(i + k // HALF) % RING][:, k % HALF, c0:c1]

            def branch_out(l, chunk, turn, o_t):
                for m in range(KT):
                    c = chunk + 3 * (m // 4)
                    if m % 4 == 0:
                        wait_chunks(l, c, 3)
                    m0 = (m % 4) * P
                    j = turn + 2 * m
                    wait_mm_empty(pe, l, j)
                    product(mm[j % 2], lambda k: weight(c, k, m0, m0 + P), lambda k: h[:, k, :], KT)\
                        .then_inc(mm_full[j % 2], 1)
                    wait_mm_empty(pe, l, j + 1)
                    product(mm[(j + 1) % 2], lambda k: weight(c + 2, k, m0, m0 + P), lambda k: o_t[:, k, :], 4)\
                        .then_inc(mm_full[(j + 1) % 2], 1)

            def values(l, chunk, turn, c0, width):
                for t in range(TT):
                    j = turn + t
                    wait_mm_empty(pe, l, j)
                    for k in range(KT):
                        last = pe.matmul(mm[j % 2][:, 0:width], h[:, k, t * P:(t + 1) * P],
                                         weight(chunk, k, c0, c0 + width), start=(k == 0), stop=(k == KT - 1))
                    last.then_inc(mm_full[j % 2], 1)

            def attention(l, n, score, tiles, p_ready, probs, v_of, width, tr, t_p, o_base, after):
                for s in range(n + 2):
                    if s < n:
                        score(s)
                    if 1 <= s <= n:
                        i = s - 1
                        p_ready(i)
                        j = tr + t_p[i]
                        wait_t_empty(pe, l, j)
                        for b in range(tiles(i)):
                            last = pe.transpose(tp[:, b * P:(b + 1) * P], probs(i)[:, b * P:(b + 1) * P], ident)
                        last.then_inc(t_full, 1)
                    if s >= 2:
                        i = s - 2
                        o = o_base + i
                        wait_t_read(pe, l, tr + t_p[i])
                        wait_o_empty(pe, l, o)
                        for b in range(tiles(i)):
                            last = pe.matmul(oo[o % 2][:, 0:width], pt[:, i % 2, b * P:(b + 1) * P], v_of(i, b),
                                             start=(b == 0), stop=(b == tiles(i) - 1))
                        last.then_inc(o_full[o % 2], 1)
                    after(s)

            def turn_outputs(l, j, o_tok, ready, n):
                pe.wait_ge(ready, n)
                wait_t_empty(pe, l, j)
                for k in range(4):
                    last = pe.transpose(tp[:, k * P:(k + 1) * P], o_tok[:, k * P:(k + 1) * P], ident)
                last.then_inc(t_full, 1)

            def latent_keys(t):
                return [(0, 512, 0), (512, T, 512)] if t < LT else [(T, KEYS, 0)]

            def window(t):
                lo, hi = max(t - 1, 0), min(t + 1, LT - 1)
                return lo, hi

            def window_tiles(t):
                if t == PRT:
                    return 1
                lo, hi = window(t)
                return hi - lo + 2

            with pe.Fori(0, DEPTH) as l:
                pe.wait_ge(small_in, l * SMALL_LOADS * 16 + SMALL_LOADS * 16)
                wait_t_empty(pe, l, TR["cols"])
                pe.transpose(tp[:, 0:NROWS], rows[:, :], ident[0:NROWS, 0:NROWS]).then_inc(t_full, 1)
                pe.wait_ge(silu_ready, l + 1)
                for b in range(12):
                    j = MM["ada"] + b
                    wait_chunks(l, 2 * b, 2)
                    wait_mm_empty(pe, l, j)
                    for m in range(4):
                        for k in range(KT):
                            last = pe.matmul(mm[j % 2][:, 2 * m:2 * m + 2], weight(2 * b, k, m * P, (m + 1) * P),
                                             silu_c[:, k, :], start=(k == 0), stop=(k == KT - 1))
                    last.then_inc(mm_full[j % 2], 1)
                norm_sum(l, MM["norm1"], 0, 0, KT)

                pe.wait_ge(ctx_kin, l * 64 + 64)
                wait_t_empty(pe, l, TR["da_ctx"])
                for m in range(4):
                    last = pe.transpose(tp[:, m * P:(m + 1) * P], da_ctx[:, m * P:(m + 1) * P], ident)
                last.then_inc(t_full, 1)
                pe.wait_ge(h_ready, l * 2 + 1)
                c = FIRST["in"]
                for name, cc in (("da_q", c), ("da_k", c + 2)):
                    wait_chunks(l, cc, 2)
                    for m in range(4):
                        j = MM[name] + m
                        wait_mm_empty(pe, l, j)
                        product(mm[j % 2], lambda k: weight(cc, k, m * P, (m + 1) * P), lambda k: h[:, k, :], KT)\
                            .then_inc(mm_full[j % 2], 1)
                for m in range(8):
                    src = da_q[:, m, 0:NLAT] if m < 4 else da_k[:, m - 4, 0:NLAT]
                    j = MM["da_rot"] + m
                    wait_mm_read(pe, l, (MM["da_q"] if m < 4 else MM["da_k"] - 4) + m)
                    wait_mm_empty(pe, l, j)
                    pe.matmul(mm[j % 2][:, 0:NLAT], c_("swap"), src, start=True, stop=True).then_inc(mm_full[j % 2], 1)
                wait_chunks(l, c + 4, 2)
                values(l, c + 4, MM["da_v"], 0, 512)
                wait_t_empty(pe, l, TR["da_new"])
                for m in range(4):
                    last = pe.transpose(tp[:, m * P:(m + 1) * P], da_k[:, m, T:KEYS], ident)
                last.then_inc(t_full, 1)
                pe.wait_ge(da_roped, l + 1)
                wait_t_read(pe, l, TR["da_ctx"])
                pe.wait_ge(ctx_vin, l * 16 + 16)
                wait_mm_read(pe, l, MM["da_v"] + TT - 1)
                wait_mm_read(pe, l, MM["da_v"] + TT - 2)

                def da_score(i):
                    t, hd = divmod(i, DA_H)
                    for m in range(2):
                        j = MM["da_s"] + 2 * i + m
                        r = slice(m * DH, (m + 1) * DH)
                        wait_mm_empty(pe, l, j)
                        for lo, hi, at in latent_keys(t):
                            last = pe.matmul(mm[j % 2][:, at:at + hi - lo], da_q[r, hd, t * P:(t + 1) * P],
                                             da_k[r, hd, lo:hi], start=True, stop=True)
                        last.then_inc(mm_full[j % 2], 1)

                def da_values(i, b):
                    t, hd = divmod(i, DA_H)
                    return da_v[:, b if t < LT else PRT + 1, hd * P:(hd + 1) * P]

                def da_after(s):
                    for t in range(TT):
                        if s == DA_H * (t + 1) + 3:
                            turn_outputs(l, TR["da"] + DA_TO[t], da_o[:, t % 2, :], o_ready, l * 3 * TT + (t + 1))

                attention(l, DA_N, da_score, lambda i: 5 if i // DA_H < LT else 1,
                          lambda i: pe.wait_ge(p_mixed, l * DA_N + (i + 1)), lambda i: da_p[i % 2][0],
                          da_values, P, TR["da"], DA_TP, OO["da"], da_after)
                turn_outputs(l, TR["da"] + DA_TO[PRT], da_o[:, PRT % 2, :], o_ready, l * 3 * TT + TT)
                wait_t_read(pe, l, TR["da"] + DA_TO[PRT])
                branch_out(l, FIRST["br_da"] - 2, MM["da_out"], da_q)

                wait_t_empty(pe, l, TR["mla_ctx"])
                pe.transpose(tp[:, 0:P], ctx_in[:, 0:KVR], ident)
                pe.transpose(tp[0:MQ, P:2 * P], ctx_in[:, KVR:KVR + MQ], ident).then_inc(t_full, 1)
                c = FIRST["qb"] - 2
                wait_chunks(l, c, 2)
                for m in range(4):
                    j = MM["mla_in"] + m
                    wait_mm_empty(pe, l, j)
                    if m < 3:
                        product(mm[j % 2], lambda k: weight(c, k, m * P, (m + 1) * P), lambda k: h[:, k, :], KT)\
                            .then_inc(mm_full[j % 2], 1)
                    else:
                        product(mm[j % 2][MNOPE:MQ, :], lambda k: weight(c, k, 3 * P, 3 * P + MROPE),
                                lambda k: h[:, k, :], KT).then_inc(mm_full[j % 2], 1)
                norm_sum(l, MM["mla_norm"], KT, KT - 1, 2)
                norm_sum(l, MM["mla_norm"] + 1, KT + 2, KT, 1)
                j = MM["kr_rot"]
                wait_mm_read(pe, l, MM["mla_in"] + 3)
                wait_mm_empty(pe, l, j)
                pe.sem_inc(pe_waited, 1)
                pe.matmul(mm[j % 2][MNOPE:MQ, 0:NLAT], c_("swap32", slice(MNOPE, MQ)), ml_k[0][MNOPE:MQ, 0:NLAT],
                          start=True, stop=True).then_inc(mm_full[j % 2], 1)
                pe.wait_ge(c_normed, l * 2 + 2)
                wait_t_read(pe, l, TR["mla_ctx"])
                wait_chunks(l, FIRST["qb"], 2)
                wqb = ring[FIRST["qb"] % RING][:, :, :].rearrange("p k c -> p (k c)")[:, 0:2 * MH * MQ].rearrange(
                    "p (k c) -> p k c", k=2)
                wkvb = ring[FIRST["kvb"] % RING][:, :, :].rearrange("p k c -> p (k c)")[:, 0:MH * (MNOPE + MV)].rearrange(
                    "p (h c) -> p h c", h=MH)
                for t in range(KEY_TILES):
                    j = MM["mla_v"] + t
                    wait_mm_empty(pe, l, j)
                    pe.matmul(mm[j % 2][:, 0:512], ckv[:, t * P:(t + 1) * P], wkvb[:, :, MNOPE:],
                              start=True, stop=True).then_inc(mm_full[j % 2], 1)

                def project_head(hd):
                    j = mla_prep(hd)
                    wait_mm_empty(pe, l, j)
                    product(mm[j % 2][0:MQ, :], lambda k: wqb[:, k, hd * MQ:(hd + 1) * MQ], lambda k: cq[:, k, :], 2)\
                        .then_inc(mm_full[j % 2], 1)
                    wait_mm_empty(pe, l, j + 1)
                    for lo, hi in ((0, 512), (512, KEYS)):
                        last = pe.matmul(mm[(j + 1) % 2][0:MNOPE, lo:hi], wkvb[:, hd, 0:MNOPE], ckv[:, lo:hi],
                                         start=True, stop=True)
                    last.then_inc(mm_full[(j + 1) % 2], 1)
                    wait_mm_read(pe, l, j)
                    wait_mm_empty(pe, l, j + 2)
                    pe.sem_inc(pe_waited, 1)
                    pe.matmul(mm[(j + 2) % 2][MNOPE:MQ, 0:NLAT], c_("swap32", slice(MNOPE, MQ)),
                              ml_q[hd % 2][MNOPE:MQ, 0:NLAT], start=True, stop=True)\
                        .then_inc(mm_full[(j + 2) % 2], 1)

                pe.wait_ge(kr_ready, l + 1)
                wait_t_empty(pe, l, TR["mla_new"])
                pe.transpose(tp[:, 0:P], ckv[:, T:KEYS], ident)
                pe.transpose(tp[:, P:P + MROPE], ml_k[0][MNOPE:MQ, T:KEYS],
                             ident[MNOPE:MQ, MNOPE:MQ]).then_inc(t_full, 1)
                project_head(0)
                wait_mm_read(pe, l, MM["mla_v"] + KEY_TILES - 1)
                wait_mm_read(pe, l, MM["mla_v"] + KEY_TILES - 2)

                def mla_score(i):
                    hd, t = divmod(i, TT)
                    if t == 2 and hd < MH - 1:
                        project_head(hd + 1)
                    if t == 0:
                        wait_mm_read(pe, l, mla_prep(hd) + 1)
                        pe.wait_ge(mq_roped, l * MH + (hd + 1))
                    j = mla_s(i)
                    wait_mm_empty(pe, l, j)
                    for lo, hi, at in latent_keys(t):
                        last = pe.matmul(mm[j % 2][:, at:at + hi - lo], ml_q[hd % 2][0:MQ, t * P:(t + 1) * P],
                                         ml_k[hd % 2][0:MQ, lo:hi], start=True, stop=True)
                    last.then_inc(mm_full[j % 2], 1)

                attention(l, MLA_N, mla_score, lambda i: 5 if i % TT < LT else 1,
                          lambda i: wait_mm_read(pe, l, mla_s(i)), lambda i: ml_p[i % 2],
                          lambda i, b: ml_v[:, b if i % TT < LT else PRT + 1, (i // TT) * MV:(i // TT + 1) * MV],
                          MV, TR["mla"], MLA_TP, OO["mla"], lambda s: None)
                for t in range(TT):
                    turn_outputs(l, TR["mla"] + MLA_TO[t], ml_otok[:, t, :], o_ready, l * 3 * TT + 2 * TT)
                wait_t_read(pe, l, TR["mla"] + MLA_TO[TT - 1])
                branch_out(l, FIRST["br_mla"] - 2, MM["mla_out"], ml_o)

                wait_t_empty(pe, l, TR["sw_ctx"])
                pe.transpose(tp[:, 0:P], ctx_in[:, 224:352], ident).then_inc(t_full, 1)
                c = FIRST["br_swa"] - 6
                wait_chunks(l, c, 2)
                for m in range(4):
                    j = MM["sw_q"] + m
                    wait_mm_empty(pe, l, j)
                    product(mm[j % 2], lambda k: weight(c, k, m * P, (m + 1) * P), lambda k: h[:, k, :], KT)\
                        .then_inc(mm_full[j % 2], 1)
                wait_chunks(l, c + 2, 2)
                j = MM["sw_k"]
                wait_mm_empty(pe, l, j)
                product(mm[j % 2], lambda k: weight(c + 2, k, 0, P), lambda k: h[:, k, :], KT).then_inc(mm_full[j % 2], 1)
                for m in range(5):
                    src = sw_q[:, m, 0:NLAT] if m < 4 else sw_kraw[:, 0:NLAT]
                    j = MM["sw_rot"] + m
                    wait_mm_read(pe, l, MM["sw_q"] + m)
                    wait_mm_empty(pe, l, j)
                    pe.matmul(mm[j % 2][:, 0:NLAT], c_("swap"), src, start=True, stop=True).then_inc(mm_full[j % 2], 1)
                values(l, c + 2, MM["sw_v"], P, SW_KV * DH)
                wait_t_empty(pe, l, TR["sw_new"])
                pe.transpose(tp[:, 0:P], sw_kraw[:, T:KEYS], ident).then_inc(t_full, 1)
                pe.wait_ge(sw_roped, l + 1)
                pe.wait_ge(sw_vin, l * 16 + 16)
                wait_mm_read(pe, l, MM["sw_v"] + TT - 1)
                wait_mm_read(pe, l, MM["sw_v"] + TT - 2)

                def sw_score(i):
                    t, hd = divmod(i, SW_H)
                    r = slice((hd % 2) * DH, (hd % 2 + 1) * DH)
                    g = hd // (SW_H // SW_KV)
                    j = MM["sw_s"] + i
                    out = mm[j % 2]
                    q = sw_q[r, hd // 2, t * P:(t + 1) * P]
                    wait_mm_empty(pe, l, j)
                    if t == PRT:
                        last = pe.matmul(out[:, 0:P], q, sw_k[r, g, T:KEYS], start=True, stop=True)
                    else:
                        lo, hi = window(t)
                        n = (hi - lo + 1) * P
                        pe.matmul(out[:, 0:n], q, sw_k[r, g, lo * P:(hi + 1) * P], start=True, stop=False)
                        masks = [(0, "mask_before")] * (t > 0) + [(n - P, "mask_after")] * (t < LT - 1)
                        for at, name in masks:
                            pe.matmul(out[:, at:at + P], ident, c_(name), start=False,
                                      stop=(name == masks[-1][1]))
                        last = pe.matmul(out[:, n:n + P], q, sw_k[r, g, NLAT:T], start=True, stop=True)
                    last.then_inc(mm_full[j % 2], 1)

                def sw_values(i, b):
                    t, hd = divmod(i, SW_H)
                    g = hd // (SW_H // SW_KV)
                    if t == PRT:
                        tile = PRT + 1
                    else:
                        lo, hi = window(t)
                        tile = lo + b if b <= hi - lo else LT
                    return sw_v[:, tile, g * DH:(g + 1) * DH]

                def sw_after(s):
                    for t in range(TT):
                        if s == SW_H * (t + 1) + 3:
                            turn_outputs(l, TR["sw"] + SW_TO[t], sw_o[:, t % 2, :], o_ready,
                                         l * 3 * TT + (2 * TT + t + 1))

                attention(l, SW_N, sw_score, lambda i: window_tiles(i // SW_H),
                          lambda i: wait_mm_read(pe, l, MM["sw_s"] + i), lambda i: sw_p[i % 2],
                          sw_values, DH, TR["sw"], SW_TP, OO["sw"], sw_after)
                turn_outputs(l, TR["sw"] + SW_TO[PRT], sw_o[:, PRT % 2, :], o_ready, l * 3 * TT + 3 * TT)
                wait_t_read(pe, l, TR["sw"] + SW_TO[PRT])
                branch_out(l, FIRST["br_swa"] - 2, MM["sw_out"], sw_q)

                pe.wait_ge(merged_ready, l * 3 + 3)
                for m in range(KT):
                    c = FIRST["o"] + 2 * (m // 4)
                    if m % 4 == 0:
                        wait_chunks(l, c, 2)
                    j = MM["o"] + m
                    wait_mm_empty(pe, l, j)
                    product(mm[j % 2], lambda k: weight(c, k, (m % 4) * P, (m % 4 + 1) * P),
                            lambda k: merged[:, k, :], KT).then_inc(mm_full[j % 2], 1)

                norm_sum(l, MM["norm2"], KT + 3, KT, KT)
                pe.wait_ge(h_ready, l * 2 + 2)
                pe.wait_ge(wr_in, l * 16 + 16)
                j = MM["router"]
                wait_mm_empty(pe, l, j)
                for t in range(TT):
                    for k in range(KT):
                        last = pe.matmul(mm[j % 2][:, t * NE:(t + 1) * NE], h[:, k, t * P:(t + 1) * P], wr[:, k, :],
                                         start=(k == 0), stop=(k == KT - 1))
                last.then_inc(mm_full[j % 2], 1)
                for t in range(TT):
                    wait_t_empty(pe, l, TR["h_tok"] + t)
                    for k in range(KT):
                        last = pe.transpose(tp[:, k * P:(k + 1) * P], h[:, k, t * P:(t + 1) * P], ident)
                    last.then_inc(t_full, 1)
                pe.wait_ge(aff_ready, l + 1)
                wait_t_empty(pe, l, TR["aff"])
                for t in range(TT):
                    last = pe.transpose(tp[0:NE, t * P:(t + 1) * P], aff[:, t, :], ident)
                last.then_inc(t_full, 1)
                pe.wait_ge(pos_ready, l + 1)
                wait_t_empty(pe, l, TR["pos"])
                pe.sem_inc(pe_waited, 1)
                for t in range(TT):
                    last = pe.transpose(tp[:, t * NE:(t + 1) * NE], cum_e[0:NE, t * P:(t + 1) * P], ident[0:NE, 0:NE])
                last.then_inc(t_full, 1)
                pe.wait_ge(hotp_ready, l + 1)
                wait_t_read(pe, l, TR["h_tok"] + TT - 1)
                for g in range(2):
                    j = MM["gather_p"] + g
                    wait_mm_empty(pe, l, j)
                    for k in range(4):
                        last = pe.matmul(mm[j % 2][:, k * SLOTS_P:(k + 1) * SLOTS_P],
                                         tok[:, PRT, (4 * g + k) * P:(4 * g + k + 1) * P],
                                         hot_p.rearrange("p e s -> p (e s)"), start=True, stop=True)
                    last.then_inc(mm_full[j % 2], 1)
                wait_t_empty(pe, l, TR["hot_p"])
                for g in range(2):
                    last = pe.transpose(tp[:, g * P:(g + 1) * P],
                                        hotw_p.rearrange("p e s -> p (e s)")[:, g * P:(g + 1) * P], ident)
                last.then_inc(t_full, 1)

                with pe.Fori(0, PAIRS) as e:
                    base = MM["pairs"]
                    pe.wait_ge(hot_ready, l * PAIRS + e + 1)
                    for g in range(2):
                        j = base + g
                        wait_mm_empty(pe, l, j, e)
                        for k in range(4):
                            for t in range(LT):
                                last = pe.matmul(mm[j % 2][:, k * P:(k + 1) * P],
                                                 tok[:, t, (4 * g + k) * P:(4 * g + k + 1) * P],
                                                 hot[:, t, :, :].rearrange("p a s -> p (a s)"),
                                                 start=(t == 0), stop=(t == LT - 1))
                        last.then_inc(mm_full[j % 2], 1)
                    pe.wait_ge(hotw_ready, l * PAIRS + e + 1)
                    wait_t_empty(pe, l, TR["pairs"], e)
                    for t in range(LT):
                        last = pe.transpose(tp[:, t * P:(t + 1) * P], hotw[:, t, :, :].rearrange("p a s -> p (a s)"), ident)
                    last.then_inc(t_full, 1)
                    pe.wait_ge(xe_ready, l * PAIRS + e + 1)
                    for half in range(2):
                        c = N_DENSE + 12 * half
                        for n in range(2):
                            j = base + 2 + 3 * half + n
                            wait_chunks(l, c + 4 * n, 2, e)
                            wait_mm_empty(pe, l, j, e)
                            for w in range(2):
                                if w == 1:
                                    wait_chunks(l, c + 4 * n + 2, 2, e)
                                for m in range(4):
                                    at = w * 512 + m * CAP
                                    for k in range(KT):
                                        last = pe.matmul(mm[j % 2][:, at:at + CAP],
                                                         weight(c + 4 * n + 2 * w, k, m * P, (m + 1) * P),
                                                         xe[half][:, k, :], start=(k == 0), stop=(k == KT - 1))
                            last.then_inc(mm_full[j % 2], 1)
                        j = base + 2 + 3 * half + 2
                        wait_mm_empty(pe, l, j, e)
                        pe.wait_ge(g_ready, (l * PAIRS + e) * 4 + (2 * half + 2))
                        for n in range(2):
                            wait_chunks(l, c + 8 + 2 * n, 2, e)
                            for m in range(4):
                                at = n * 512 + m * CAP
                                for k in range(KT):
                                    last = pe.matmul(mm[j % 2][:, at:at + CAP],
                                                     weight(c + 8 + 2 * n, k, m * P, (m + 1) * P),
                                                     hid[half][:, k, :], start=(k == 0), stop=(k == KT - 1))
                        last.then_inc(mm_full[j % 2], 1)
                    wait_mm_read(pe, l, base + 2 + 3 + 2, e)
                    wait_t_empty(pe, l, TR["pairs"] + 1, e)
                    for k in range(KT):
                        last = pe.transpose(tp[:, k * P:(k + 1) * P], ye[:, k, :], ident)
                    last.then_inc(t_full, 1)
                    wait_t_read(pe, l, TR["pairs"] + 1, e)
                    for k in range(KT):
                        j = OO["pairs"] + k
                        wait_o_empty(pe, l, j, e)
                        pe.matmul(oo[j % 2][:, :], ye_tok[:, k * P:(k + 1) * P], hotw_t, start=True, stop=True)\
                            .then_inc(o_full[j % 2], 1)

                for g in range(2):
                    wait_t_empty(pe, l, TR["ye_p"] + g)
                    for k in range(KT):
                        last = pe.transpose(tp[:, k * P:(k + 1) * P], ye_p[:, k, g * P:(g + 1) * P], ident)
                    last.then_inc(t_full, 1)
                wait_t_read(pe, l, TR["ye_p"] + 1)
                j = MM["combine_p"]
                wait_mm_empty(pe, l, j)
                for k in range(KT):
                    for g in range(2):
                        last = pe.matmul(mm[j % 2][:, k * P:(k + 1) * P], ye_ptok[:, g, k * P:(k + 1) * P],
                                         hotw_pt[:, g, :], start=(g == 0), stop=(g == 1))
                last.then_inc(mm_full[j % 2], 1)

            norm_sum(DEPTH, 0, 0, 0, KT)
            pe.wait_ge(h_ready, DEPTH * 2 + 1)
            for t in range(TT):
                wait_t_empty(pe, DEPTH, t)
                for k in range(KT):
                    last = pe.transpose(tp[:, k * P:(k + 1) * P], h[:, k, t * P:(t + 1) * P], ident)
                last.then_inc(t_full, 1)

        @block.scalar
        def _(act):
            def copy(out, in_, scale=1.0):
                return act.activation(out, in_, ACT.Copy, scale=scale)

            def squares(l, tiles, sq0, used0, src):
                for k in range(tiles):
                    if k >= 2:
                        act.wait_ge(sq_used, l * PER_LAYER["sq_used"] + (used0 + k - 1))
                    act.activation(tmp[k % 2][:, :], src(k), ACT.Square).then_inc(sq_ready, 1)

            def first_rstd(l, n):
                act.wait_ge(var_ready, l * PER_LAYER["var_ready"] + (n + 1))
                act.activation(rstd[:, :], tmp[2][:, :], ACT.Ln)
                act.drain()
                act.activation(rstd[:, :], rstd[:, :], ACT.Exp, scale=-0.5).then_inc(r0_ready, 1)

            def shifts(l, n, shift):
                for k in range(KT):
                    act.wait_ge(scaled, l * PER_LAYER["scaled"] + (n * KT + k + 1))
                    act.activation(h[:, k, 0:NLAT], h[:, k, 0:NLAT], ACT.Identity, bias=mod[:, shift + k, 0:1])
                    last = act.activation(h[:, k, NLAT:T], h[:, k, NLAT:T], ACT.Identity, bias=mod[:, shift + k, 1:2])
                last.then_inc(h_ready, 1)

            def gates(l, turn):
                for m in range(KT):
                    j = turn + 2 * m
                    wait_mm_full(act, l, j)
                    if m >= 2:
                        wait_mm_read(act, l, j - 3)
                    act.activation(tmp[m % 2][:, :], mm[j % 2][:, 0:T], ACT.Exp, scale=-1.0).then_inc(mm_empty[j % 2], 1)

            def exps(l, i0, i, j, out, width, sum_at):
                act.wait_ge(nm_ready, l * NM_LAYER + (i0 + i + 1))
                wait_mm_full(act, l, j)
                act.activation(out, mm[j % 2][:, 0:width], ACT.Exp, bias=stat[:, sum_at:sum_at + 1],
                               accum_out=stat[:, sum_at + 16:sum_at + 17])

            with act.Fori(0, DEPTH) as l:
                act.wait_ge(cols_ready, l + 1)
                lo, hi = ROWS["c"][0], ROWS["c_ctx"][1]
                act.activation(silu_t[:, :], cols[:, lo:hi], ACT.Exp, scale=-1.0).then_inc(silu_e, 1)
                act.wait_ge(lam_e, l + 1)
                act.activation(lam[:, 2:4], lam[:, 0:2], ACT.Exp).then_inc(lam_e_done, 1)
                act.wait_ge(x_ready, l * 2 + 1)
                squares(l, KT, 0, 0, lambda k: x[:, k, :])
                first_rstd(l, 0)
                shifts(l, 0, 0)

                wait_t_full(act, l, TR["da_ctx"])
                copy(da_k[:, :, NLAT:T], tp[:, 0:512].rearrange("p (m t) -> p m t", m=4)).then_inc(t_empty, 1)
                for m in range(4):
                    j = MM["da_q"] + m
                    wait_mm_full(act, l, j)
                    copy(da_q[:, m, :], mm[j % 2][:, 0:T], DH ** -0.5).then_inc(mm_empty[j % 2], 1)
                for m in range(4):
                    j = MM["da_k"] + m
                    wait_mm_full(act, l, j)
                    copy(da_k[:, m, 0:NLAT], mm[j % 2][:, 0:NLAT])
                    copy(da_k[:, m, T:KEYS], mm[j % 2][:, NLAT:T]).then_inc(mm_empty[j % 2], 1)
                for t in range(TT):
                    j = MM["da_v"] + t
                    wait_mm_full(act, l, j)
                    copy(da_v[:, t if t < LT else PRT + 1, :], mm[j % 2][:, 0:512]).then_inc(mm_empty[j % 2], 1)
                wait_mm_read(act, l, MM["da_v"] + TT - 1)
                act.dma_start(a["new_da_v"][0, l].rearrange("t h d -> t (h d)"), da_v[:, PRT + 1, :]).then_inc(v_sent, 16)
                wait_t_full(act, l, TR["da_new"])
                copy(new_out[:, :], tp[:, 0:512]).then_inc(t_empty, 1)
                wait_t_read(act, l, TR["da_new"])
                act.dma_start(a["new_da_k"][0, l].rearrange("t h d -> t (h d)"), new_out[:, :]).then_inc(new_sent, 16)

                def turn_probs(l, j, i, n):
                    wait_t_full(act, l, j)
                    copy(pt[:, i % 2, 0:n * P], tp[:, 0:n * P]).then_inc(t_empty, 1)

                def turn_out_da(t):
                    wait_t_full(act, l, TR["da"] + DA_TO[t])
                    copy(da_q[:, :, t * P:(t + 1) * P], tp[:, 0:512].rearrange("p (m t) -> p m t", m=4),
                         lam[:, 7:8]).then_inc(t_empty, 1)

                def keep_squares(i):
                    o = OO["da"] + i
                    wait_o_full(act, l, o)
                    act.activation(rstd[:, 0:P], oo[o % 2][:, 0:P], ACT.Square,
                                   accum_out=stat[:, 32 + i % 8:33 + i % 8])
                    act.drain()
                    act.sem_inc(ss_ready, 1)
                    if i % DA_H == DA_H - 1:
                        t = i // DA_H
                        s0 = 32 + (t % 2) * 4
                        act.wait_ge(rs_ln, l * TT + (t + 1))
                        act.activation(stat[:, s0 + 8:s0 + 12], stat[:, s0:s0 + 4], ACT.Ln)
                        act.drain()
                        act.activation(stat[:, s0 + 8:s0 + 12], stat[:, s0 + 8:s0 + 12], ACT.Exp, scale=-0.5)\
                            .then_inc(rs_done, 1)

                for s in range(DA_N + 2):
                    if s < DA_N:
                        width = T if s // DA_H < LT else P
                        for m in range(2):
                            j = MM["da_s"] + 2 * s + m
                            exps(l, 0, 2 * s + m, j, da_p[s % 2][m][:, 0:width], width, 2 * (s % 4) + m)
                            act.drain()
                            act.sem_inc(mm_empty[j % 2], 1)
                    if 1 <= s <= DA_N:
                        turn_probs(l, TR["da"] + DA_TP[s - 1], s - 1, 5 if (s - 1) // DA_H < LT else 1)
                    if s >= 2:
                        keep_squares(s - 2)
                    for t in range(TT):
                        if s == DA_H * (t + 1) + 3:
                            turn_out_da(t)
                turn_out_da(PRT)
                gates(l, MM["da_out"])

                act.wait_ge(merged_ready, l * 3 + 1)
                act.wait_ge(v_sent, l * 32 + 16)
                wait_t_full(act, l, TR["mla_ctx"])
                copy(ckv[:, NLAT:T], tp[:, 0:P])
                copy(ml_k[0][MNOPE:MQ, NLAT:T], tp[MNOPE:MQ, P:2 * P]).then_inc(t_empty, 1)
                for m in range(2):
                    j = MM["mla_in"] + m
                    wait_mm_full(act, l, j)
                    copy(cq[:, m, :], mm[j % 2][:, 0:T]).then_inc(mm_empty[j % 2], 1)
                j = MM["mla_in"] + 2
                wait_mm_full(act, l, j)
                copy(ckv[:, 0:NLAT], mm[j % 2][:, 0:NLAT])
                copy(ckv[:, T:KEYS], mm[j % 2][:, NLAT:T]).then_inc(mm_empty[j % 2], 1)
                j = MM["mla_in"] + 3
                wait_mm_full(act, l, j)
                copy(ml_k[0][MNOPE:MQ, 0:NLAT], mm[j % 2][MNOPE:MQ, 0:NLAT])
                copy(ml_k[0][MNOPE:MQ, T:KEYS], mm[j % 2][MNOPE:MQ, NLAT:T]).then_inc(mm_empty[j % 2], 1)
                act.drain()
                squares(l, 2, KT, KT - 1, lambda k: cq[:, k, :])
                first_rstd(l, 1)
                act.wait_ge(c_normed, l * 2 + 1)
                act.activation(tmp[0][:, 0:NLAT], ckv[:, 0:NLAT], ACT.Square)
                act.activation(tmp[0][:, NLAT:T], ckv[:, T:KEYS], ACT.Square).then_inc(sq_ready, 1)
                first_rstd(l, 2)
                for t in range(KEY_TILES):
                    j = MM["mla_v"] + t
                    wait_mm_full(act, l, j)
                    copy(ml_v[:, t, :], mm[j % 2][:, 0:512]).then_inc(mm_empty[j % 2], 1)
                wait_t_full(act, l, TR["mla_new"])
                act.wait_ge(new_sent, l * NEW_STORES * 16 + 16)
                copy(new_out[:, 0:P + MROPE], tp[:, 0:P + MROPE]).then_inc(t_empty, 1)
                wait_t_read(act, l, TR["mla_new"])
                act.dma_start(a["new_mla_ckv"][0, l], new_out[:, 0:P]).then_inc(new_sent, 16)
                act.dma_start(a["new_mla_krope"][0, l], new_out[:, P:P + MROPE]).then_inc(new_sent, 16)

                def head_in(hd):
                    j = mla_prep(hd)
                    wait_mm_full(act, l, j)
                    copy(ml_q[hd % 2][0:MQ, :], mm[j % 2][0:MQ, 0:T], MQ ** -0.5).then_inc(mm_empty[j % 2], 1)
                    j += 1
                    wait_mm_full(act, l, j)
                    copy(ml_k[hd % 2][0:MNOPE, :], mm[j % 2][0:MNOPE, 0:KEYS]).then_inc(mm_empty[j % 2], 1)

                head_in(0)
                for s in range(MLA_N + 2):
                    if s < MLA_N:
                        hd, t = divmod(s, TT)
                        if t == 2 and hd < MH - 1:
                            head_in(hd + 1)
                        width = T if t < LT else P
                        j = mla_s(s)
                        exps(l, 2 * DA_N, s, j, ml_p[s % 2][:, 0:width], width, s % 8)
                        act.drain()
                        act.sem_inc(mm_empty[j % 2], 1)
                    if 1 <= s <= MLA_N and s % 2 == 0:
                        turn_probs(l, TR["mla"] + MLA_TP[s - 1], s - 1, 5 if (s - 1) % TT < LT else 1)
                for t in range(TT):
                    wait_t_full(act, l, TR["mla"] + MLA_TO[t])
                    copy(ml_o[:, :, t * P:(t + 1) * P],
                         tp[:, 0:512].rearrange("p (m t) -> p m t", m=4)).then_inc(t_empty, 1)
                gates(l, MM["mla_out"])

                act.wait_ge(merged_ready, l * 3 + 2)
                wait_t_full(act, l, TR["sw_ctx"])
                copy(sw_kraw[:, NLAT:T], tp[:, 0:P]).then_inc(t_empty, 1)
                for m in range(4):
                    j = MM["sw_q"] + m
                    wait_mm_full(act, l, j)
                    copy(sw_q[:, m, :], mm[j % 2][:, 0:T], DH ** -0.5).then_inc(mm_empty[j % 2], 1)
                j = MM["sw_k"]
                wait_mm_full(act, l, j)
                copy(sw_kraw[:, 0:NLAT], mm[j % 2][:, 0:NLAT])
                copy(sw_kraw[:, T:KEYS], mm[j % 2][:, NLAT:T]).then_inc(mm_empty[j % 2], 1)
                for t in range(TT):
                    j = MM["sw_v"] + t
                    wait_mm_full(act, l, j)
                    copy(sw_v[:, t if t < LT else PRT + 1, :], mm[j % 2][:, 0:SW_KV * DH]).then_inc(mm_empty[j % 2], 1)
                wait_mm_read(act, l, MM["sw_v"] + TT - 1)
                act.dma_start(a["new_swa_v"][0, l].rearrange("t h d -> t (h d)"), sw_v[:, PRT + 1, :]).then_inc(v_sent, 16)
                wait_t_full(act, l, TR["sw_new"])
                act.wait_ge(new_sent, l * NEW_STORES * 16 + 48)
                copy(new_out[:, 0:P], tp[:, 0:P]).then_inc(t_empty, 1)
                wait_t_read(act, l, TR["sw_new"])
                act.dma_start(a["new_swa_k"][0, l].rearrange("t h d -> t (h d)"), new_out[:, 0:P]).then_inc(new_sent, 16)

                def win_tiles(t):
                    return 1 if t == PRT else min(t + 1, LT - 1) - max(t - 1, 0) + 2

                for s in range(SW_N + 2):
                    if s < SW_N:
                        t, hd = divmod(s, SW_H)
                        width = win_tiles(t) * P
                        j = MM["sw_s"] + s
                        exps(l, 2 * DA_N + MLA_N, s, j, sw_p[s % 2][:, 0:width], width, hd)
                        act.drain()
                        act.sem_inc(mm_empty[j % 2], 1)
                        if hd == SW_H - 1:
                            act.wait_ge(sink_in, l * TT + (t + 1))
                            act.activation(stat[:, 40:48], stat[:, 32:40], ACT.Exp).then_inc(sink_e, 1)
                    if 1 <= s <= SW_N and s % 2 == 0:
                        turn_probs(l, TR["sw"] + SW_TP[s - 1], s - 1, win_tiles((s - 1) // SW_H))
                    for t in range(TT):
                        if s == SW_H * (t + 1) + 3:
                            wait_t_full(act, l, TR["sw"] + SW_TO[t])
                            copy(sw_q[:, :, t * P:(t + 1) * P],
                                 tp[:, 0:512].rearrange("p (m t) -> p m t", m=4)).then_inc(t_empty, 1)
                wait_t_full(act, l, TR["sw"] + SW_TO[PRT])
                copy(sw_q[:, :, PRT * P:T], tp[:, 0:512].rearrange("p (m t) -> p m t", m=4)).then_inc(t_empty, 1)
                gates(l, MM["sw_out"])

                act.wait_ge(new_sent, l * NEW_STORES * 16 + NEW_STORES * 16)
                act.wait_ge(x_ready, l * 2 + 2)
                squares(l, KT, KT + 3, KT, lambda k: x[:, k, :])
                first_rstd(l, 3)
                shifts(l, 1, 24)
                act.wait_ge(lg_ready, l + 1)
                act.activation(aff[:, :, :], aff[:, :, :], ACT.Exp).then_inc(lg_e, 1)
                for t in range(TT):
                    wait_t_full(act, l, TR["h_tok"] + t)
                    copy(tok[:, t, :], tp[:, :]).then_inc(t_empty, 1)
                for g in range(2):
                    j = MM["gather_p"] + g
                    wait_mm_full(act, l, j)
                    copy(xe_p[:, 4 * g:4 * g + 4, :],
                         mm[j % 2][:, :].rearrange("p (k s) -> p k s", k=4)).then_inc(mm_empty[j % 2], 1)
                wait_t_full(act, l, TR["hot_p"])
                copy(hotw_pt.rearrange("p g s -> p (g s)"), tp[:, 0:2 * P]).then_inc(t_empty, 1)

                with act.Fori(0, PAIRS) as e:
                    wait_t_full(act, l, TR["pairs"], e)
                    copy(hotw_t, tp[:, 0:NLAT]).then_inc(t_empty, 1)
                    for half in range(2):
                        for n in range(2):
                            j = MM["pairs"] + 2 + 3 * half + n
                            wait_mm_full(act, l, j, e)
                            act.activation(tmp[n][:, 0:4 * CAP], mm[j % 2][:, 0:4 * CAP], ACT.Exp, scale=-1.0)\
                                .then_inc(g_e, 1)
                    wait_t_full(act, l, TR["pairs"] + 1, e)
                    copy(ye_tok, tp[:, :]).then_inc(t_empty, 1)
                for g in range(2):
                    wait_t_full(act, l, TR["ye_p"] + g)
                    copy(ye_ptok[:, g, :], tp[:, :]).then_inc(t_empty, 1)

            act.wait_ge(x_ready, DEPTH * 2 + 1)
            squares(DEPTH, KT, 0, 0, lambda k: x[:, k, :])
            first_rstd(DEPTH, 0)
            for t in range(TT):
                wait_t_full(act, DEPTH, t)
                copy(tok[:, t, :], tp[:, :]).then_inc(t_empty, 1)
            act.drain()
            act.sem_inc(y_ready, 2)

        @block.vector
        def _(dve):
            def tt(out, in0, in1, op):
                return dve.tensor_tensor(out, in0, in1, op)

            def ts(out, in0, s1, op0, s2=None, op1=None):
                if op1 is None:
                    return dve.tensor_scalar(out, in0, s1, None, op0)
                return dve.tensor_scalar(out, in0, s1, s2, op0, op1)

            def stt(out, in0, s, in1, op0, op1):
                return dve.scalar_tensor_tensor(out=out, in0=in0, scalar=s, in1=in1, op0=op0, op1=op1)

            groups = ((0, NLAT, 0), (NLAT, T, 1))

            def refine_rstd(l, turn, n, width):
                wait_mm_full(dve, l, turn)
                ts(tmp[2][:, :], mm[turn % 2][:, 0:T], 1.0 / width, ALU.mult, EPS, ALU.add).then_inc(var_ready, 1)
                dve.drain()
                dve.sem_inc(mm_empty[turn % 2], 1)
                dve.wait_ge(r0_ready, l * PER_LAYER["r0_ready"] + (n + 1))
                tt(tmp[2][:, :], tmp[2][:, :], rstd[:, :], ALU.mult)
                dve.drain()
                tt(tmp[2][:, :], tmp[2][:, :], rstd[:, :], ALU.mult)
                dve.drain()
                ts(tmp[2][:, :], tmp[2][:, :], -0.5, ALU.mult, 1.5, ALU.add)
                dve.drain()
                tt(rstd[:, :], rstd[:, :], tmp[2][:, :], ALU.mult)
                dve.drain()

            def scale_h(n):
                for k in range(KT):
                    for lo, hi, g in groups:
                        last = stt(h[:, k, lo:hi], x[:, k, lo:hi], gain[:, n, k, g:g + 1], rstd[:, lo:hi],
                                   ALU.mult, ALU.mult)
                    last.then_inc(scaled, 1)

            def rope(l, j, dst, rows_, cos, sin):
                wait_mm_full(dve, l, j)
                tt(tmp[j % 2][rows_, 0:NLAT], mm[j % 2][rows_, 0:NLAT], sin, ALU.mult).then_inc(mm_empty[j % 2], 1)
                tt(dst, dst, cos, ALU.mult)
                dve.drain()
                return tt(dst, dst, tmp[j % 2][rows_, 0:NLAT], ALU.add)

            def merge(l, turn, first):
                for m in range(KT):
                    t_ = tmp[m % 2]
                    wait_mm_read(dve, l, turn + 2 * m)
                    ts(t_[:, :], t_[:, :], 1.0, ALU.add)
                    dve.drain()
                    dve.reciprocal(t_[:, :], t_[:, :])
                    dve.drain()
                    j = turn + 2 * m + 1
                    wait_mm_full(dve, l, j)
                    if first:
                        tt(merged[:, m, :], mm[j % 2][:, 0:T], t_[:, :], ALU.mult)
                    else:
                        tt(t_[:, :], mm[j % 2][:, 0:T], t_[:, :], ALU.mult)
                        dve.drain()
                        tt(merged[:, m, :], merged[:, m, :], t_[:, :], ALU.add)
                    dve.drain()
                    dve.sem_inc(mm_empty[j % 2], 1)
                dve.sem_inc(merged_ready, 1)

            def neg_max(l, j, width, at):
                wait_mm_full(dve, l, j)
                return dve.tensor_reduce(stat[:, at:at + 1], mm[j % 2][:, 0:width], AX.X, ALU.max, negate=True)

            def turn_probs(l, j, i, n):
                wait_t_full(dve, l, j)
                dve.tensor_copy(pt[:, i % 2, 0:n * P], tp[:, 0:n * P]).then_inc(t_empty, 1)

            for t in range(TT):
                dve.wait_ge(t_full, t + 1)
                dve.tensor_copy(x[:, :, t * P:(t + 1) * P],
                                tp[:, :].rearrange("p (k t) -> p k t", k=KT)).then_inc(t_empty, 1)
            dve.memset(ctx_in[:, :], 0.0)
            dve.drain()
            dve.sem_inc(x_ready, 1)
            dve.sem_inc(layer_free, 1)

            with dve.Fori(0, DEPTH) as l:
                wait_t_full(dve, l, TR["cols"])
                dve.tensor_copy(cols[:, :], tp[:, 0:NROWS])
                dve.drain()
                dve.sem_inc(t_empty, 1)
                dve.sem_inc(cols_ready, 1)
                dve.wait_ge(silu_e, l + 1)
                ts(silu_t[:, :], silu_t[:, :], 1.0, ALU.add)
                dve.drain()
                dve.reciprocal(silu_t[:, :], silu_t[:, :])
                dve.drain()
                for g, name in enumerate(("c", "c_ctx")):
                    lo, hi = ROWS[name]
                    last = tt(silu_c[:, :, g], silu_t[:, g * KT:(g + 1) * KT], cols[:, lo:hi], ALU.mult)
                last.then_inc(silu_ready, 1)
                tt(bc[:, 0:DH], bc[:, 0:DH], bc[:, DH:2 * DH], ALU.mult)
                tt(bc[:, 2 * DH:3 * DH], bc[:, 2 * DH:3 * DH], bc[:, 3 * DH:4 * DH], ALU.mult)
                dve.drain()
                dve.tensor_reduce(lam[:, 0:2], bc[:, 0:4 * DH].rearrange("p (g d) -> p g d", g=2)[:, :, 0:DH],
                                  AX.X, ALU.add).then_inc(lam_e, 1)
                dve.wait_ge(lam_e_done, l + 1)
                tt(lam[:, 4:5], lam[:, 3:4], lam[:, 2:3], ALU.subtract)
                dve.drain()
                tt(lam[:, 5:6], lam[:, 4:5], bc[:, 4 * DH + SW_H:4 * DH + SW_H + 1], ALU.subtract)
                tt(lam[:, 7:8], col("subln"), bc[:, 4 * DH + SW_H + 1:4 * DH + SW_H + 2], ALU.mult)
                b0 = ROWS["b_ada"][0]
                for b in range(12):
                    j = MM["ada"] + b
                    wait_mm_full(dve, l, j)
                    tt(mod[:, 4 * b:4 * b + 4, :], mm[j % 2][:, 0:8].rearrange("p (m g) -> p m g", g=2),
                       cols[:, b0 + 4 * b:b0 + 4 * b + 4].unsqueeze(2).to_broadcast([P, 4, 2]), ALU.add)\
                        .then_inc(mm_empty[j % 2], 1)
                dve.drain()
                for n, name in enumerate(("norm1", "norm2")):
                    lo, hi = ROWS[name]
                    for g in range(2):
                        stt(gain[:, n, :, g], mod[:, 24 * n + 8:24 * n + 16, g], 1.0, cols[:, lo:hi],
                            ALU.add, ALU.mult)
                dve.drain()
                refine_rstd(l, MM["norm1"], 0, D)
                scale_h(0)

                for m in range(8):
                    dst = da_q[:, m, 0:NLAT] if m < 4 else da_k[:, m - 4, 0:NLAT]
                    last = rope(l, MM["da_rot"] + m, dst, slice(0, P), c_("cos64"), c_("sin64"))
                last.then_inc(da_roped, 1)

                def mix(i):
                    width = T if i // DA_H < LT else P
                    s0 = 16 + 2 * (i % 4)
                    for m in range(2):
                        wait_mm_read(dve, l, MM["da_s"] + 2 * i + m)
                    dve.reciprocal(stat[:, s0:s0 + 2], stat[:, s0:s0 + 2])
                    dve.drain()
                    p1, p2 = da_p[i % 2][0][:, 0:width], da_p[i % 2][1][:, 0:width]
                    ts(p2, p2, stat[:, s0 + 1:s0 + 2], ALU.mult, lam[:, 5:6], ALU.mult)
                    dve.drain()
                    stt(p1, p1, stat[:, s0:s0 + 1], p2, ALU.mult, ALU.add).then_inc(p_mixed, 1)

                def da_keep(i):
                    t, hd = divmod(i, DA_H)
                    o = OO["da"] + i
                    dve.wait_ge(ss_ready, l * DA_N + (i + 1))
                    dve.tensor_copy(da_o[:, t % 2, hd * P:(hd + 1) * P], oo[o % 2][:, 0:P]).then_inc(o_empty[o % 2], 1)
                    if hd == DA_H - 1:
                        s0 = 32 + (t % 2) * 4
                        ts(stat[:, s0:s0 + 4], stat[:, s0:s0 + 4], 1.0 / P, ALU.mult, EPS, ALU.add).then_inc(rs_ln, 1)
                        r0 = stat[:, s0 + 8:s0 + 12]
                        v = stat[:, s0:s0 + 4]
                        dve.drain()
                        dve.wait_ge(rs_done, l * TT + (t + 1))
                        tt(v, v, r0, ALU.mult)
                        dve.drain()
                        tt(v, v, r0, ALU.mult)
                        dve.drain()
                        ts(v, v, -0.5, ALU.mult, 1.5, ALU.add)
                        dve.drain()
                        tt(r0, r0, v, ALU.mult)
                        dve.drain()
                        o_ = da_o[:, t % 2, :].rearrange("p (h d) -> p h d", h=DA_H)
                        tt(o_, o_, r0.unsqueeze(2).to_broadcast([P, DA_H, P]), ALU.mult).then_inc(o_ready, 1)

                for s in range(DA_N + 2):
                    if 1 <= s <= DA_N:
                        mix(s - 1)
                    if s < DA_N:
                        for m in range(2):
                            neg_max(l, MM["da_s"] + 2 * s + m, T if s // DA_H < LT else P, 2 * (s % 4) + m)\
                                .then_inc(nm_ready, 1)
                    if s >= 2:
                        da_keep(s - 2)
                merge(l, MM["da_out"], True)

                refine_rstd(l, MM["mla_norm"], 1, QR)
                for m in range(2):
                    last = stt(cq[:, m, :], cq[:, m, :], col("q_norm", m), rstd[:, :], ALU.mult, ALU.mult)
                last.then_inc(c_normed, 1)
                dve.drain()
                refine_rstd(l, MM["mla_norm"] + 1, 2, KVR)
                stt(ckv[:, 0:NLAT], ckv[:, 0:NLAT], col("kv_norm"), rstd[:, 0:NLAT], ALU.mult, ALU.mult)
                stt(ckv[:, T:KEYS], ckv[:, T:KEYS], col("kv_norm"), rstd[:, NLAT:T], ALU.mult, ALU.mult)\
                    .then_inc(c_normed, 1)
                r32 = slice(MNOPE, MQ)
                wait_t_read(dve, l, TR["mla_ctx"])
                rope(l, MM["kr_rot"], ml_k[0][r32, 0:NLAT], r32, c_("cos32", r32), c_("sin32", r32))
                dve.drain()
                dve.tensor_copy(ml_k[1][r32, :], ml_k[0][r32, :]).then_inc(kr_ready, 1)

                def rope_head(hd):
                    rope(l, mla_prep(hd) + 2, ml_q[hd % 2][r32, 0:NLAT], r32, c_("cos32", r32), c_("sin32", r32))\
                        .then_inc(mq_roped, 1)

                def mla_keep(i):
                    hd, t = divmod(i, TT)
                    o = OO["mla"] + i
                    s0 = 16 + i % 8
                    dve.reciprocal(stat[:, s0:s0 + 1], stat[:, s0:s0 + 1])
                    dve.drain()
                    wait_o_full(dve, l, o)
                    ts(ml_otok[:, t, hd * MV:(hd + 1) * MV], oo[o % 2][:, 0:MV], stat[:, s0:s0 + 1], ALU.mult)\
                        .then_inc(o_empty[o % 2], 1)

                rope_head(0)
                for s in range(MLA_N + 2):
                    if s < MLA_N:
                        hd, t = divmod(s, TT)
                        if t == 2 and hd < MH - 1:
                            rope_head(hd + 1)
                        neg_max(l, mla_s(s), T if t < LT else P, s % 8).then_inc(nm_ready, 1)
                    if 1 <= s <= MLA_N and s % 2 == 1:
                        turn_probs(l, TR["mla"] + MLA_TP[s - 1], s - 1, 5 if (s - 1) % TT < LT else 1)
                    if s >= 2:
                        wait_mm_read(dve, l, mla_s(s - 2))
                        mla_keep(s - 2)
                dve.drain()
                dve.sem_inc(o_ready, TT)
                merge(l, MM["mla_out"], False)

                for m in range(5):
                    dst = sw_q[:, m, 0:NLAT] if m < 4 else sw_kraw[:, 0:NLAT]
                    rope(l, MM["sw_rot"] + m, dst, slice(0, P), c_("cos64"), c_("sin64"))
                dve.drain()
                wait_t_read(dve, l, TR["sw_ctx"])
                for g in range(2):
                    for half in range(2):
                        last = dve.tensor_copy(sw_k[half * DH:(half + 1) * DH, g, :], sw_kraw[g * DH:(g + 1) * DH, :])
                last.then_inc(sw_roped, 1)
                sinks = bc[:, 4 * DH:4 * DH + SW_H]
                ts(stat[:, 48:56], sinks, -1.0, ALU.mult)
                dve.drain()

                def win_tiles(t):
                    return 1 if t == PRT else min(t + 1, LT - 1) - max(t - 1, 0) + 2

                def sw_keep(i):
                    t, hd = divmod(i, SW_H)
                    o = OO["sw"] + i
                    wait_o_full(dve, l, o)
                    dve.tensor_copy(sw_o[:, t % 2, hd * DH:(hd + 1) * DH], oo[o % 2][:, 0:DH])\
                        .then_inc(o_empty[o % 2], 1)
                    if hd == SW_H - 1:
                        dve.drain()
                        o_ = sw_o[:, t % 2, :].rearrange("p (h d) -> p h d", h=SW_H)
                        r = stat[:, 56:64]
                        tt(o_, o_, r.unsqueeze(2).to_broadcast([P, SW_H, DH]), ALU.mult).then_inc(o_ready, 1)

                for s in range(SW_N + 2):
                    if s < SW_N:
                        t, hd = divmod(s, SW_H)
                        if hd == 0 and t > 0:
                            wait_mm_read(dve, l, MM["sw_s"] + s - 1)
                            dve.wait_ge(sink_e, l * TT + t)
                            tt(stat[:, 56:64], stat[:, 16:24], stat[:, 40:48], ALU.add)
                            dve.drain()
                            dve.reciprocal(stat[:, 56:64], stat[:, 56:64])
                            dve.drain()
                        neg_max(l, MM["sw_s"] + s, win_tiles(t) * P, hd)
                        dve.drain()
                        tt(stat[:, hd:hd + 1], stat[:, hd:hd + 1], stat[:, 48 + hd:49 + hd], ALU.min)
                        dve.drain()
                        dve.sem_inc(nm_ready, 1)
                        if hd == SW_H - 1:
                            tt(stat[:, 32:40], sinks, stat[:, 0:8], ALU.add).then_inc(sink_in, 1)
                    if 1 <= s <= SW_N and s % 2 == 1:
                        turn_probs(l, TR["sw"] + SW_TP[s - 1], s - 1, win_tiles((s - 1) // SW_H))
                    if s == SW_N:
                        wait_mm_read(dve, l, MM["sw_s"] + SW_N - 1)
                        dve.wait_ge(sink_e, l * TT + TT)
                    if s >= 2:
                        if s == SW_N + 1:
                            tt(stat[:, 56:64], stat[:, 16:24], stat[:, 40:48], ALU.add)
                            dve.drain()
                            dve.reciprocal(stat[:, 56:64], stat[:, 56:64])
                        sw_keep(s - 2)
                merge(l, MM["sw_out"], False)

                for m in range(KT):
                    j = MM["o"] + m
                    wait_mm_full(dve, l, j)
                    for lo, hi, g in groups:
                        last = stt(x[:, m, lo:hi], mm[j % 2][:, lo:hi], mod[:, 16 + m, g:g + 1], x[:, m, lo:hi],
                                   ALU.mult, ALU.add)
                    last.then_inc(mm_empty[j % 2], 1)
                dve.drain()
                dve.sem_inc(x_ready, 1)

                refine_rstd(l, MM["norm2"], 3, D)
                scale_h(1)
                j = MM["router"]
                wait_mm_full(dve, l, j)
                lg = mm[j % 2][:, 0:TT * NE].rearrange("p (t e) -> p t e", e=NE)
                dve.tensor_reduce(stat[:, 0:TT], lg, AX.X, ALU.max)
                dve.drain()
                tt(aff[:, :, :], lg, stat[:, 0:TT].unsqueeze(2).to_broadcast([P, TT, NE]), ALU.subtract)\
                    .then_inc(mm_empty[j % 2], 1)
                dve.drain()
                dve.sem_inc(lg_ready, 1)
                dve.wait_ge(lg_e, l + 1)
                dve.tensor_reduce(stat[:, 0:TT], aff[:, :, :], AX.X, ALU.add)
                dve.drain()
                dve.reciprocal(stat[:, 0:TT], stat[:, 0:TT])
                dve.drain()
                tt(aff[:, :, :], aff[:, :, :], stat[:, 0:TT].unsqueeze(2).to_broadcast([P, TT, NE]), ALU.mult)\
                    .then_inc(aff_ready, 1)
                e16 = slice(0, NE)
                dve.wait_ge(v_sent, l * 32 + 32)
                wait_t_full(dve, l, TR["aff"])
                dve.tensor_copy(work_e[e16, :], tp[e16, 0:T]).then_inc(t_empty, 1)
                dve.memset(ones_e[e16, :], 1.0)
                dve.drain()
                for lo, hi, rounds in ((0, NLAT, CAP_L // 8), (NLAT, T, CAP_P // 8)):
                    for _ in range(rounds):
                        dve.max(top8[e16, :], work_e[e16, lo:hi])
                        dve.drain()
                        dve.match_replace(work_e[e16, lo:hi], top8[e16, :], work_e[e16, lo:hi], -1.0)
                        dve.drain()
                ts(mask_e[e16, :], work_e[e16, :], 0.0, ALU.is_lt)
                dve.drain()
                for lo, hi, _ in groups:
                    dve.tensor_tensor_scan(cum_e[e16, lo:hi], ones_e[e16, lo:hi], mask_e[e16, lo:hi], 0.0,
                                           ALU.mult, ALU.add)
                dve.drain()
                tt(cum_e[e16, :], cum_e[e16, :], mask_e[e16, :], ALU.mult)
                dve.drain()
                ts(cum_e[e16, :], cum_e[e16, :], -1.0, ALU.add).then_inc(pos_ready, 1)
                wait_t_full(dve, l, TR["pos"])
                dve.tensor_copy(pos_t[:, :, :], tp[:, 0:TT * NE].rearrange("p (t e) -> p t e", e=NE)).then_inc(t_empty, 1)
                dve.drain()
                lo, _ = CONST["iota"]
                tt(hot_p, const[:, lo:lo + CAP_P].unsqueeze(1).to_broadcast([P, NE, CAP_P]),
                   pos_t[:, PRT, :].unsqueeze(2).to_broadcast([P, NE, CAP_P]), ALU.is_equal)
                dve.drain()
                tt(hotw_p, hot_p, aff[:, PRT, :].unsqueeze(2).to_broadcast([P, NE, CAP_P]), ALU.mult)\
                    .then_inc(hotp_ready, 1)

                with dve.Fori(0, PAIRS) as e:
                    for half in range(2):
                        last = tt(hot[:, :, half, :], c_("iota").unsqueeze(1).to_broadcast([P, LT, CAP_L]),
                                  pos_t[:, 0:LT, bass.ds(2 * e + half, 1)].to_broadcast([P, LT, CAP_L]), ALU.is_equal)
                    last.then_inc(hot_ready, 1)
                    dve.drain()
                    for half in range(2):
                        last = tt(hotw[:, :, half, :], hot[:, :, half, :],
                                  aff[:, 0:LT, bass.ds(2 * e + half, 1)].to_broadcast([P, LT, CAP_L]), ALU.mult)
                    last.then_inc(hotw_ready, 1)
                    for g in range(2):
                        j = MM["pairs"] + g
                        wait_mm_full(dve, l, j, e)
                        v = mm[j % 2][:, 0:512].rearrange("p (k a s) -> p k a s", k=4, a=2)
                        for half in range(2):
                            last = dve.tensor_copy(xe[half][:, 4 * g:4 * g + 4, 0:CAP_L], v[:, :, half, :])
                        last.then_inc(mm_empty[j % 2], 1)
                    if True:
                        wait_mm_read(dve, l, MM["gather_p"])
                        wait_mm_read(dve, l, MM["gather_p"] + 1)
                    for half in range(2):
                        last = dve.tensor_copy(xe[half][:, :, CAP_L:CAP],
                                               xe_p[:, :, bass.ds(CAP_P * (2 * e + half), CAP_P)])
                    last.then_inc(xe_ready, 1)
                    for half in range(2):
                        for n in range(2):
                            j = MM["pairs"] + 2 + 3 * half + n
                            s_ = tmp[n][:, 0:4 * CAP]
                            dve.wait_ge(g_e, (l * PAIRS + e) * 4 + (2 * half + n + 1))
                            ts(s_, s_, 1.0, ALU.add)
                            dve.drain()
                            dve.reciprocal(s_, s_)
                            dve.drain()
                            tt(s_, mm[j % 2][:, 0:4 * CAP], s_, ALU.mult)
                            dve.drain()
                            tt(hid[half][:, 4 * n:4 * n + 4, :], mm[j % 2][:, 512:512 + 4 * CAP].rearrange(
                                "p (m s) -> p m s", m=4), s_.rearrange("p (m s) -> p m s", m=4), ALU.mult)
                            dve.drain()
                            dve.sem_inc(mm_empty[j % 2], 1)
                            dve.sem_inc(g_ready, 1)
                        j = MM["pairs"] + 2 + 3 * half + 2
                        wait_mm_full(dve, l, j, e)
                        for n in range(2):
                            v = mm[j % 2][:, 512 * n:512 * n + 4 * CAP].rearrange("p (m s) -> p m s", m=4)
                            dve.tensor_copy(ye[:, 4 * n:4 * n + 4, half * CAP_L:(half + 1) * CAP_L], v[:, :, 0:CAP_L])
                            last = dve.tensor_copy(ye_p[:, 4 * n:4 * n + 4, bass.ds(CAP_P * (2 * e + half), CAP_P)],
                                                   v[:, :, CAP_L:CAP])
                        last.then_inc(mm_empty[j % 2], 1)
                    for k in range(KT):
                        j = OO["pairs"] + k
                        wait_o_full(dve, l, j, e)
                        stt(x[:, k, 0:NLAT], oo[j % 2][:, :], mod[:, 40 + k, 0:1], x[:, k, 0:NLAT], ALU.mult, ALU.add)\
                            .then_inc(o_empty[j % 2], 1)
                    dve.drain()
                j = MM["combine_p"]
                wait_mm_full(dve, l, j)
                for k in range(KT):
                    stt(x[:, k, NLAT:T], mm[j % 2][:, k * P:(k + 1) * P], mod[:, 40 + k, 1:2], x[:, k, NLAT:T],
                        ALU.mult, ALU.add)
                dve.drain()
                for s in (mm_empty[j % 2], x_ready, small_free, layer_free):
                    dve.sem_inc(s, 1)

            refine_rstd(DEPTH, 0, 0, D)
            for k in range(KT):
                last = stt(h[:, k, :], x[:, k, :], col("final", k), rstd[:, :], ALU.mult, ALU.mult)
            last.then_inc(h_ready, 1)

        return nc


_INS = ["x_prompt", "x_sample", "cache_da_k", "cache_da_v", "cache_mla_ckv", "cache_mla_krope",
        "cache_swa_k", "cache_swa_v", "c", "c_ctx", "w_ada", "b_ada", "norm1", "norm2", "w_in",
        "da_lq1", "da_lk1", "da_lq2", "da_lk2", "da_subln", "mla_q_norm", "mla_w_qb", "mla_kv_norm",
        "mla_w_kvb", "swa_sink", "w_gate", "w_br_da", "w_br_mla", "w_br_swa", "w_o", "w_router",
        "w_ff1", "w_ff3", "w_ff2", "final_norm"]
_OUTS = [("y_prompt", (1, NPR, D)), ("y_sample", (1, NLAT, D)),
         ("new_da_k", (1, DEPTH, NPR, DA_H, 2 * DH)), ("new_da_v", (1, DEPTH, NPR, DA_H, 2 * DH)),
         ("new_mla_ckv", (1, DEPTH, NPR, KVR)), ("new_mla_krope", (1, DEPTH, NPR, MROPE)),
         ("new_swa_k", (1, DEPTH, NPR, SW_KV, DH)), ("new_swa_v", (1, DEPTH, NPR, SW_KV, DH))]


def kernel(**inputs):
    import concourse.bacc as _bacc
    from concourse.bass_utils import run_bass_kernel_spmd as _run

    nc = _bacc.Bacc("TRN2", target_bir_lowering=False, num_devices=1)
    table, lam = shape_constants()
    arrays, a = {}, {}
    for name, value in [(n, inputs[n]) for n in _INS] + [("const", table), ("lam", lam)]:
        v = np.ascontiguousarray(value)
        arrays[f"in_{name}"] = v
        a[name] = nc.dram_tensor(f"in_{name}", v.shape, mybir.dt.from_np(v.dtype), kind="ExternalInput").ap()
    for name, shape in _OUTS:
        a[name] = nc.dram_tensor(f"out_{name}", shape, FP32, kind="ExternalOutput").ap()
    build(nc, a)
    r = _run(nc, [arrays], core_ids=[0])
    return tuple(r.results[0][f"out_{name}"] for name, _ in _OUTS)
```

```python
import math
from contextlib import ExitStack

import numpy as np

import concourse.bass as bass
from concourse import mybir

FP32 = mybir.dt.float32
FP32R = mybir.dt.float32r
ALU = mybir.AluOpType
ACT = mybir.ActivationFunctionType
AX = mybir.AxisListType

P = 128
D = 1024
KT = D // P
DEPTH = 2
NLAT, NPR, NCTX = 512, 128, 128
T = NLAT + NPR
TT = T // P
PRT = TT - 1
LT = NLAT // P
KEYS = NLAT + NCTX + NPR
KEY_TILES = KEYS // P
GRID_W = 64
ROPE_BASE = 10000.0
EPS = 1e-6
DA_H, DH = 4, 64
QR, KVR, MROPE, MNOPE, MV, MH = 256, 128, 32, 64, 64, 8
MQ = MNOPE + MROPE
SW_H, SW_KV = 8, 2
BR = 512
IN_COLS = 3 * BR + QR + KVR + MROPE + SW_H * DH + 2 * SW_KV * DH
MLA_AT = 3 * BR
SWQ_AT = MLA_AT + QR + KVR + MROPE
SWK_AT = SWQ_AT + SW_H * DH
SWV_AT = SWK_AT + SW_KV * DH
NE, FF = 16, 1024
CAP_L, CAP_P = 2 * NLAT // NE, 2 * NPR // NE
CAP = CAP_L + CAP_P
PAIRS = NE // 2
SLOTS_P = NE * CAP_P
NEG = -1.0e30

RING = 6
HALF = 4
CHUNK = HALF * 512


def _layout(parts):
    at, out = 0, {}
    for name, width in parts:
        out[name] = (at, at + width)
        at += width
    return out, at


CONST, CONST_COLS = _layout([
    ("ident", P), ("swap", P), ("swap32", MROPE), ("ones", P), ("mask_before", P), ("mask_after", P),
    ("iota", CAP_L), ("cos64", NLAT), ("sin64", NLAT), ("cos32", NLAT), ("sin32", NLAT)])

ROWS, NROWS = _layout([
    ("b_ada", 48), ("norm1", KT), ("norm2", KT), ("q_norm", 2), ("kv_norm", 1), ("subln", 1),
    ("final", KT), ("c", KT), ("c_ctx", KT)])


def shape_constants():
    t = np.zeros((P, CONST_COLS), np.float32)

    def put(name, rows, value):
        a, b = CONST[name]
        t[rows, a:b] = value

    p = np.arange(P)
    put("ident", slice(0, P), np.eye(P))
    swap = np.zeros((P, P), np.float32)
    swap[p[1::2], p[0::2]] = -1.0
    swap[p[0::2], p[1::2]] = 1.0
    put("swap", slice(0, P), swap)
    put("swap32", slice(MNOPE, MQ), swap[:MROPE, :MROPE])
    put("ones", slice(0, P), 1.0)
    put("mask_before", slice(0, P), np.where(p[None, :] >= p[:, None], 0.0, NEG))
    put("mask_after", slice(0, P), np.where(p[None, :] <= p[:, None], 0.0, NEG))
    put("iota", slice(0, P), np.arange(CAP_L))
    tok = np.arange(NLAT)
    row, col = (tok // GRID_W).astype(np.float32), (tok % GRID_W).astype(np.float32)

    def angles(rot):
        n = rot // 4
        inv = (np.float32(ROPE_BASE) ** (-np.arange(n, dtype=np.float32) / np.float32(n))).astype(np.float32)
        ang = np.concatenate([row[:, None] * inv, col[:, None] * inv], axis=-1)
        return np.repeat(ang, 2, axis=1).T.astype(np.float32)

    a64 = angles(DH)
    a64 = np.concatenate([a64, a64])
    a32 = angles(MROPE)
    put("cos64", slice(0, P), np.cos(a64))
    put("sin64", slice(0, P), np.sin(a64))
    put("cos32", slice(MNOPE, MQ), np.cos(a32))
    put("sin32", slice(MNOPE, MQ), np.sin(a32))
    lam = np.array([[0.8 - 0.6 * math.exp(-0.3 * l) for l in range(DEPTH)]]).T
    lam = np.concatenate([lam, 1.0 - lam], axis=1).astype(np.float32)
    return t, lam


def layer_chunks():
    out = []

    def block(kind, c0, width=512):
        out.append((kind, 0, c0, width))
        out.append((kind, HALF, c0, width))

    def gates(b, branch):
        for mb in range(2):
            block("gate", b * D + mb * 512)
            out.append((branch, 0, mb * 512, 512))

    for b in range(12):
        block("ada", b * 512)
    for b in range(3):
        block("in", b * BR)
    gates(0, "br_da")
    block("in", MLA_AT, QR + KVR + MROPE)
    out.append(("qb", 0, 0, MH * MQ))
    out.append(("kvb", 0, 0, MH * (MNOPE + MV)))
    gates(1, "br_mla")
    block("in", SWQ_AT)
    block("in", SWK_AT, 2 * SW_KV * DH)
    gates(2, "br_swa")
    for b in range(2):
        block("o", b * 512)
    return out


CHUNKS = layer_chunks()
FIRST = {}
for _i, _c in enumerate(CHUNKS):
    FIRST.setdefault(_c[0], _i)
N_DENSE = len(CHUNKS)
PAIR_CHUNKS = 2 * 12
LAYER_CHUNKS = N_DENSE + PAIRS * PAIR_CHUNKS
PAIR_SLOT = N_DENSE % RING
assert PAIR_CHUNKS % RING == 0
assert LAYER_CHUNKS % RING == PAIR_SLOT


def _turns(parts):
    at, out = 0, {}
    for name, n in parts:
        out[name] = at
        at += n
    return out, at


DA_N, SW_N, MLA_N = TT * DA_H, TT * SW_H, TT * MH
PAIR_MM, PAIR_T, PAIR_O = 8, 5, 8
MM, _mm_dense = _turns([
    ("ada", 12), ("norm1", 1), ("da_q", 4), ("da_k", 4), ("da_rot", 8), ("da_v", TT), ("da_s", 2 * DA_N),
    ("da_out", 16), ("mla_in", 4), ("mla_norm", 2), ("kr_rot", 1), ("mla_v", KEY_TILES),
    ("mla_heads", MLA_N + 3 * MH), ("mla_out", 16), ("sw_q", 4), ("sw_k", 1), ("sw_rot", 5), ("sw_v", TT),
    ("sw_s", SW_N), ("sw_out", 16), ("o", 8), ("norm2", 1), ("router", 1), ("gather_p", 2),
    ("pairs", 0)])
MM["combine_p"] = _mm_dense + PAIRS * PAIR_MM
MM_LAYER = MM["combine_p"] + 1
MM_USES = [(MM_LAYER + 1) // 2, MM_LAYER // 2]
T_BEFORE = TT
TR, _t_dense = _turns([
    ("cols", 1), ("ada", 1), ("da_ctx", 1), ("da_new", 1), ("da", DA_N + TT), ("mla_ctx", 1), ("mla_new", 1),
    ("mla", MLA_N + TT), ("sw_ctx", 1), ("sw_new", 1), ("sw", SW_N + TT), ("h_tok", TT), ("aff", 1),
    ("pos", 1), ("hot_p", 1), ("pairs", 0)])
T_LAYER = _t_dense + PAIRS * PAIR_T
OO, _o_dense = _turns([("da", DA_N), ("mla", MLA_N), ("sw", SW_N), ("pairs", 0)])
O_LAYER = _o_dense + PAIRS * PAIR_O
O_USES = [O_LAYER // 2, O_LAYER // 2]
assert O_LAYER % 2 == 0 and _o_dense % 2 == 0


AF0, AF1, BF0, BF1, AO, BO = range(6)
UNITS = 2
SPLITS = 4
UK = HALF // UNITS
PAIR_UNITS = PAIR_CHUNKS * UNITS
JOB_UNITS = 4 * UNITS
USED_PAIR = PAIR_UNITS - 6
G0, G1 = 5, 6


def job_turn(q, last):
    return MM["pairs"] + 2 + (q if q < BO else (5 if last else 7))


def mla_s(i):
    h, t = divmod(i, TT)
    return MM["mla_heads"] + 3 + h * (TT + 3) + t + (3 if t >= 2 and h < MH - 1 else 0)


def mla_prep(h):
    return MM["mla_heads"] + (0 if h == 0 else 3 + (h - 1) * (TT + 3) + 2)


def t_order(n, per_tile, every):
    p, o, at = {}, {}, 0
    for s in range(n + 2):
        if 1 <= s <= n:
            p[s - 1] = at
            at += 1
        if every and s >= per_tile + 3 and (s - 3) % per_tile == 0:
            o[(s - 3) // per_tile - 1] = at
            at += 1
    for t in range(TT):
        if t not in o:
            o[t] = at
            at += 1
    return p, o


DA_TP, DA_TO = t_order(DA_N, DA_H, True)
SW_TP, SW_TO = t_order(SW_N, SW_H, True)
MLA_TP, MLA_TO = t_order(MLA_N, MH, False)

NEW_STORES = 4
SMALL_LOADS = 15
NM_LAYER = 2 * DA_N + MLA_N + SW_N
PER_LAYER = {
    "sq_ready": 2 * KT + 3, "sq_used": 2 * (KT - 1) + 1, "var_ready": 4, "r0_ready": 4,
    "scaled": 2 * KT, "h_ready": 2,
}


def build(nc, a):
    ctx = ExitStack()
    with ctx:
        place = {}

        def sb(name, shape):
            cols_ = int(np.prod(shape[1:]))
            t = nc.alloc_sbuf_tensor_at(name, shape, FP32, offset=arena_at + place["end"])
            place[name] = arena_at + place["end"]
            place["end"] += (cols_ * 4 + 31) // 32 * 32
            assert place["end"] <= ARENA * 4, place["end"]
            return t

        def rounded(name, host, at, shape):
            return nc.alloc_sbuf_tensor_at(name, shape, FP32R, offset=place[host] + 4 * at)

        ARENA = 53184
        arena_at = (nc.sbuf_base + 31) // 32 * 32
        ctx.enter_context(nc.sbuf_tensor("arena", [P, ARENA], FP32))
        place["end"] = 0

        def sem(name):
            return ctx.enter_context(nc.semaphore(name))

        ring = [sb(f"ring{i}", [P, HALF, 512]) for i in range(RING)]
        x = sb("x", [P, KT, T])
        h = sb("h", [P, KT, T])
        merged = sb("merged", [P, KT, T])
        tok = merged[:, :, :].rearrange("p k t -> p (k t)").rearrange("p (t c) -> p t c", c=D)
        SCRATCH = 15872
        scratch = sb("scratch", [P, SCRATCH])
        pt = sb("pt", [P, 2, T])
        tmp = [sb(f"tmp{i}", [P, T]) for i in range(3)]
        rstd = tmp_r = sb("rstd", [P, T])
        const = sb("const", [P, CONST_COLS])
        rows = sb("rows", [NROWS, P])
        cols = sb("cols", [P, NROWS])
        mod = sb("mod", [P, 48, 2])
        gain = sb("gain", [P, 2, KT, 2])
        silu_c = sb("silu_c", [P, KT, 2])
        silu_t = sb("silu_t", [P, 2 * KT])
        bc = sb("bc", [P, 4 * DH + SW_H + 2])
        lam = sb("lam", [P, 8])
        ctx_in = sb("ctx_in", [P, 352])
        new_out = sb("new_out", [P, 512])
        stat = sb("stat", [P, 64])
        wr = sb("wr", [P, KT, NE])
        pos_t = sb("pos_t", [P, TT, NE])
        aff = sb("aff", [P, TT, NE])

        def c_(name, rows_=slice(0, P)):
            lo, hi = CONST[name]
            return const[rows_, lo:hi]

        def col(name, k=0):
            lo = ROWS[name][0]
            return cols[:, lo + k:lo + k + 1]

        def view(at, *shape):
            n = int(np.prod(shape))
            assert at + n <= SCRATCH, (at, shape)
            v = scratch[:, at:at + n]
            if len(shape) == 1:
                return v
            if len(shape) == 2:
                return v.rearrange("p (a b) -> p a b", b=shape[1])
            return v.rearrange("p (a b c) -> p a b c", b=shape[1], c=shape[2])

        ident = c_("ident")
        ones = c_("ones")

        da_q, da_k = view(0, 4, T), view(2560, 4, KEYS)
        da_v = view(5632, KEY_TILES, 512)
        da_o = view(8704, 2, 512)
        da_p = [[view(9728 + (2 * i + m) * T, T) for m in range(2)] for i in range(2)]
        da_ctx = view(9728, 512)
        cq, ckv = view(0, 2, T), view(1280, KEYS)
        ml_v = view(2048, KEY_TILES, 512)
        ml_q = [view(5120 + i * T, T) for i in range(2)]
        ml_k = [view(6400 + i * KEYS, KEYS) for i in range(2)]
        ml_otok = view(7936, TT, 512)
        ml_p = [view(10496 + i * T, T) for i in range(2)]
        ml_o = view(2048, 4, T)
        sw_q, sw_kraw = view(0, 4, T), view(2560, KEYS)
        sw_k = view(3328, 2, KEYS)
        sw_v = view(4864, KEY_TILES, SW_KV * DH)
        sw_o = view(5632, 2, 512)
        sw_p = [view(6656 + i * 512, 512) for i in range(2)]
        ada_row = view(0, 6 * D)
        xe_p = view(0, KT, SLOTS_P)
        ye_ptok = view(0, 2, D)
        w_lo = [rounded(f"w_lo{i}", "scratch", 2048 + i * UK * 512, [P, UK, 512]) for i in range(SPLITS)]
        w_hi = [rounded(f"w_hi{i}", "h", i * UK * 512, [P, UK, 512]) for i in range(SPLITS)]
        x_hi = [rounded("xa_hi", "scratch", 6144, [P, KT, CAP]), rounded("xb_hi", "scratch", 7424, [P, KT, P])]
        x_lo = [rounded("xa_lo", "scratch", 6784, [P, KT, CAP]), rounded("xb_lo", "scratch", 8448, [P, KT, P])]
        hid = view(9472, FF)
        hid_hi = rounded("hid_hi", "h", 2 * CHUNK, [P, KT, P])
        hid_lo = rounded("hid_lo", "scratch", 10496, [P, KT, P])
        ye = view(11520, D)
        ye_pr = view(12544, D)
        hot = view(13568, LT, 2, CAP_L)
        hotw = view(14080, LT, 2, CAP_L)
        hotw_t = view(14592, NLAT)
        hot_p = view(15104, NE, CAP_P)
        hotw_p = view(15360, NE, CAP_P)
        hotw_pt = view(15616, 2, P)
        ROWS_OF = (CAP, P)
        LAT_OF = (slice(0, CAP_L), slice(P - CAP_L, P))
        PR_OF = (slice(CAP_L, CAP), slice(0, CAP_P))
        aff_e, work_e, mask_e = view(9472, T), view(10112, T), view(10752, T)
        cum_e = view(11392, T)
        ones_e, top8 = view(12032, T), view(12672, 8)

        mm = [ctx.enter_context(nc.psum_tensor(f"mm{i}", [P, 1024], FP32)) for i in range(2)]
        tp = ctx.enter_context(nc.psum_tensor("tp", [P, 1024], FP32))
        oo = [ctx.enter_context(nc.psum_tensor(f"oo{i}", [P, 512], FP32)) for i in range(2)]

        slot_in = [sem(f"slot{i}_in") for i in range(RING)]
        chunks_free = sem("chunks_free")
        mm_full = [sem(f"mm{i}_full") for i in range(2)]
        mm_empty = [sem(f"mm{i}_empty") for i in range(2)]
        t_full, t_empty = sem("t_full"), sem("t_empty")
        o_full = [sem(f"o{i}_full") for i in range(2)]
        o_empty = [sem(f"o{i}_empty") for i in range(2)]
        const_in, x_in = sem("const_in"), sem("x_in")
        small_in, ctx_kin, ctx_vin, sw_vin, wr_in = (sem("small_in"), sem("ctx_kin"), sem("ctx_vin"),
                                                     sem("sw_vin"), sem("wr_in"))
        small_free, layer_free = sem("small_free"), sem("layer_free")
        cols_ready, silu_e, silu_ready, mod_ready = (sem("cols_ready"), sem("silu_e"), sem("silu_ready"),
                                                     sem("mod_ready"))
        lam_e, lam_e_done = sem("lam_e"), sem("lam_e_done")
        sq_ready, sq_used, var_ready, r0_ready = sem("sq_ready"), sem("sq_used"), sem("var_ready"), sem("r0_ready")
        scaled, h_ready = sem("scaled"), sem("h_ready")
        da_roped, da_kctx_sent, nm_ready, p_mixed = (sem("da_roped"), sem("da_ctx_done"), sem("nm_ready"),
                                                     sem("p_mixed"))
        new_ready, new_sent, v_sent = sem("new_ready"), sem("new_sent"), sem("v_sent")
        ss_ready, o_ready = sem("ss_ready"), sem("o_ready")
        rs_ln, rs_done = sem("rs_ln"), sem("rs_done")
        e_ready, merged_ready = sem("e_ready"), sem("merged_ready")
        c_normed, kr_ready, mq_roped = sem("c_normed"), sem("kr_ready"), sem("mq_roped")
        sw_kready, sw_roped = sem("sw_kready"), sem("sw_roped")
        sink_in, sink_e = sem("sink_in"), sem("sink_e")
        x_ready = sem("x_ready")
        lg_ready, lg_e, aff_ready, pos_ready = sem("lg_ready"), sem("lg_e"), sem("aff_ready"), sem("pos_ready")
        hotp_ready, hot_ready, hotw_ready = sem("hotp_ready"), sem("hot_ready"), sem("hotw_ready")
        xhi_ready, xe_ready = sem("xhi_ready"), sem("xe_ready")
        w_hi_ready, w_ready, w_used = sem("w_hi_ready"), sem("w_ready"), sem("w_used")
        silu_out, hid_ready, hid_hi_ready = sem("silu_out"), sem("hid_ready"), sem("hid_hi_ready")
        ye_stored, ye_back, ye_done = sem("ye_stored"), sem("ye_back"), sem("ye_done")
        y_ready, y_sent = sem("y_ready"), sem("y_sent")
        pe_waited = sem("pe_waited")

        def mm_count(l, j, e):
            n = l * MM_USES[j % 2] + j // 2 + 1
            return n if e is None else n + e * (PAIR_MM // 2)

        def t_count(l, j, e):
            n = l * T_LAYER + (T_BEFORE + j + 1)
            return n if e is None else n + e * PAIR_T

        def o_count(l, j, e):
            n = l * O_USES[j % 2] + j // 2 + 1
            return n if e is None else n + e * (PAIR_O // 2)

        def wait_mm_full(eng, l, j, e=None):
            eng.wait_ge(mm_full[j % 2], mm_count(l, j, e))

        def wait_mm_empty(eng, l, j, e=None):
            eng.wait_ge(mm_empty[j % 2], mm_count(l, j, e))

        def wait_mm_read(eng, l, j, e=None):
            eng.wait_ge(mm_empty[j % 2], mm_count(l, j, e) + 1)

        def wait_t_full(eng, l, j, e=None):
            eng.wait_ge(t_full, t_count(l, j, e))

        def wait_t_empty(eng, l, j, e=None):
            eng.wait_ge(t_empty, t_count(l, j, e))

        def wait_t_read(eng, l, j, e=None):
            eng.wait_ge(t_empty, t_count(l, j, e) + 1)

        def wait_o_full(eng, l, j, e=None):
            eng.wait_ge(o_full[j % 2], o_count(l, j, e))

        def wait_o_empty(eng, l, j, e=None):
            eng.wait_ge(o_empty[j % 2], o_count(l, j, e))

        def chunk_use(l, i, e=None):
            before = LAYER_CHUNKS // RING + (1 if i % RING < LAYER_CHUNKS % RING else 0)
            n = l * before + i // RING + 1
            return n if e is None else n + e * (PAIR_CHUNKS // RING)

        block = ctx.enter_context(nc.Block())

        @block.sync
        def _(sp):
            sp.dma_start(const[:, :], a["const"]).then_inc(const_in, 16)
            sp.dma_start(tok[:, 0:LT, :], a["x_sample"][0].rearrange("(t p) c -> p t c", p=P)).then_inc(x_in, 16)
            sp.dma_start(tok[:, PRT, :], a["x_prompt"][0]).then_inc(x_in, 16)

            def chunk_source(l, kind, k0, c0, width):
                r0 = k0 * P
                if kind == "qb":
                    return a["mla_w_qb"][l].rearrange("(k p) c -> p k c", p=P)
                if kind == "kvb":
                    return a["mla_w_kvb"][l]
                w = {"ada": "w_ada", "in": "w_in", "gate": "w_gate", "br_da": "w_br_da",
                     "br_mla": "w_br_mla", "br_swa": "w_br_swa", "o": "w_o"}[kind]
                return a[w][l, r0:r0 + HALF * P, c0:c0 + width].rearrange("(k p) c -> p k c", p=P)

            def chunk_target(kind, slot, width):
                if kind == "qb":
                    return ring[slot][:, :, :].rearrange("p k c -> p (k c)")[:, 0:2 * MH * MQ].rearrange(
                        "p (k c) -> p k c", k=2)
                if kind == "kvb":
                    return ring[slot][:, :, :].rearrange("p k c -> p (k c)")[:, 0:MH * (MNOPE + MV)]
                return ring[slot][:, :, 0:width]

            with sp.Fori(0, DEPTH) as l:
                sp.wait_ge(small_free, l + 1)
                for name, key, per in (("b_ada", "b_ada", 48), ("norm1", "norm1", KT), ("norm2", "norm2", KT),
                                       ("q_norm", "mla_q_norm", 2), ("kv_norm", "mla_kv_norm", 1),
                                       ("subln", "da_subln", 1)):
                    lo, hi = ROWS[name]
                    sp.dma_start(rows[lo:hi, :], a[key][l].rearrange("(r c) -> r c", c=P)).then_inc(small_in, 16)
                for name, src in (("final", a["final_norm"]), ("c", a["c"][0]), ("c_ctx", a["c_ctx"])):
                    lo, hi = ROWS[name]
                    sp.dma_start(rows[lo:hi, :], src.rearrange("(r c) -> r c", c=P)).then_inc(small_in, 16)
                for i, key in enumerate(("da_lq1", "da_lk1", "da_lq2", "da_lk2")):
                    sp.dma_start(bc[:, i * DH:(i + 1) * DH], a[key][l].partition_broadcast(P)).then_inc(small_in, 16)
                sp.dma_start(bc[:, 4 * DH:4 * DH + SW_H], a["swa_sink"][l].partition_broadcast(P)).then_inc(small_in, 16)
                sp.dma_start(bc[:, 4 * DH + SW_H:], a["lam"][l].partition_broadcast(P)).then_inc(small_in, 16)

                def load(i):
                    kind, k0, c0, width = CHUNKS[i]
                    sp.wait_ge(chunks_free, l * LAYER_CHUNKS + (i + 1))
                    sp.dma_start(chunk_target(kind, i % RING, width),
                                 chunk_source(l, kind, k0, c0, width)).then_inc(slot_in[i % RING], 16)

                for i in range(FIRST["in"]):
                    load(i)
                sp.wait_ge(layer_free, l + 1)
                sp.dma_start(da_ctx, a["cache_da_k"][0, l].rearrange("t h d -> t (h d)")).then_inc(ctx_kin, 16)
                sp.dma_start(ctx_in[:, 0:KVR], a["cache_mla_ckv"][0, l]).then_inc(ctx_kin, 16)
                sp.dma_start(ctx_in[:, KVR + MNOPE:KVR + MQ], a["cache_mla_krope"][0, l]).then_inc(ctx_kin, 16)
                sp.dma_start(ctx_in[:, 224:352], a["cache_swa_k"][0, l].rearrange("t h d -> t (h d)")).then_inc(ctx_kin, 16)
                sp.dma_start(da_v[:, LT, :], a["cache_da_v"][0, l].rearrange("t h d -> t (h d)")).then_inc(ctx_vin, 16)
                sp.dma_start(wr[:, :, :], a["w_router"][l].rearrange("(k p) e -> p k e", p=P)).then_inc(wr_in, 16)
                for i in range(FIRST["in"], FIRST["qb"] + 2):
                    load(i)
                for i in range(FIRST["qb"] + 2, N_DENSE):
                    if i == FIRST["br_swa"] - 6:
                        wait_mm_full(sp, l, MM["mla_out"] + 15)
                        sp.dma_start(sw_v[:, LT, :],
                                     a["cache_swa_v"][0, l].rearrange("t h d -> t (h d)")).then_inc(sw_vin, 16)
                    load(i)

                with sp.Fori(0, PAIRS) as e:
                    i = N_DENSE
                    hidden = [("w_ff1", 0), ("w_ff3", 0), ("w_ff1", 512), ("w_ff3", 512)]
                    out = [("w_ff2", 0), ("w_ff2", 512)]
                    for half, blocks in ((0, hidden), (1, hidden), (0, out), (1, out)):
                        for w, c0 in blocks:
                            for k0 in (0, HALF):
                                sp.wait_ge(chunks_free, l * LAYER_CHUNKS + e * PAIR_CHUNKS + (i + 1))
                                sp.dma_start(ring[i % RING][:, :, :],
                                             a[w][l, 2 * e + half, k0 * P:(k0 + HALF) * P, c0:c0 + 512]
                                             .rearrange("(k p) c -> p k c", p=P)).then_inc(slot_in[i % RING], 16)
                                i += 1
            sp.wait_ge(y_ready, 2)
            sp.dma_start(a["y_sample"][0].rearrange("(t p) c -> p t c", p=P), tok[:, 0:LT, :]).then_inc(y_sent, 16)
            sp.dma_start(a["y_prompt"][0], tok[:, PRT, :]).then_inc(y_sent, 16)
            sp.wait_ge(y_sent, 32)
            sp.wait_ge(new_sent, DEPTH * NEW_STORES * 16)
            sp.wait_ge(v_sent, DEPTH * 2 * 16)

        @block.gpsimd
        def _(pool):
            pool.sem_inc(chunks_free, RING)
            pool.sem_inc(small_free, 1)
            for s in (*mm_empty, t_empty, *o_empty, w_used):
                pool.sem_inc(s, 1)
            pool.sem_inc(ye_stored, 32)

            with pool.Fori(0, DEPTH) as l:
                def consumed(turn, n, e=None):
                    wait_mm_full(pool, l, turn, e)
                    pool.sem_inc(chunks_free, n)

                for b in range(12):
                    consumed(MM["ada"] + b, 2)
                consumed(MM["da_q"] + 3, 2)
                consumed(MM["da_k"] + 3, 2)
                consumed(MM["da_v"] + TT - 1, 2)
                consumed(MM["da_out"] + 7, 3)
                consumed(MM["da_out"] + 15, 3)
                consumed(MM["mla_in"] + 3, 2)
                consumed(mla_prep(MH - 1) + 2, 2)
                consumed(MM["mla_out"] + 7, 3)
                consumed(MM["mla_out"] + 15, 3)
                consumed(MM["sw_q"] + 3, 2)
                consumed(MM["sw_v"] + TT - 1, 2)
                consumed(MM["sw_out"] + 7, 3)
                consumed(MM["sw_out"] + 15, 3)
                consumed(MM["o"] + 3, 2)
                consumed(MM["o"] + 7, 2)
                with pool.Fori(0, PAIRS) as e:
                    for n in range(PAIR_CHUNKS):
                        pool.wait_ge(w_ready, (l * PAIRS + e) * PAIR_UNITS + (n + 1) * UNITS)
                        pool.sem_inc(chunks_free, 1)

        @block.tensor
        def _(pe):
            pe.wait_ge(const_in, 16)
            pe.wait_ge(x_in, 32)
            for t in range(TT):
                pe.wait_ge(t_empty, t + 1)
                for k in range(KT):
                    last = pe.transpose(tp[:, k * P:(k + 1) * P], tok[:, t, k * P:(k + 1) * P], ident)
                last.then_inc(t_full, 1)

            def product(out, lhs, rhs, terms):
                for n in range(terms):
                    for lo, hi in ((0, 512), (512, T)):
                        last = pe.matmul(out[:, lo:hi], lhs(n), rhs(n)[:, lo:hi],
                                         start=(n == 0), stop=(n == terms - 1))
                return last

            def norm_sum(l, turn, sq0, used0, tiles):
                wait_mm_empty(pe, l, turn)
                for k in range(tiles):
                    pe.wait_ge(sq_ready, l * PER_LAYER["sq_ready"] + (sq0 + k + 1))
                    for lo, hi in ((0, 512), (512, T)):
                        last = pe.matmul(mm[turn % 2][:, lo:hi], ones, tmp[k % 2][:, lo:hi],
                                         start=(k == 0), stop=(k == tiles - 1))
                    last.then_inc(sq_used if k < tiles - 1 else mm_full[turn % 2], 1)

            def wait_chunks(l, i, n, e=None):
                for c in range(i, i + n):
                    pe.wait_ge(slot_in[c % RING], 16 * chunk_use(l, c, e))

            def weight(i, k, c0, c1):
                return ring[(i + k // HALF) % RING][:, k % HALF, c0:c1]

            def branch_out(l, chunk, turn, o_t):
                for m in range(KT):
                    c = chunk + 3 * (m // 4)
                    if m % 4 == 0:
                        wait_chunks(l, c, 3)
                    m0 = (m % 4) * P
                    j = turn + 2 * m
                    wait_mm_empty(pe, l, j)
                    product(mm[j % 2], lambda k: weight(c, k, m0, m0 + P), lambda k: h[:, k, :], KT)\
                        .then_inc(mm_full[j % 2], 1)
                    wait_mm_empty(pe, l, j + 1)
                    product(mm[(j + 1) % 2], lambda k: weight(c + 2, k, m0, m0 + P), lambda k: o_t[:, k, :], 4)\
                        .then_inc(mm_full[(j + 1) % 2], 1)

            def values(l, chunk, turn, c0, width):
                for t in range(TT):
                    j = turn + t
                    wait_mm_empty(pe, l, j)
                    for k in range(KT):
                        last = pe.matmul(mm[j % 2][:, 0:width], h[:, k, t * P:(t + 1) * P],
                                         weight(chunk, k, c0, c0 + width), start=(k == 0), stop=(k == KT - 1))
                    last.then_inc(mm_full[j % 2], 1)

            def attention(l, n, score, tiles, p_ready, probs, v_of, width, tr, t_p, o_base, after):
                for s in range(n + 2):
                    if s < n:
                        score(s)
                    if 1 <= s <= n:
                        i = s - 1
                        p_ready(i)
                        j = tr + t_p[i]
                        wait_t_empty(pe, l, j)
                        for b in range(tiles(i)):
                            last = pe.transpose(tp[:, b * P:(b + 1) * P], probs(i)[:, b * P:(b + 1) * P], ident)
                        last.then_inc(t_full, 1)
                    if s >= 2:
                        i = s - 2
                        o = o_base + i
                        wait_t_read(pe, l, tr + t_p[i])
                        wait_o_empty(pe, l, o)
                        for b in range(tiles(i)):
                            last = pe.matmul(oo[o % 2][:, 0:width], pt[:, i % 2, b * P:(b + 1) * P], v_of(i, b),
                                             start=(b == 0), stop=(b == tiles(i) - 1))
                        last.then_inc(o_full[o % 2], 1)
                    after(s)

            def turn_outputs(l, j, o_tok, ready, n):
                pe.wait_ge(ready, n)
                wait_t_empty(pe, l, j)
                for k in range(4):
                    last = pe.transpose(tp[:, k * P:(k + 1) * P], o_tok[:, k * P:(k + 1) * P], ident)
                last.then_inc(t_full, 1)

            def latent_keys(t):
                return [(0, 512, 0), (512, T, 512)] if t < LT else [(T, KEYS, 0)]

            def window(t):
                lo, hi = max(t - 1, 0), min(t + 1, LT - 1)
                return lo, hi

            def window_tiles(t):
                if t == PRT:
                    return 1
                lo, hi = window(t)
                return hi - lo + 2

            with pe.Fori(0, DEPTH) as l:
                pe.wait_ge(small_in, l * SMALL_LOADS * 16 + SMALL_LOADS * 16)
                wait_t_empty(pe, l, TR["cols"])
                pe.transpose(tp[:, 0:NROWS], rows[:, :], ident[0:NROWS, 0:NROWS]).then_inc(t_full, 1)
                pe.wait_ge(silu_ready, l + 1)
                for b in range(12):
                    j = MM["ada"] + b
                    wait_chunks(l, 2 * b, 2)
                    wait_mm_empty(pe, l, j)
                    for k in range(KT):
                        last = pe.matmul(mm[j % 2][0:2, 0:512], silu_c[:, k, :], weight(2 * b, k, 0, 512),
                                         start=(k == 0), stop=(k == KT - 1))
                    last.then_inc(mm_full[j % 2], 1)
                wait_mm_read(pe, l, MM["ada"] + 10)
                wait_mm_read(pe, l, MM["ada"] + 11)
                wait_t_empty(pe, l, TR["ada"])
                pe.sem_inc(pe_waited, 1)
                for m in range(48):
                    last = pe.transpose(tp[:, 2 * m:2 * m + 2], ada_row[0:2, m * P:(m + 1) * P], ident[0:2, 0:2])
                last.then_inc(t_full, 1)
                norm_sum(l, MM["norm1"], 0, 0, KT)

                pe.wait_ge(ctx_kin, l * 64 + 64)
                wait_t_empty(pe, l, TR["da_ctx"])
                for m in range(4):
                    last = pe.transpose(tp[:, m * P:(m + 1) * P], da_ctx[:, m * P:(m + 1) * P], ident)
                last.then_inc(t_full, 1)
                pe.wait_ge(h_ready, l * 2 + 1)
                c = FIRST["in"]
                for name, cc in (("da_q", c), ("da_k", c + 2)):
                    wait_chunks(l, cc, 2)
                    for m in range(4):
                        j = MM[name] + m
                        wait_mm_empty(pe, l, j)
                        product(mm[j % 2], lambda k: weight(cc, k, m * P, (m + 1) * P), lambda k: h[:, k, :], KT)\
                            .then_inc(mm_full[j % 2], 1)
                for m in range(8):
                    src = da_q[:, m, 0:NLAT] if m < 4 else da_k[:, m - 4, 0:NLAT]
                    j = MM["da_rot"] + m
                    wait_mm_read(pe, l, (MM["da_q"] if m < 4 else MM["da_k"] - 4) + m)
                    wait_mm_empty(pe, l, j)
                    pe.matmul(mm[j % 2][:, 0:NLAT], c_("swap"), src, start=True, stop=True).then_inc(mm_full[j % 2], 1)
                wait_chunks(l, c + 4, 2)
                values(l, c + 4, MM["da_v"], 0, 512)
                wait_t_empty(pe, l, TR["da_new"])
                for m in range(4):
                    last = pe.transpose(tp[:, m * P:(m + 1) * P], da_k[:, m, T:KEYS], ident)
                last.then_inc(t_full, 1)
                pe.wait_ge(da_roped, l + 1)
                wait_t_read(pe, l, TR["da_ctx"])
                pe.wait_ge(ctx_vin, l * 16 + 16)
                wait_mm_read(pe, l, MM["da_v"] + TT - 1)
                wait_mm_read(pe, l, MM["da_v"] + TT - 2)

                def da_score(i):
                    t, hd = divmod(i, DA_H)
                    for m in range(2):
                        j = MM["da_s"] + 2 * i + m
                        r = slice(m * DH, (m + 1) * DH)
                        wait_mm_empty(pe, l, j)
                        for lo, hi, at in latent_keys(t):
                            last = pe.matmul(mm[j % 2][:, at:at + hi - lo], da_q[r, hd, t * P:(t + 1) * P],
                                             da_k[r, hd, lo:hi], start=True, stop=True)
                        last.then_inc(mm_full[j % 2], 1)

                def da_values(i, b):
                    t, hd = divmod(i, DA_H)
                    return da_v[:, b if t < LT else PRT + 1, hd * P:(hd + 1) * P]

                def da_after(s):
                    for t in range(TT):
                        if s == DA_H * (t + 1) + 3:
                            turn_outputs(l, TR["da"] + DA_TO[t], da_o[:, t % 2, :], o_ready, l * 3 * TT + (t + 1))

                attention(l, DA_N, da_score, lambda i: 5 if i // DA_H < LT else 1,
                          lambda i: pe.wait_ge(p_mixed, l * DA_N + (i + 1)), lambda i: da_p[i % 2][0],
                          da_values, P, TR["da"], DA_TP, OO["da"], da_after)
                turn_outputs(l, TR["da"] + DA_TO[PRT], da_o[:, PRT % 2, :], o_ready, l * 3 * TT + TT)
                wait_t_read(pe, l, TR["da"] + DA_TO[PRT])
                branch_out(l, FIRST["br_da"] - 2, MM["da_out"], da_q)

                wait_t_empty(pe, l, TR["mla_ctx"])
                pe.transpose(tp[:, 0:P], ctx_in[:, 0:KVR], ident)
                pe.transpose(tp[0:MQ, P:2 * P], ctx_in[:, KVR:KVR + MQ], ident).then_inc(t_full, 1)
                c = FIRST["qb"] - 2
                wait_chunks(l, c, 2)
                for m in range(4):
                    j = MM["mla_in"] + m
                    wait_mm_empty(pe, l, j)
                    if m < 3:
                        product(mm[j % 2], lambda k: weight(c, k, m * P, (m + 1) * P), lambda k: h[:, k, :], KT)\
                            .then_inc(mm_full[j % 2], 1)
                    else:
                        product(mm[j % 2][MNOPE:MQ, :], lambda k: weight(c, k, 3 * P, 3 * P + MROPE),
                                lambda k: h[:, k, :], KT).then_inc(mm_full[j % 2], 1)
                norm_sum(l, MM["mla_norm"], KT, KT - 1, 2)
                norm_sum(l, MM["mla_norm"] + 1, KT + 2, KT, 1)
                j = MM["kr_rot"]
                wait_mm_read(pe, l, MM["mla_in"] + 3)
                wait_mm_empty(pe, l, j)
                pe.sem_inc(pe_waited, 1)
                pe.matmul(mm[j % 2][MNOPE:MQ, 0:NLAT], c_("swap32", slice(MNOPE, MQ)), ml_k[0][MNOPE:MQ, 0:NLAT],
                          start=True, stop=True).then_inc(mm_full[j % 2], 1)
                pe.wait_ge(c_normed, l * 2 + 2)
                wait_t_read(pe, l, TR["mla_ctx"])
                wait_chunks(l, FIRST["qb"], 2)
                wqb = ring[FIRST["qb"] % RING][:, :, :].rearrange("p k c -> p (k c)")[:, 0:2 * MH * MQ].rearrange(
                    "p (k c) -> p k c", k=2)
                wkvb = ring[FIRST["kvb"] % RING][:, :, :].rearrange("p k c -> p (k c)")[:, 0:MH * (MNOPE + MV)].rearrange(
                    "p (h c) -> p h c", h=MH)
                for t in range(KEY_TILES):
                    j = MM["mla_v"] + t
                    wait_mm_empty(pe, l, j)
                    pe.matmul(mm[j % 2][:, 0:512], ckv[:, t * P:(t + 1) * P], wkvb[:, :, MNOPE:],
                              start=True, stop=True).then_inc(mm_full[j % 2], 1)

                def project_head(hd):
                    j = mla_prep(hd)
                    wait_mm_empty(pe, l, j)
                    product(mm[j % 2][0:MQ, :], lambda k: wqb[:, k, hd * MQ:(hd + 1) * MQ], lambda k: cq[:, k, :], 2)\
                        .then_inc(mm_full[j % 2], 1)
                    wait_mm_empty(pe, l, j + 1)
                    for lo, hi in ((0, 512), (512, KEYS)):
                        last = pe.matmul(mm[(j + 1) % 2][0:MNOPE, lo:hi], wkvb[:, hd, 0:MNOPE], ckv[:, lo:hi],
                                         start=True, stop=True)
                    last.then_inc(mm_full[(j + 1) % 2], 1)
                    wait_mm_read(pe, l, j)
                    wait_mm_empty(pe, l, j + 2)
                    pe.sem_inc(pe_waited, 1)
                    pe.matmul(mm[(j + 2) % 2][MNOPE:MQ, 0:NLAT], c_("swap32", slice(MNOPE, MQ)),
                              ml_q[hd % 2][MNOPE:MQ, 0:NLAT], start=True, stop=True)\
                        .then_inc(mm_full[(j + 2) % 2], 1)

                pe.wait_ge(kr_ready, l + 1)
                wait_t_empty(pe, l, TR["mla_new"])
                pe.transpose(tp[:, 0:P], ckv[:, T:KEYS], ident)
                pe.transpose(tp[:, P:P + MROPE], ml_k[0][MNOPE:MQ, T:KEYS],
                             ident[MNOPE:MQ, MNOPE:MQ]).then_inc(t_full, 1)
                project_head(0)
                wait_mm_read(pe, l, MM["mla_v"] + KEY_TILES - 1)
                wait_mm_read(pe, l, MM["mla_v"] + KEY_TILES - 2)

                def mla_score(i):
                    hd, t = divmod(i, TT)
                    if t == 2 and hd < MH - 1:
                        project_head(hd + 1)
                    if t == 0:
                        wait_mm_read(pe, l, mla_prep(hd) + 1)
                        pe.wait_ge(mq_roped, l * MH + (hd + 1))
                    j = mla_s(i)
                    wait_mm_empty(pe, l, j)
                    for lo, hi, at in latent_keys(t):
                        last = pe.matmul(mm[j % 2][:, at:at + hi - lo], ml_q[hd % 2][0:MQ, t * P:(t + 1) * P],
                                         ml_k[hd % 2][0:MQ, lo:hi], start=True, stop=True)
                    last.then_inc(mm_full[j % 2], 1)

                attention(l, MLA_N, mla_score, lambda i: 5 if i % TT < LT else 1,
                          lambda i: wait_mm_read(pe, l, mla_s(i)), lambda i: ml_p[i % 2],
                          lambda i, b: ml_v[:, b if i % TT < LT else PRT + 1, (i // TT) * MV:(i // TT + 1) * MV],
                          MV, TR["mla"], MLA_TP, OO["mla"], lambda s: None)
                for t in range(TT):
                    turn_outputs(l, TR["mla"] + MLA_TO[t], ml_otok[:, t, :], o_ready, l * 3 * TT + 2 * TT)
                wait_t_read(pe, l, TR["mla"] + MLA_TO[TT - 1])
                branch_out(l, FIRST["br_mla"] - 2, MM["mla_out"], ml_o)

                wait_t_empty(pe, l, TR["sw_ctx"])
                pe.transpose(tp[:, 0:P], ctx_in[:, 224:352], ident).then_inc(t_full, 1)
                c = FIRST["br_swa"] - 6
                wait_chunks(l, c, 2)
                for m in range(4):
                    j = MM["sw_q"] + m
                    wait_mm_empty(pe, l, j)
                    product(mm[j % 2], lambda k: weight(c, k, m * P, (m + 1) * P), lambda k: h[:, k, :], KT)\
                        .then_inc(mm_full[j % 2], 1)
                wait_chunks(l, c + 2, 2)
                j = MM["sw_k"]
                wait_mm_empty(pe, l, j)
                product(mm[j % 2], lambda k: weight(c + 2, k, 0, P), lambda k: h[:, k, :], KT).then_inc(mm_full[j % 2], 1)
                for m in range(5):
                    src = sw_q[:, m, 0:NLAT] if m < 4 else sw_kraw[:, 0:NLAT]
                    j = MM["sw_rot"] + m
                    wait_mm_read(pe, l, MM["sw_q"] + m)
                    wait_mm_empty(pe, l, j)
                    pe.matmul(mm[j % 2][:, 0:NLAT], c_("swap"), src, start=True, stop=True).then_inc(mm_full[j % 2], 1)
                values(l, c + 2, MM["sw_v"], P, SW_KV * DH)
                wait_t_empty(pe, l, TR["sw_new"])
                pe.transpose(tp[:, 0:P], sw_kraw[:, T:KEYS], ident).then_inc(t_full, 1)
                pe.wait_ge(sw_roped, l + 1)
                pe.wait_ge(sw_vin, l * 16 + 16)
                wait_mm_read(pe, l, MM["sw_v"] + TT - 1)
                wait_mm_read(pe, l, MM["sw_v"] + TT - 2)

                def sw_score(i):
                    t, hd = divmod(i, SW_H)
                    r = slice((hd % 2) * DH, (hd % 2 + 1) * DH)
                    g = hd // (SW_H // SW_KV)
                    j = MM["sw_s"] + i
                    out = mm[j % 2]
                    q = sw_q[r, hd // 2, t * P:(t + 1) * P]
                    wait_mm_empty(pe, l, j)
                    if t == PRT:
                        last = pe.matmul(out[:, 0:P], q, sw_k[r, g, T:KEYS], start=True, stop=True)
                    else:
                        lo, hi = window(t)
                        n = (hi - lo + 1) * P
                        pe.matmul(out[:, 0:n], q, sw_k[r, g, lo * P:(hi + 1) * P], start=True, stop=False)
                        masks = [(0, "mask_before")] * (t > 0) + [(n - P, "mask_after")] * (t < LT - 1)
                        for at, name in masks:
                            pe.matmul(out[:, at:at + P], ident, c_(name), start=False,
                                      stop=(name == masks[-1][1]))
                        last = pe.matmul(out[:, n:n + P], q, sw_k[r, g, NLAT:T], start=True, stop=True)
                    last.then_inc(mm_full[j % 2], 1)

                def sw_values(i, b):
                    t, hd = divmod(i, SW_H)
                    g = hd // (SW_H // SW_KV)
                    if t == PRT:
                        tile = PRT + 1
                    else:
                        lo, hi = window(t)
                        tile = lo + b if b <= hi - lo else LT
                    return sw_v[:, tile, g * DH:(g + 1) * DH]

                def sw_after(s):
                    for t in range(TT):
                        if s == SW_H * (t + 1) + 3:
                            turn_outputs(l, TR["sw"] + SW_TO[t], sw_o[:, t % 2, :], o_ready,
                                         l * 3 * TT + (2 * TT + t + 1))

                attention(l, SW_N, sw_score, lambda i: window_tiles(i // SW_H),
                          lambda i: wait_mm_read(pe, l, MM["sw_s"] + i), lambda i: sw_p[i % 2],
                          sw_values, DH, TR["sw"], SW_TP, OO["sw"], sw_after)
                turn_outputs(l, TR["sw"] + SW_TO[PRT], sw_o[:, PRT % 2, :], o_ready, l * 3 * TT + 3 * TT)
                wait_t_read(pe, l, TR["sw"] + SW_TO[PRT])
                branch_out(l, FIRST["br_swa"] - 2, MM["sw_out"], sw_q)

                pe.wait_ge(merged_ready, l * 3 + 3)
                for m in range(KT):
                    c = FIRST["o"] + 2 * (m // 4)
                    if m % 4 == 0:
                        wait_chunks(l, c, 2)
                    j = MM["o"] + m
                    wait_mm_empty(pe, l, j)
                    product(mm[j % 2], lambda k: weight(c, k, (m % 4) * P, (m % 4 + 1) * P),
                            lambda k: merged[:, k, :], KT).then_inc(mm_full[j % 2], 1)

                norm_sum(l, MM["norm2"], KT + 3, KT, KT)
                pe.wait_ge(h_ready, l * 2 + 2)
                pe.wait_ge(wr_in, l * 16 + 16)
                j = MM["router"]
                wait_mm_empty(pe, l, j)
                for t in range(TT):
                    for k in range(KT):
                        last = pe.matmul(mm[j % 2][:, t * NE:(t + 1) * NE], h[:, k, t * P:(t + 1) * P], wr[:, k, :],
                                         start=(k == 0), stop=(k == KT - 1))
                last.then_inc(mm_full[j % 2], 1)
                for t in range(TT):
                    wait_t_empty(pe, l, TR["h_tok"] + t)
                    for k in range(KT):
                        last = pe.transpose(tp[:, k * P:(k + 1) * P], h[:, k, t * P:(t + 1) * P], ident)
                    last.then_inc(t_full, 1)
                pe.wait_ge(aff_ready, l + 1)
                wait_t_empty(pe, l, TR["aff"])
                for t in range(TT):
                    last = pe.transpose(tp[0:NE, t * P:(t + 1) * P], aff[:, t, :], ident)
                last.then_inc(t_full, 1)
                pe.wait_ge(pos_ready, l + 1)
                wait_t_empty(pe, l, TR["pos"])
                pe.sem_inc(pe_waited, 1)
                for t in range(TT):
                    last = pe.transpose(tp[:, t * NE:(t + 1) * NE], cum_e[0:NE, t * P:(t + 1) * P], ident[0:NE, 0:NE])
                last.then_inc(t_full, 1)
                pe.wait_ge(hotp_ready, l + 1)
                wait_t_read(pe, l, TR["h_tok"] + TT - 1)
                for g in range(2):
                    j = MM["gather_p"] + g
                    wait_mm_empty(pe, l, j)
                    for k in range(4):
                        last = pe.matmul(mm[j % 2][:, k * SLOTS_P:(k + 1) * SLOTS_P],
                                         tok[:, PRT, (4 * g + k) * P:(4 * g + k + 1) * P],
                                         hot_p.rearrange("p e s -> p (e s)"), start=True, stop=True)
                    last.then_inc(mm_full[j % 2], 1)
                wait_t_empty(pe, l, TR["hot_p"])
                for g in range(2):
                    last = pe.transpose(tp[:, g * P:(g + 1) * P],
                                        hotw_p.rearrange("p e s -> p (e s)")[:, g * P:(g + 1) * P], ident)
                last.then_inc(t_full, 1)

                def gather(turn, g, e, of):
                    if g == 0:
                        pe.wait_ge(hot_ready, l * PAIRS + of + 1)
                    wait_mm_empty(pe, l, turn, e)
                    for k in range(4):
                        for t in range(LT):
                            last = pe.matmul(mm[turn % 2][:, k * P:(k + 1) * P],
                                             tok[:, t, (4 * g + k) * P:(4 * g + k + 1) * P],
                                             hot[:, t, :, :].rearrange("p a s -> p (a s)"),
                                             start=(t == 0), stop=(t == LT - 1))
                    last.then_inc(mm_full[turn % 2], 1)

                def turn_hot(turn, e, of):
                    pe.wait_ge(hotw_ready, l * PAIRS + of + 1)
                    wait_t_empty(pe, l, turn, e)
                    for t in range(LT):
                        last = pe.transpose(tp[:, t * P:(t + 1) * P], hotw[:, t, :, :].rearrange("p a s -> p (a s)"),
                                            ident)
                    last.then_inc(t_full, 1)

                def job(q, e, last_pair):
                    half = q % 2 if q >= AO else q // 2
                    rows_ = ROWS_OF[half]
                    hi, lo = (hid_hi, hid_lo) if q >= AO else (x_hi[half], x_lo[half])
                    j = job_turn(q, last_pair)
                    out = mm[j % 2]
                    wait_mm_empty(pe, l, j, e)
                    for c in range(JOB_UNITS):
                        n = JOB_UNITS * q + c
                        pe.wait_ge(w_ready, (l * PAIRS + e) * PAIR_UNITS + (n + 1))
                        bank = (c // (2 * UNITS)) * 512
                        for kk in range(UK):
                            k = (c % (2 * UNITS)) * UK + kk
                            for i, (a_, b_) in enumerate(((hi, w_lo), (lo, w_hi), (hi, w_hi))):
                                last = pe.matmul(out[0:rows_, bank:bank + 512], a_[:, k, 0:rows_],
                                                 b_[n % SPLITS][:, kk, :], start=(k == 0 and i == 0),
                                                 stop=(k == KT - 1 and i == 2))
                        last.then_inc(mm_full[j % 2] if c == JOB_UNITS - 1 else w_used, 1)

                def turn_hidden(q, turn, e):
                    half, n = q // 2, q % 2
                    rows_ = ROWS_OF[half]
                    pe.wait_ge(hid_ready, (l * PAIRS + e) * 4 + (q + 1))
                    wait_t_empty(pe, l, turn, e)
                    for k in range(4):
                        last = pe.transpose(tp[:, k * P:k * P + rows_],
                                            hid[0:rows_, (4 * n + k) * P:(4 * n + k + 1) * P],
                                            ident[0:rows_, 0:rows_])
                    last.then_inc(t_full, 1)

                def pair(e, last_pair=False):
                    m0, t0 = MM["pairs"] + 2, TR["pairs"] + 1
                    pe.wait_ge(xe_ready, l * PAIRS + e + 1)
                    job(AF0, e, last_pair)
                    job(AF1, e, last_pair)
                    turn_hidden(AF0, t0, e)
                    job(BF0, e, last_pair)
                    turn_hidden(AF1, t0 + 1, e)
                    job(BF1, e, last_pair)
                    wait_t_read(pe, l, t0 + 1, e)
                    job(AO, e, last_pair)
                    turn_hidden(BF0, t0 + 2, e)
                    if not last_pair:
                        gather(m0 + G0, 0, e, e + 1)
                    turn_hidden(BF1, t0 + 3, e)
                    if not last_pair:
                        gather(m0 + G1, 1, e, e + 1)
                    wait_t_read(pe, l, t0 + 3, e)
                    job(BO, e, last_pair)
                    pe.wait_ge(ye_done, l * PAIRS + e + 1)
                    if last_pair:
                        wait_t_read(pe, l, TR["pairs"] + 5, e - 1)
                    for k in range(KT):
                        j = OO["pairs"] + k
                        wait_o_empty(pe, l, j, e)
                        pe.matmul(oo[j % 2][:, :], ye[:, k * P:(k + 1) * P], hotw_t, start=True, stop=True)\
                            .then_inc(o_full[j % 2], 1)
                    if not last_pair:
                        turn_hot(t0 + 4, e, e + 1)

                gather(MM["pairs"], 0, None, 0)
                gather(MM["pairs"] + 1, 1, None, 0)
                turn_hot(TR["pairs"], None, 0)
                wait_t_read(pe, l, TR["pairs"])
                pe.sem_inc(pe_waited, 1)
                with pe.Fori(0, PAIRS - 1) as e:
                    pair(e)
                pair(PAIRS - 1, True)

                pe.wait_ge(ye_back, l * 16 + 16)
                j = MM["combine_p"]
                wait_mm_empty(pe, l, j)
                for k in range(KT):
                    for g in range(2):
                        last = pe.matmul(mm[j % 2][:, k * P:(k + 1) * P], ye_ptok[:, g, k * P:(k + 1) * P],
                                         hotw_pt[:, g, :], start=(g == 0), stop=(g == 1))
                last.then_inc(mm_full[j % 2], 1)

            norm_sum(DEPTH, 0, 0, 0, KT)
            pe.wait_ge(h_ready, DEPTH * 2 + 1)
            for t in range(TT):
                wait_t_empty(pe, DEPTH, t)
                for k in range(KT):
                    last = pe.transpose(tp[:, k * P:(k + 1) * P], h[:, k, t * P:(t + 1) * P], ident)
                last.then_inc(t_full, 1)

        @block.scalar
        def _(act):
            def copy(out, in_, scale=1.0):
                return act.activation(out, in_, ACT.Copy, scale=scale)

            def squares(l, tiles, sq0, used0, src):
                for k in range(tiles):
                    if k >= 2:
                        act.wait_ge(sq_used, l * PER_LAYER["sq_used"] + (used0 + k - 1))
                    act.activation(tmp[k % 2][:, :], src(k), ACT.Square).then_inc(sq_ready, 1)

            def first_rstd(l, n):
                act.wait_ge(var_ready, l * PER_LAYER["var_ready"] + (n + 1))
                act.activation(rstd[:, :], tmp[2][:, :], ACT.Ln)
                act.drain()
                act.activation(rstd[:, :], rstd[:, :], ACT.Exp, scale=-0.5).then_inc(r0_ready, 1)

            def shifts(l, n, shift):
                for k in range(KT):
                    act.wait_ge(scaled, l * PER_LAYER["scaled"] + (n * KT + k + 1))
                    act.activation(h[:, k, 0:NLAT], h[:, k, 0:NLAT], ACT.Identity, bias=mod[:, shift + k, 0:1])
                    last = act.activation(h[:, k, NLAT:T], h[:, k, NLAT:T], ACT.Identity, bias=mod[:, shift + k, 1:2])
                last.then_inc(h_ready, 1)

            def gates(l, turn):
                for m in range(KT):
                    j = turn + 2 * m
                    wait_mm_full(act, l, j)
                    if m >= 2:
                        wait_mm_read(act, l, j - 3)
                    act.activation(tmp[m % 2][:, :], mm[j % 2][:, 0:T], ACT.Exp, scale=-1.0).then_inc(mm_empty[j % 2], 1)

            def exps(l, i0, i, j, out, width, sum_at):
                act.wait_ge(nm_ready, l * NM_LAYER + (i0 + i + 1))
                wait_mm_full(act, l, j)
                act.activation(out, mm[j % 2][:, 0:width], ACT.Exp, bias=stat[:, sum_at:sum_at + 1],
                               accum_out=stat[:, sum_at + 16:sum_at + 17])

            with act.Fori(0, DEPTH) as l:
                act.wait_ge(cols_ready, l + 1)
                lo, hi = ROWS["c"][0], ROWS["c_ctx"][1]
                act.activation(silu_t[:, :], cols[:, lo:hi], ACT.Exp, scale=-1.0).then_inc(silu_e, 1)
                act.wait_ge(lam_e, l + 1)
                act.activation(lam[:, 2:4], lam[:, 0:2], ACT.Exp).then_inc(lam_e_done, 1)
                for b in range(12):
                    j = MM["ada"] + b
                    wait_mm_full(act, l, j)
                    copy(ada_row[0:2, b * 512:(b + 1) * 512], mm[j % 2][0:2, 0:512]).then_inc(mm_empty[j % 2], 1)
                act.wait_ge(x_ready, l * 2 + 1)
                squares(l, KT, 0, 0, lambda k: x[:, k, :])
                first_rstd(l, 0)
                shifts(l, 0, 0)

                wait_t_full(act, l, TR["da_ctx"])
                copy(da_k[:, :, NLAT:T], tp[:, 0:512].rearrange("p (m t) -> p m t", m=4)).then_inc(t_empty, 1)
                for m in range(4):
                    j = MM["da_q"] + m
                    wait_mm_full(act, l, j)
                    copy(da_q[:, m, :], mm[j % 2][:, 0:T], DH ** -0.5).then_inc(mm_empty[j % 2], 1)
                for m in range(4):
                    j = MM["da_k"] + m
                    wait_mm_full(act, l, j)
                    copy(da_k[:, m, 0:NLAT], mm[j % 2][:, 0:NLAT])
                    copy(da_k[:, m, T:KEYS], mm[j % 2][:, NLAT:T]).then_inc(mm_empty[j % 2], 1)
                for t in range(TT):
                    j = MM["da_v"] + t
                    wait_mm_full(act, l, j)
                    copy(da_v[:, t if t < LT else PRT + 1, :], mm[j % 2][:, 0:512]).then_inc(mm_empty[j % 2], 1)
                wait_mm_read(act, l, MM["da_v"] + TT - 1)
                act.dma_start(a["new_da_v"][0, l].rearrange("t h d -> t (h d)"), da_v[:, PRT + 1, :]).then_inc(v_sent, 16)
                wait_t_full(act, l, TR["da_new"])
                copy(new_out[:, :], tp[:, 0:512]).then_inc(t_empty, 1)
                wait_t_read(act, l, TR["da_new"])
                act.dma_start(a["new_da_k"][0, l].rearrange("t h d -> t (h d)"), new_out[:, :]).then_inc(new_sent, 16)

                def turn_probs(l, j, i, n):
                    wait_t_full(act, l, j)
                    copy(pt[:, i % 2, 0:n * P], tp[:, 0:n * P]).then_inc(t_empty, 1)

                def turn_out_da(t):
                    wait_t_full(act, l, TR["da"] + DA_TO[t])
                    copy(da_q[:, :, t * P:(t + 1) * P], tp[:, 0:512].rearrange("p (m t) -> p m t", m=4),
                         lam[:, 7:8]).then_inc(t_empty, 1)

                def keep_squares(i):
                    o = OO["da"] + i
                    wait_o_full(act, l, o)
                    act.activation(rstd[:, 0:P], oo[o % 2][:, 0:P], ACT.Square,
                                   accum_out=stat[:, 32 + i % 8:33 + i % 8])
                    act.drain()
                    act.sem_inc(ss_ready, 1)
                    if i % DA_H == DA_H - 1:
                        t = i // DA_H
                        s0 = 32 + (t % 2) * 4
                        act.wait_ge(rs_ln, l * TT + (t + 1))
                        act.activation(stat[:, s0 + 8:s0 + 12], stat[:, s0:s0 + 4], ACT.Ln)
                        act.drain()
                        act.activation(stat[:, s0 + 8:s0 + 12], stat[:, s0 + 8:s0 + 12], ACT.Exp, scale=-0.5)\
                            .then_inc(rs_done, 1)

                for s in range(DA_N + 2):
                    if s < DA_N:
                        width = T if s // DA_H < LT else P
                        for m in range(2):
                            j = MM["da_s"] + 2 * s + m
                            exps(l, 0, 2 * s + m, j, da_p[s % 2][m][:, 0:width], width, 2 * (s % 4) + m)
                            act.drain()
                            act.sem_inc(mm_empty[j % 2], 1)
                    if 1 <= s <= DA_N:
                        turn_probs(l, TR["da"] + DA_TP[s - 1], s - 1, 5 if (s - 1) // DA_H < LT else 1)
                    if s >= 2:
                        keep_squares(s - 2)
                    for t in range(TT):
                        if s == DA_H * (t + 1) + 3:
                            turn_out_da(t)
                turn_out_da(PRT)
                gates(l, MM["da_out"])

                act.wait_ge(merged_ready, l * 3 + 1)
                act.wait_ge(v_sent, l * 32 + 16)
                wait_t_full(act, l, TR["mla_ctx"])
                copy(ckv[:, NLAT:T], tp[:, 0:P])
                copy(ml_k[0][MNOPE:MQ, NLAT:T], tp[MNOPE:MQ, P:2 * P]).then_inc(t_empty, 1)
                for m in range(2):
                    j = MM["mla_in"] + m
                    wait_mm_full(act, l, j)
                    copy(cq[:, m, :], mm[j % 2][:, 0:T]).then_inc(mm_empty[j % 2], 1)
                j = MM["mla_in"] + 2
                wait_mm_full(act, l, j)
                copy(ckv[:, 0:NLAT], mm[j % 2][:, 0:NLAT])
                copy(ckv[:, T:KEYS], mm[j % 2][:, NLAT:T]).then_inc(mm_empty[j % 2], 1)
                j = MM["mla_in"] + 3
                wait_mm_full(act, l, j)
                copy(ml_k[0][MNOPE:MQ, 0:NLAT], mm[j % 2][MNOPE:MQ, 0:NLAT])
                copy(ml_k[0][MNOPE:MQ, T:KEYS], mm[j % 2][MNOPE:MQ, NLAT:T]).then_inc(mm_empty[j % 2], 1)
                act.drain()
                squares(l, 2, KT, KT - 1, lambda k: cq[:, k, :])
                first_rstd(l, 1)
                act.wait_ge(c_normed, l * 2 + 1)
                act.activation(tmp[0][:, 0:NLAT], ckv[:, 0:NLAT], ACT.Square)
                act.activation(tmp[0][:, NLAT:T], ckv[:, T:KEYS], ACT.Square).then_inc(sq_ready, 1)
                first_rstd(l, 2)
                for t in range(KEY_TILES):
                    j = MM["mla_v"] + t
                    wait_mm_full(act, l, j)
                    copy(ml_v[:, t, :], mm[j % 2][:, 0:512]).then_inc(mm_empty[j % 2], 1)
                wait_t_full(act, l, TR["mla_new"])
                act.wait_ge(new_sent, l * NEW_STORES * 16 + 16)
                copy(new_out[:, 0:P + MROPE], tp[:, 0:P + MROPE]).then_inc(t_empty, 1)
                wait_t_read(act, l, TR["mla_new"])
                act.dma_start(a["new_mla_ckv"][0, l], new_out[:, 0:P]).then_inc(new_sent, 16)
                act.dma_start(a["new_mla_krope"][0, l], new_out[:, P:P + MROPE]).then_inc(new_sent, 16)

                def head_in(hd):
                    j = mla_prep(hd)
                    wait_mm_full(act, l, j)
                    copy(ml_q[hd % 2][0:MQ, :], mm[j % 2][0:MQ, 0:T], MQ ** -0.5).then_inc(mm_empty[j % 2], 1)
                    j += 1
                    wait_mm_full(act, l, j)
                    copy(ml_k[hd % 2][0:MNOPE, :], mm[j % 2][0:MNOPE, 0:KEYS]).then_inc(mm_empty[j % 2], 1)

                head_in(0)
                for s in range(MLA_N + 2):
                    if s < MLA_N:
                        hd, t = divmod(s, TT)
                        if t == 2 and hd < MH - 1:
                            head_in(hd + 1)
                        width = T if t < LT else P
                        j = mla_s(s)
                        exps(l, 2 * DA_N, s, j, ml_p[s % 2][:, 0:width], width, s % 8)
                        act.drain()
                        act.sem_inc(mm_empty[j % 2], 1)
                    if 1 <= s <= MLA_N and s % 2 == 0:
                        turn_probs(l, TR["mla"] + MLA_TP[s - 1], s - 1, 5 if (s - 1) % TT < LT else 1)
                for t in range(TT):
                    wait_t_full(act, l, TR["mla"] + MLA_TO[t])
                    copy(ml_o[:, :, t * P:(t + 1) * P],
                         tp[:, 0:512].rearrange("p (m t) -> p m t", m=4)).then_inc(t_empty, 1)
                gates(l, MM["mla_out"])

                act.wait_ge(merged_ready, l * 3 + 2)
                wait_t_full(act, l, TR["sw_ctx"])
                copy(sw_kraw[:, NLAT:T], tp[:, 0:P]).then_inc(t_empty, 1)
                for m in range(4):
                    j = MM["sw_q"] + m
                    wait_mm_full(act, l, j)
                    copy(sw_q[:, m, :], mm[j % 2][:, 0:T], DH ** -0.5).then_inc(mm_empty[j % 2], 1)
                j = MM["sw_k"]
                wait_mm_full(act, l, j)
                copy(sw_kraw[:, 0:NLAT], mm[j % 2][:, 0:NLAT])
                copy(sw_kraw[:, T:KEYS], mm[j % 2][:, NLAT:T]).then_inc(mm_empty[j % 2], 1)
                for t in range(TT):
                    j = MM["sw_v"] + t
                    wait_mm_full(act, l, j)
                    copy(sw_v[:, t if t < LT else PRT + 1, :], mm[j % 2][:, 0:SW_KV * DH]).then_inc(mm_empty[j % 2], 1)
                wait_mm_read(act, l, MM["sw_v"] + TT - 1)
                act.dma_start(a["new_swa_v"][0, l].rearrange("t h d -> t (h d)"), sw_v[:, PRT + 1, :]).then_inc(v_sent, 16)
                wait_t_full(act, l, TR["sw_new"])
                act.wait_ge(new_sent, l * NEW_STORES * 16 + 48)
                copy(new_out[:, 0:P], tp[:, 0:P]).then_inc(t_empty, 1)
                wait_t_read(act, l, TR["sw_new"])
                act.dma_start(a["new_swa_k"][0, l].rearrange("t h d -> t (h d)"), new_out[:, 0:P]).then_inc(new_sent, 16)

                def win_tiles(t):
                    return 1 if t == PRT else min(t + 1, LT - 1) - max(t - 1, 0) + 2

                for s in range(SW_N + 2):
                    if s < SW_N:
                        t, hd = divmod(s, SW_H)
                        width = win_tiles(t) * P
                        j = MM["sw_s"] + s
                        exps(l, 2 * DA_N + MLA_N, s, j, sw_p[s % 2][:, 0:width], width, hd)
                        act.drain()
                        act.sem_inc(mm_empty[j % 2], 1)
                        if hd == SW_H - 1:
                            act.wait_ge(sink_in, l * TT + (t + 1))
                            act.activation(stat[:, 40:48], stat[:, 32:40], ACT.Exp).then_inc(sink_e, 1)
                    if 1 <= s <= SW_N and s % 2 == 0:
                        turn_probs(l, TR["sw"] + SW_TP[s - 1], s - 1, win_tiles((s - 1) // SW_H))
                    for t in range(TT):
                        if s == SW_H * (t + 1) + 3:
                            wait_t_full(act, l, TR["sw"] + SW_TO[t])
                            copy(sw_q[:, :, t * P:(t + 1) * P],
                                 tp[:, 0:512].rearrange("p (m t) -> p m t", m=4)).then_inc(t_empty, 1)
                wait_t_full(act, l, TR["sw"] + SW_TO[PRT])
                copy(sw_q[:, :, PRT * P:T], tp[:, 0:512].rearrange("p (m t) -> p m t", m=4)).then_inc(t_empty, 1)
                gates(l, MM["sw_out"])

                act.wait_ge(new_sent, l * NEW_STORES * 16 + NEW_STORES * 16)
                act.wait_ge(x_ready, l * 2 + 2)
                squares(l, KT, KT + 3, KT, lambda k: x[:, k, :])
                first_rstd(l, 3)
                shifts(l, 1, 24)
                act.wait_ge(lg_ready, l + 1)
                act.activation(aff[:, :, :], aff[:, :, :], ACT.Exp).then_inc(lg_e, 1)
                for t in range(TT):
                    wait_t_full(act, l, TR["h_tok"] + t)
                    copy(tok[:, t, :], tp[:, :]).then_inc(t_empty, 1)
                for g in range(2):
                    j = MM["gather_p"] + g
                    wait_mm_full(act, l, j)
                    copy(xe_p[:, 4 * g:4 * g + 4, :],
                         mm[j % 2][:, :].rearrange("p (k s) -> p k s", k=4)).then_inc(mm_empty[j % 2], 1)
                wait_t_full(act, l, TR["hot_p"])
                copy(hotw_pt.rearrange("p g s -> p (g s)"), tp[:, 0:2 * P]).then_inc(t_empty, 1)

                def hi_of_chunk(n, e, last_pair=False):
                    i = N_DENSE + n
                    for u in range(UNITS):
                        m = UNITS * n + u
                        p = m - SPLITS
                        if p >= 0:
                            if p % JOB_UNITS == JOB_UNITS - 1:
                                wait_mm_full(act, l, job_turn(p // JOB_UNITS, last_pair), e)
                            else:
                                act.wait_ge(w_used, (l * PAIRS + e) * USED_PAIR + (p - p // JOB_UNITS + 2))
                        if u == 0:
                            act.wait_ge(slot_in[i % RING], 16 * chunk_use(l, i, e))
                        copy(w_hi[m % SPLITS][:, :, :], ring[i % RING][:, u * UK:(u + 1) * UK, :])\
                            .then_inc(w_hi_ready, 1)

                def hi_of_tokens(turn, g, e):
                    wait_mm_full(act, l, turn, e)
                    v = mm[turn % 2][:, 0:512].rearrange("p (k s) -> p k s", k=4)
                    copy(x_hi[0][:, 4 * g:4 * g + 4, LAT_OF[0]], v[:, :, 0:CAP_L])
                    copy(x_hi[1][:, 4 * g:4 * g + 4, LAT_OF[1]], v[:, :, CAP_L:]).then_inc(xhi_ready, 1)

                def hi_of_prompt(of):
                    for half in range(2):
                        last = copy(x_hi[half][:, :, PR_OF[half]],
                                    xe_p[:, :, bass.ds(CAP_P * (2 * of + half), CAP_P)])
                    last.then_inc(xhi_ready, 1)

                def silu(q, e, last_pair):
                    j = job_turn(q, last_pair)
                    rows_ = ROWS_OF[q // 2]
                    wait_mm_full(act, l, j, e)
                    act.activation(tmp[q % 2][0:rows_, 0:512], mm[j % 2][0:rows_, 0:512], ACT.Silu)\
                        .then_inc(silu_out, 1)

                def hi_of_hidden(q, turn, e):
                    rows_ = ROWS_OF[q // 2]
                    n = q % 2
                    wait_t_full(act, l, turn, e)
                    copy(hid_hi[:, 4 * n:4 * n + 4, 0:rows_],
                         tp[:, 0:512].rearrange("p (k s) -> p k s", k=4)[:, :, 0:rows_]).then_inc(hid_hi_ready, 1)

                def outputs(q, e, last_pair):
                    half = q - AO
                    j = job_turn(q, last_pair)
                    wait_mm_full(act, l, j, e)
                    if half == 0:
                        act.wait_ge(ye_stored, 32 * (l * PAIRS + e) + 32)
                    copy(ye_pr[PR_OF[half], :], mm[j % 2][PR_OF[half], :])
                    copy(ye[LAT_OF[half], :], mm[j % 2][LAT_OF[half], :]).then_inc(mm_empty[j % 2], 1)
                    act.drain()
                    if half == 1:
                        act.sem_inc(ye_done, 1)
                    act.dma_start(a["ye_pr"][2 * e + half], ye_pr[PR_OF[half], :]).then_inc(ye_stored, 16)

                def pair(e, last_pair=False):
                    m0, t0 = MM["pairs"] + 2, TR["pairs"] + 1
                    for n in range(2, PAIR_CHUNKS if last_pair else PAIR_CHUNKS + 2):
                        if n == PAIR_CHUNKS + 1:
                            outputs(BO, e, last_pair)
                        hi_of_chunk(n, e, last_pair)
                        if n == 5:
                            silu(AF0, e, last_pair)
                        if n == 9:
                            silu(AF1, e, last_pair)
                            hi_of_hidden(AF0, t0, e)
                        if n == 13:
                            silu(BF0, e, last_pair)
                            hi_of_hidden(AF1, t0 + 1, e)
                        if n == 17:
                            silu(BF1, e, last_pair)
                        if n == 21:
                            outputs(AO, e, last_pair)
                            hi_of_hidden(BF0, t0 + 2, e)
                            if not last_pair:
                                hi_of_tokens(m0 + G0, 0, e)
                            hi_of_hidden(BF1, t0 + 3, e)
                            if not last_pair:
                                hi_of_tokens(m0 + G1, 1, e)
                                hi_of_prompt(e + 1)
                    if last_pair:
                        outputs(BO, e, last_pair)
                    else:
                        wait_t_full(act, l, t0 + 4, e)
                        copy(hotw_t, tp[:, 0:NLAT]).then_inc(t_empty, 1)

                hi_of_chunk(0, 0)
                hi_of_chunk(1, 0)
                hi_of_tokens(MM["pairs"], 0, None)
                hi_of_tokens(MM["pairs"] + 1, 1, None)
                hi_of_prompt(0)
                wait_t_full(act, l, TR["pairs"])
                copy(hotw_t, tp[:, 0:NLAT]).then_inc(t_empty, 1)
                with act.Fori(0, PAIRS - 1) as e:
                    pair(e)
                pair(PAIRS - 1, True)
                act.wait_ge(ye_stored, 32 * PAIRS * l + (32 * PAIRS + 32))
                act.dma_start(ye_ptok, a["ye_pr"].rearrange("e s c -> (e s) c").rearrange("(g p) c -> p g c", p=P))\
                    .then_inc(ye_back, 16)

            act.wait_ge(x_ready, DEPTH * 2 + 1)
            squares(DEPTH, KT, 0, 0, lambda k: x[:, k, :])
            first_rstd(DEPTH, 0)
            for t in range(TT):
                wait_t_full(act, DEPTH, t)
                copy(tok[:, t, :], tp[:, :]).then_inc(t_empty, 1)
            act.drain()
            act.sem_inc(y_ready, 2)

        @block.vector
        def _(dve):
            def tt(out, in0, in1, op):
                return dve.tensor_tensor(out, in0, in1, op)

            def ts(out, in0, s1, op0, s2=None, op1=None):
                if op1 is None:
                    return dve.tensor_scalar(out, in0, s1, None, op0)
                return dve.tensor_scalar(out, in0, s1, s2, op0, op1)

            def stt(out, in0, s, in1, op0, op1):
                return dve.scalar_tensor_tensor(out=out, in0=in0, scalar=s, in1=in1, op0=op0, op1=op1)

            groups = ((0, NLAT, 0), (NLAT, T, 1))

            def refine_rstd(l, turn, n, width):
                wait_mm_full(dve, l, turn)
                ts(tmp[2][:, :], mm[turn % 2][:, 0:T], 1.0 / width, ALU.mult, EPS, ALU.add).then_inc(var_ready, 1)
                dve.drain()
                dve.sem_inc(mm_empty[turn % 2], 1)
                dve.wait_ge(r0_ready, l * PER_LAYER["r0_ready"] + (n + 1))
                tt(tmp[2][:, :], tmp[2][:, :], rstd[:, :], ALU.mult)
                dve.drain()
                tt(tmp[2][:, :], tmp[2][:, :], rstd[:, :], ALU.mult)
                dve.drain()
                ts(tmp[2][:, :], tmp[2][:, :], -0.5, ALU.mult, 1.5, ALU.add)
                dve.drain()
                tt(rstd[:, :], rstd[:, :], tmp[2][:, :], ALU.mult)
                dve.drain()

            def scale_h(n):
                for k in range(KT):
                    for lo, hi, g in groups:
                        last = stt(h[:, k, lo:hi], x[:, k, lo:hi], gain[:, n, k, g:g + 1], rstd[:, lo:hi],
                                   ALU.mult, ALU.mult)
                    last.then_inc(scaled, 1)

            def rope(l, j, dst, rows_, cos, sin):
                wait_mm_full(dve, l, j)
                tt(tmp[j % 2][rows_, 0:NLAT], mm[j % 2][rows_, 0:NLAT], sin, ALU.mult).then_inc(mm_empty[j % 2], 1)
                tt(dst, dst, cos, ALU.mult)
                dve.drain()
                return tt(dst, dst, tmp[j % 2][rows_, 0:NLAT], ALU.add)

            def merge(l, turn, first):
                for m in range(KT):
                    t_ = tmp[m % 2]
                    wait_mm_read(dve, l, turn + 2 * m)
                    ts(t_[:, :], t_[:, :], 1.0, ALU.add)
                    dve.drain()
                    dve.reciprocal(t_[:, :], t_[:, :])
                    dve.drain()
                    j = turn + 2 * m + 1
                    wait_mm_full(dve, l, j)
                    if first:
                        tt(merged[:, m, :], mm[j % 2][:, 0:T], t_[:, :], ALU.mult)
                    else:
                        tt(t_[:, :], mm[j % 2][:, 0:T], t_[:, :], ALU.mult)
                        dve.drain()
                        tt(merged[:, m, :], merged[:, m, :], t_[:, :], ALU.add)
                    dve.drain()
                    dve.sem_inc(mm_empty[j % 2], 1)
                dve.sem_inc(merged_ready, 1)

            def neg_max(l, j, width, at):
                wait_mm_full(dve, l, j)
                return dve.tensor_reduce(stat[:, at:at + 1], mm[j % 2][:, 0:width], AX.X, ALU.max, negate=True)

            def turn_probs(l, j, i, n):
                wait_t_full(dve, l, j)
                dve.tensor_copy(pt[:, i % 2, 0:n * P], tp[:, 0:n * P]).then_inc(t_empty, 1)

            for t in range(TT):
                dve.wait_ge(t_full, t + 1)
                dve.tensor_copy(x[:, :, t * P:(t + 1) * P],
                                tp[:, :].rearrange("p (k t) -> p k t", k=KT)).then_inc(t_empty, 1)
            dve.memset(ctx_in[:, :], 0.0)
            dve.drain()
            dve.sem_inc(x_ready, 1)
            dve.sem_inc(layer_free, 1)

            with dve.Fori(0, DEPTH) as l:
                wait_t_full(dve, l, TR["cols"])
                dve.tensor_copy(cols[:, :], tp[:, 0:NROWS])
                dve.drain()
                dve.sem_inc(t_empty, 1)
                dve.sem_inc(cols_ready, 1)
                dve.wait_ge(silu_e, l + 1)
                ts(silu_t[:, :], silu_t[:, :], 1.0, ALU.add)
                dve.drain()
                dve.reciprocal(silu_t[:, :], silu_t[:, :])
                dve.drain()
                for g, name in enumerate(("c", "c_ctx")):
                    lo, hi = ROWS[name]
                    last = tt(silu_c[:, :, g], silu_t[:, g * KT:(g + 1) * KT], cols[:, lo:hi], ALU.mult)
                last.then_inc(silu_ready, 1)
                tt(bc[:, 0:DH], bc[:, 0:DH], bc[:, DH:2 * DH], ALU.mult)
                tt(bc[:, 2 * DH:3 * DH], bc[:, 2 * DH:3 * DH], bc[:, 3 * DH:4 * DH], ALU.mult)
                dve.drain()
                dve.tensor_reduce(lam[:, 0:2], bc[:, 0:4 * DH].rearrange("p (g d) -> p g d", g=2)[:, :, 0:DH],
                                  AX.X, ALU.add).then_inc(lam_e, 1)
                dve.wait_ge(lam_e_done, l + 1)
                tt(lam[:, 4:5], lam[:, 3:4], lam[:, 2:3], ALU.subtract)
                dve.drain()
                tt(lam[:, 5:6], lam[:, 4:5], bc[:, 4 * DH + SW_H:4 * DH + SW_H + 1], ALU.subtract)
                tt(lam[:, 7:8], col("subln"), bc[:, 4 * DH + SW_H + 1:4 * DH + SW_H + 2], ALU.mult)
                b0 = ROWS["b_ada"][0]
                wait_t_full(dve, l, TR["ada"])
                tt(mod[:, :, :], tp[:, 0:96].rearrange("p (m g) -> p m g", g=2),
                   cols[:, b0:b0 + 48].unsqueeze(2).to_broadcast([P, 48, 2]), ALU.add).then_inc(t_empty, 1)
                dve.drain()
                for n, name in enumerate(("norm1", "norm2")):
                    lo, hi = ROWS[name]
                    for g in range(2):
                        stt(gain[:, n, :, g], mod[:, 24 * n + 8:24 * n + 16, g], 1.0, cols[:, lo:hi],
                            ALU.add, ALU.mult)
                dve.drain()
                refine_rstd(l, MM["norm1"], 0, D)
                scale_h(0)

                for m in range(8):
                    dst = da_q[:, m, 0:NLAT] if m < 4 else da_k[:, m - 4, 0:NLAT]
                    last = rope(l, MM["da_rot"] + m, dst, slice(0, P), c_("cos64"), c_("sin64"))
                last.then_inc(da_roped, 1)

                def mix(i):
                    width = T if i // DA_H < LT else P
                    s0 = 16 + 2 * (i % 4)
                    for m in range(2):
                        wait_mm_read(dve, l, MM["da_s"] + 2 * i + m)
                    dve.reciprocal(stat[:, s0:s0 + 2], stat[:, s0:s0 + 2])
                    dve.drain()
                    p1, p2 = da_p[i % 2][0][:, 0:width], da_p[i % 2][1][:, 0:width]
                    ts(p2, p2, stat[:, s0 + 1:s0 + 2], ALU.mult, lam[:, 5:6], ALU.mult)
                    dve.drain()
                    stt(p1, p1, stat[:, s0:s0 + 1], p2, ALU.mult, ALU.add).then_inc(p_mixed, 1)

                def da_keep(i):
                    t, hd = divmod(i, DA_H)
                    o = OO["da"] + i
                    dve.wait_ge(ss_ready, l * DA_N + (i + 1))
                    dve.tensor_copy(da_o[:, t % 2, hd * P:(hd + 1) * P], oo[o % 2][:, 0:P]).then_inc(o_empty[o % 2], 1)
                    if hd == DA_H - 1:
                        s0 = 32 + (t % 2) * 4
                        ts(stat[:, s0:s0 + 4], stat[:, s0:s0 + 4], 1.0 / P, ALU.mult, EPS, ALU.add).then_inc(rs_ln, 1)
                        r0 = stat[:, s0 + 8:s0 + 12]
                        v = stat[:, s0:s0 + 4]
                        dve.drain()
                        dve.wait_ge(rs_done, l * TT + (t + 1))
                        tt(v, v, r0, ALU.mult)
                        dve.drain()
                        tt(v, v, r0, ALU.mult)
                        dve.drain()
                        ts(v, v, -0.5, ALU.mult, 1.5, ALU.add)
                        dve.drain()
                        tt(r0, r0, v, ALU.mult)
                        dve.drain()
                        o_ = da_o[:, t % 2, :].rearrange("p (h d) -> p h d", h=DA_H)
                        tt(o_, o_, r0.unsqueeze(2).to_broadcast([P, DA_H, P]), ALU.mult).then_inc(o_ready, 1)

                for s in range(DA_N + 2):
                    if 1 <= s <= DA_N:
                        mix(s - 1)
                    if s < DA_N:
                        for m in range(2):
                            neg_max(l, MM["da_s"] + 2 * s + m, T if s // DA_H < LT else P, 2 * (s % 4) + m)\
                                .then_inc(nm_ready, 1)
                    if s >= 2:
                        da_keep(s - 2)
                merge(l, MM["da_out"], True)

                refine_rstd(l, MM["mla_norm"], 1, QR)
                for m in range(2):
                    last = stt(cq[:, m, :], cq[:, m, :], col("q_norm", m), rstd[:, :], ALU.mult, ALU.mult)
                last.then_inc(c_normed, 1)
                dve.drain()
                refine_rstd(l, MM["mla_norm"] + 1, 2, KVR)
                stt(ckv[:, 0:NLAT], ckv[:, 0:NLAT], col("kv_norm"), rstd[:, 0:NLAT], ALU.mult, ALU.mult)
                stt(ckv[:, T:KEYS], ckv[:, T:KEYS], col("kv_norm"), rstd[:, NLAT:T], ALU.mult, ALU.mult)\
                    .then_inc(c_normed, 1)
                r32 = slice(MNOPE, MQ)
                wait_t_read(dve, l, TR["mla_ctx"])
                rope(l, MM["kr_rot"], ml_k[0][r32, 0:NLAT], r32, c_("cos32", r32), c_("sin32", r32))
                dve.drain()
                dve.tensor_copy(ml_k[1][r32, :], ml_k[0][r32, :]).then_inc(kr_ready, 1)

                def rope_head(hd):
                    rope(l, mla_prep(hd) + 2, ml_q[hd % 2][r32, 0:NLAT], r32, c_("cos32", r32), c_("sin32", r32))\
                        .then_inc(mq_roped, 1)

                def mla_keep(i):
                    hd, t = divmod(i, TT)
                    o = OO["mla"] + i
                    s0 = 16 + i % 8
                    dve.reciprocal(stat[:, s0:s0 + 1], stat[:, s0:s0 + 1])
                    dve.drain()
                    wait_o_full(dve, l, o)
                    ts(ml_otok[:, t, hd * MV:(hd + 1) * MV], oo[o % 2][:, 0:MV], stat[:, s0:s0 + 1], ALU.mult)\
                        .then_inc(o_empty[o % 2], 1)

                rope_head(0)
                for s in range(MLA_N + 2):
                    if s < MLA_N:
                        hd, t = divmod(s, TT)
                        if t == 2 and hd < MH - 1:
                            rope_head(hd + 1)
                        neg_max(l, mla_s(s), T if t < LT else P, s % 8).then_inc(nm_ready, 1)
                    if 1 <= s <= MLA_N and s % 2 == 1:
                        turn_probs(l, TR["mla"] + MLA_TP[s - 1], s - 1, 5 if (s - 1) % TT < LT else 1)
                    if s >= 2:
                        wait_mm_read(dve, l, mla_s(s - 2))
                        mla_keep(s - 2)
                dve.drain()
                dve.sem_inc(o_ready, TT)
                merge(l, MM["mla_out"], False)

                for m in range(5):
                    dst = sw_q[:, m, 0:NLAT] if m < 4 else sw_kraw[:, 0:NLAT]
                    rope(l, MM["sw_rot"] + m, dst, slice(0, P), c_("cos64"), c_("sin64"))
                dve.drain()
                wait_t_read(dve, l, TR["sw_ctx"])
                for g in range(2):
                    for half in range(2):
                        last = dve.tensor_copy(sw_k[half * DH:(half + 1) * DH, g, :], sw_kraw[g * DH:(g + 1) * DH, :])
                last.then_inc(sw_roped, 1)
                sinks = bc[:, 4 * DH:4 * DH + SW_H]
                ts(stat[:, 48:56], sinks, -1.0, ALU.mult)
                dve.drain()

                def win_tiles(t):
                    return 1 if t == PRT else min(t + 1, LT - 1) - max(t - 1, 0) + 2

                def sw_keep(i):
                    t, hd = divmod(i, SW_H)
                    o = OO["sw"] + i
                    wait_o_full(dve, l, o)
                    dve.tensor_copy(sw_o[:, t % 2, hd * DH:(hd + 1) * DH], oo[o % 2][:, 0:DH])\
                        .then_inc(o_empty[o % 2], 1)
                    if hd == SW_H - 1:
                        dve.drain()
                        o_ = sw_o[:, t % 2, :].rearrange("p (h d) -> p h d", h=SW_H)
                        r = stat[:, 56:64]
                        tt(o_, o_, r.unsqueeze(2).to_broadcast([P, SW_H, DH]), ALU.mult).then_inc(o_ready, 1)

                for s in range(SW_N + 2):
                    if s < SW_N:
                        t, hd = divmod(s, SW_H)
                        if hd == 0 and t > 0:
                            wait_mm_read(dve, l, MM["sw_s"] + s - 1)
                            dve.wait_ge(sink_e, l * TT + t)
                            tt(stat[:, 56:64], stat[:, 16:24], stat[:, 40:48], ALU.add)
                            dve.drain()
                            dve.reciprocal(stat[:, 56:64], stat[:, 56:64])
                            dve.drain()
                        neg_max(l, MM["sw_s"] + s, win_tiles(t) * P, hd)
                        dve.drain()
                        tt(stat[:, hd:hd + 1], stat[:, hd:hd + 1], stat[:, 48 + hd:49 + hd], ALU.min)
                        dve.drain()
                        dve.sem_inc(nm_ready, 1)
                        if hd == SW_H - 1:
                            tt(stat[:, 32:40], sinks, stat[:, 0:8], ALU.add).then_inc(sink_in, 1)
                    if 1 <= s <= SW_N and s % 2 == 1:
                        turn_probs(l, TR["sw"] + SW_TP[s - 1], s - 1, win_tiles((s - 1) // SW_H))
                    if s == SW_N:
                        wait_mm_read(dve, l, MM["sw_s"] + SW_N - 1)
                        dve.wait_ge(sink_e, l * TT + TT)
                    if s >= 2:
                        if s == SW_N + 1:
                            tt(stat[:, 56:64], stat[:, 16:24], stat[:, 40:48], ALU.add)
                            dve.drain()
                            dve.reciprocal(stat[:, 56:64], stat[:, 56:64])
                        sw_keep(s - 2)
                merge(l, MM["sw_out"], False)

                for m in range(KT):
                    j = MM["o"] + m
                    wait_mm_full(dve, l, j)
                    for lo, hi, g in groups:
                        last = stt(x[:, m, lo:hi], mm[j % 2][:, lo:hi], mod[:, 16 + m, g:g + 1], x[:, m, lo:hi],
                                   ALU.mult, ALU.add)
                    last.then_inc(mm_empty[j % 2], 1)
                dve.drain()
                dve.sem_inc(x_ready, 1)

                refine_rstd(l, MM["norm2"], 3, D)
                scale_h(1)
                j = MM["router"]
                wait_mm_full(dve, l, j)
                lg = mm[j % 2][:, 0:TT * NE].rearrange("p (t e) -> p t e", e=NE)
                dve.tensor_reduce(stat[:, 0:TT], lg, AX.X, ALU.max)
                dve.drain()
                tt(aff[:, :, :], lg, stat[:, 0:TT].unsqueeze(2).to_broadcast([P, TT, NE]), ALU.subtract)\
                    .then_inc(mm_empty[j % 2], 1)
                dve.drain()
                dve.sem_inc(lg_ready, 1)
                dve.wait_ge(lg_e, l + 1)
                dve.tensor_reduce(stat[:, 0:TT], aff[:, :, :], AX.X, ALU.add)
                dve.drain()
                dve.reciprocal(stat[:, 0:TT], stat[:, 0:TT])
                dve.drain()
                tt(aff[:, :, :], aff[:, :, :], stat[:, 0:TT].unsqueeze(2).to_broadcast([P, TT, NE]), ALU.mult)\
                    .then_inc(aff_ready, 1)
                e16 = slice(0, NE)
                dve.wait_ge(v_sent, l * 32 + 32)
                wait_t_full(dve, l, TR["aff"])
                dve.tensor_copy(work_e[e16, :], tp[e16, 0:T]).then_inc(t_empty, 1)
                dve.memset(ones_e[e16, :], 1.0)
                dve.drain()
                for lo, hi, rounds in ((0, NLAT, CAP_L // 8), (NLAT, T, CAP_P // 8)):
                    for _ in range(rounds):
                        dve.max(top8[e16, :], work_e[e16, lo:hi])
                        dve.drain()
                        dve.match_replace(work_e[e16, lo:hi], top8[e16, :], work_e[e16, lo:hi], -1.0)
                        dve.drain()
                ts(mask_e[e16, :], work_e[e16, :], 0.0, ALU.is_lt)
                dve.drain()
                for lo, hi, _ in groups:
                    dve.tensor_tensor_scan(cum_e[e16, lo:hi], ones_e[e16, lo:hi], mask_e[e16, lo:hi], 0.0,
                                           ALU.mult, ALU.add)
                dve.drain()
                tt(cum_e[e16, :], cum_e[e16, :], mask_e[e16, :], ALU.mult)
                dve.drain()
                ts(cum_e[e16, :], cum_e[e16, :], -1.0, ALU.add).then_inc(pos_ready, 1)
                wait_t_full(dve, l, TR["pos"])
                dve.tensor_copy(pos_t[:, :, :], tp[:, 0:TT * NE].rearrange("p (t e) -> p t e", e=NE)).then_inc(t_empty, 1)
                dve.drain()
                lo, _ = CONST["iota"]
                tt(hot_p, const[:, lo:lo + CAP_P].unsqueeze(1).to_broadcast([P, NE, CAP_P]),
                   pos_t[:, PRT, :].unsqueeze(2).to_broadcast([P, NE, CAP_P]), ALU.is_equal)
                dve.drain()
                tt(hotw_p, hot_p, aff[:, PRT, :].unsqueeze(2).to_broadcast([P, NE, CAP_P]), ALU.mult)\
                    .then_inc(hotp_ready, 1)

                for v in (x_hi[1], x_lo[1]):
                    dve.memset(v[:, :, CAP_P:P - CAP_L].bitcast(FP32), 0.0)

                def f(v):
                    return v.bitcast(FP32)

                def select(of):
                    for half in range(2):
                        last = tt(hot[:, :, half, :], c_("iota").unsqueeze(1).to_broadcast([P, LT, CAP_L]),
                                  pos_t[:, 0:LT, bass.ds(2 * of + half, 1)].to_broadcast([P, LT, CAP_L]),
                                  ALU.is_equal)
                    last.then_inc(hot_ready, 1)

                def weigh(of):
                    for half in range(2):
                        last = tt(hotw[:, :, half, :], hot[:, :, half, :],
                                  aff[:, 0:LT, bass.ds(2 * of + half, 1)].to_broadcast([P, LT, CAP_L]), ALU.mult)
                    last.then_inc(hotw_ready, 1)

                def lo_of_chunk(n, e):
                    i = N_DENSE + n
                    for u in range(UNITS):
                        m = UNITS * n + u
                        dve.wait_ge(w_hi_ready, (l * PAIRS + e) * PAIR_UNITS + (m + 1))
                        tt(w_lo[m % SPLITS][:, :, :], ring[i % RING][:, u * UK:(u + 1) * UK, :],
                           f(w_hi[m % SPLITS][:, :, :]), ALU.subtract).then_inc(w_ready, 1)

                def lo_of_tokens(turn, g, e, of):
                    dve.wait_ge(xhi_ready, (l * PAIRS + of) * 3 + (g + 1))
                    v = mm[turn % 2][:, 0:512].rearrange("p (k s) -> p k s", k=4)
                    for half in range(2):
                        cs = LAT_OF[half]
                        last = tt(x_lo[half][:, 4 * g:4 * g + 4, cs], v[:, :, half * CAP_L:(half + 1) * CAP_L],
                                  f(x_hi[half][:, 4 * g:4 * g + 4, cs]), ALU.subtract)
                    last.then_inc(mm_empty[turn % 2], 1)

                def lo_of_prompt(of):
                    dve.wait_ge(xhi_ready, (l * PAIRS + of) * 3 + 3)
                    for half in range(2):
                        cs = PR_OF[half]
                        last = tt(x_lo[half][:, :, cs], xe_p[:, :, bass.ds(CAP_P * (2 * of + half), CAP_P)],
                                  f(x_hi[half][:, :, cs]), ALU.subtract)
                    dve.drain()
                    dve.sem_inc(xe_ready, 1)

                def hidden(q, e, last_pair):
                    j = job_turn(q, last_pair)
                    rows_ = ROWS_OF[q // 2]
                    n = q % 2
                    dve.wait_ge(silu_out, (l * PAIRS + e) * 4 + (q + 1))
                    tt(hid[0:rows_, n * 512:(n + 1) * 512], mm[j % 2][0:rows_, 512:1024], tmp[n][0:rows_, 0:512],
                       ALU.mult).then_inc(mm_empty[j % 2], 1)
                    dve.drain()
                    dve.sem_inc(hid_ready, 1)

                def lo_of_hidden(q, e):
                    rows_ = ROWS_OF[q // 2]
                    n = q % 2
                    dve.wait_ge(hid_hi_ready, (l * PAIRS + e) * 4 + (q + 1))
                    tt(hid_lo[:, 4 * n:4 * n + 4, 0:rows_],
                       tp[:, 0:512].rearrange("p (k s) -> p k s", k=4)[:, :, 0:rows_],
                       f(hid_hi[:, 4 * n:4 * n + 4, 0:rows_]), ALU.subtract).then_inc(t_empty, 1)

                def pair(e, last_pair=False):
                    m0, t0 = MM["pairs"] + 2, TR["pairs"] + 1
                    for n in range(2, PAIR_CHUNKS if last_pair else PAIR_CHUNKS + 2):
                        lo_of_chunk(n, e)
                        if n == 3 and not last_pair:
                            select(e + 1)
                            dve.drain()
                            weigh(e + 1)
                        if n == 5:
                            hidden(AF0, e, last_pair)
                        if n == 9:
                            hidden(AF1, e, last_pair)
                            lo_of_hidden(AF0, e)
                        if n == 13:
                            hidden(BF0, e, last_pair)
                            lo_of_hidden(AF1, e)
                        if n == 17:
                            hidden(BF1, e, last_pair)
                        if n == 21:
                            lo_of_hidden(BF0, e)
                            if not last_pair:
                                lo_of_tokens(m0 + G0, 0, e, e + 1)
                            lo_of_hidden(BF1, e)
                            if not last_pair:
                                lo_of_tokens(m0 + G1, 1, e, e + 1)
                                lo_of_prompt(e + 1)
                    for k in range(KT):
                        j = OO["pairs"] + k
                        wait_o_full(dve, l, j, e)
                        stt(x[:, k, 0:NLAT], oo[j % 2][:, :], mod[:, 40 + k, 0:1], x[:, k, 0:NLAT], ALU.mult, ALU.add)\
                            .then_inc(o_empty[j % 2], 1)
                    dve.drain()

                select(0)
                dve.drain()
                weigh(0)
                lo_of_chunk(0, 0)
                lo_of_chunk(1, 0)
                lo_of_tokens(MM["pairs"], 0, None, 0)
                lo_of_tokens(MM["pairs"] + 1, 1, None, 0)
                lo_of_prompt(0)
                with dve.Fori(0, PAIRS - 1) as e:
                    pair(e)
                pair(PAIRS - 1, True)
                j = MM["combine_p"]
                wait_mm_full(dve, l, j)
                for k in range(KT):
                    stt(x[:, k, NLAT:T], mm[j % 2][:, k * P:(k + 1) * P], mod[:, 40 + k, 1:2], x[:, k, NLAT:T],
                        ALU.mult, ALU.add)
                dve.drain()
                for s in (mm_empty[j % 2], x_ready, small_free, layer_free):
                    dve.sem_inc(s, 1)

            refine_rstd(DEPTH, 0, 0, D)
            for k in range(KT):
                last = stt(h[:, k, :], x[:, k, :], col("final", k), rstd[:, :], ALU.mult, ALU.mult)
            last.then_inc(h_ready, 1)

        return nc


_INS = ["x_prompt", "x_sample", "cache_da_k", "cache_da_v", "cache_mla_ckv", "cache_mla_krope",
        "cache_swa_k", "cache_swa_v", "c", "c_ctx", "w_ada", "b_ada", "norm1", "norm2", "w_in",
        "da_lq1", "da_lk1", "da_lq2", "da_lk2", "da_subln", "mla_q_norm", "mla_w_qb", "mla_kv_norm",
        "mla_w_kvb", "swa_sink", "w_gate", "w_br_da", "w_br_mla", "w_br_swa", "w_o", "w_router",
        "w_ff1", "w_ff3", "w_ff2", "final_norm"]
_OUTS = [("y_prompt", (1, NPR, D)), ("y_sample", (1, NLAT, D)),
         ("new_da_k", (1, DEPTH, NPR, DA_H, 2 * DH)), ("new_da_v", (1, DEPTH, NPR, DA_H, 2 * DH)),
         ("new_mla_ckv", (1, DEPTH, NPR, KVR)), ("new_mla_krope", (1, DEPTH, NPR, MROPE)),
         ("new_swa_k", (1, DEPTH, NPR, SW_KV, DH)), ("new_swa_v", (1, DEPTH, NPR, SW_KV, DH))]


def kernel(**inputs):
    import concourse.bacc as _bacc
    from concourse.bass_utils import run_bass_kernel_spmd as _run

    nc = _bacc.Bacc("TRN2", target_bir_lowering=False, num_devices=1)
    table, lam = shape_constants()
    arrays, a = {}, {}
    for name, value in [(n, inputs[n]) for n in _INS] + [("const", table), ("lam", lam)]:
        v = np.ascontiguousarray(value)
        arrays[f"in_{name}"] = v
        a[name] = nc.dram_tensor(f"in_{name}", v.shape, mybir.dt.from_np(v.dtype), kind="ExternalInput").ap()
    for name, shape in _OUTS:
        a[name] = nc.dram_tensor(f"out_{name}", shape, FP32, kind="ExternalOutput").ap()
    a["ye_pr"] = nc.dram_tensor("ye_pr_rows", (NE, CAP_P, D), FP32, kind="Internal").ap()
    build(nc, a)
    r = _run(nc, [arrays], core_ids=[0])
    return tuple(r.results[0][f"out_{name}"] for name, _ in _OUTS)
```

```python
import math
from contextlib import ExitStack

import numpy as np

import concourse.bass as bass
from concourse import mybir

FP32 = mybir.dt.float32
FP32R = mybir.dt.float32r
ALU = mybir.AluOpType
ACT = mybir.ActivationFunctionType
AX = mybir.AxisListType

P = 128
D = 1024
KT = D // P
DEPTH = 2
NLAT, NPR, NCTX = 512, 128, 128
T = NLAT + NPR
TT = T // P
PRT = TT - 1
LT = NLAT // P
KEYS = NLAT + NCTX + NPR
KEY_TILES = KEYS // P
GRID_W = 64
ROPE_BASE = 10000.0
EPS = 1e-6
DA_H, DH = 4, 64
QR, KVR, MROPE, MNOPE, MV, MH = 256, 128, 32, 64, 64, 8
MQ = MNOPE + MROPE
SW_H, SW_KV = 8, 2
BR = 512
IN_COLS = 3 * BR + QR + KVR + MROPE + SW_H * DH + 2 * SW_KV * DH
MLA_AT = 3 * BR
SWQ_AT = MLA_AT + QR + KVR + MROPE
SWK_AT = SWQ_AT + SW_H * DH
SWV_AT = SWK_AT + SW_KV * DH
NE, FF = 16, 1024
CAP_L, CAP_P = 2 * NLAT // NE, 2 * NPR // NE
CAP = CAP_L + CAP_P
PAIRS = NE // 2
SLOTS_P = NE * CAP_P
NEG = -1.0e30

RING = 6
HALF = 4
CHUNK = HALF * 512


def _layout(parts):
    at, out = 0, {}
    for name, width in parts:
        out[name] = (at, at + width)
        at += width
    return out, at


CONST, CONST_COLS = _layout([
    ("ident", P), ("swap", P), ("swap32", MROPE), ("ones", P), ("mask_before", P), ("mask_after", P),
    ("iota", CAP_L), ("cos64", NLAT), ("sin64", NLAT), ("cos32", NLAT), ("sin32", NLAT)])

ROWS, NROWS = _layout([
    ("b_ada", 48), ("norm1", KT), ("norm2", KT), ("q_norm", 2), ("kv_norm", 1), ("subln", 1),
    ("final", KT), ("c", KT), ("c_ctx", KT)])


def shape_constants():
    t = np.zeros((P, CONST_COLS), np.float32)

    def put(name, rows, value):
        a, b = CONST[name]
        t[rows, a:b] = value

    p = np.arange(P)
    put("ident", slice(0, P), np.eye(P))
    swap = np.zeros((P, P), np.float32)
    swap[p[1::2], p[0::2]] = -1.0
    swap[p[0::2], p[1::2]] = 1.0
    put("swap", slice(0, P), swap)
    put("swap32", slice(MNOPE, MQ), swap[:MROPE, :MROPE])
    put("ones", slice(0, P), 1.0)
    put("mask_before", slice(0, P), np.where(p[None, :] >= p[:, None], 0.0, NEG))
    put("mask_after", slice(0, P), np.where(p[None, :] <= p[:, None], 0.0, NEG))
    put("iota", slice(0, P), np.arange(CAP_L))
    tok = np.arange(NLAT)
    row, col = (tok // GRID_W).astype(np.float32), (tok % GRID_W).astype(np.float32)

    def angles(rot):
        n = rot // 4
        inv = (np.float32(ROPE_BASE) ** (-np.arange(n, dtype=np.float32) / np.float32(n))).astype(np.float32)
        ang = np.concatenate([row[:, None] * inv, col[:, None] * inv], axis=-1)
        return np.repeat(ang, 2, axis=1).T.astype(np.float32)

    a64 = angles(DH)
    a64 = np.concatenate([a64, a64])
    a32 = angles(MROPE)
    put("cos64", slice(0, P), np.cos(a64))
    put("sin64", slice(0, P), np.sin(a64))
    put("cos32", slice(MNOPE, MQ), np.cos(a32))
    put("sin32", slice(MNOPE, MQ), np.sin(a32))
    lam = np.array([[0.8 - 0.6 * math.exp(-0.3 * l) for l in range(DEPTH)]]).T
    lam = np.concatenate([lam, 1.0 - lam], axis=1).astype(np.float32)
    return t, lam


def layer_chunks():
    out = []

    def block(kind, c0, width=512):
        out.append((kind, 0, c0, width))
        out.append((kind, HALF, c0, width))

    def gates(b, branch):
        for mb in range(2):
            block("gate", b * D + mb * 512)
            out.append((branch, 0, mb * 512, 512))

    for b in range(12):
        block("ada", b * 512)
    for b in (2, 0, 1):
        block("in", b * BR)
    gates(0, "br_da")
    block("in", MLA_AT, QR + KVR + MROPE)
    block("in", SWQ_AT)
    out.append(("qb", 0, 0, MH * MQ))
    out.append(("kvb", 0, 0, MH * (MNOPE + MV)))
    gates(1, "br_mla")
    block("in", SWK_AT, 2 * SW_KV * DH)
    gates(2, "br_swa")
    for b in range(2):
        block("o", b * 512)
    return out


CHUNKS = layer_chunks()
FIRST = {}
for _i, _c in enumerate(CHUNKS):
    FIRST.setdefault(_c[0], _i)
N_DENSE = len(CHUNKS)
PAIR_CHUNKS = 2 * 12
LAYER_CHUNKS = N_DENSE + PAIRS * PAIR_CHUNKS
PAIR_SLOT = N_DENSE % RING
assert PAIR_CHUNKS % RING == 0
assert LAYER_CHUNKS % RING == PAIR_SLOT


def _turns(parts):
    at, out = 0, {}
    for name, n in parts:
        out[name] = at
        at += n
    return out, at


DA_N, SW_N, MLA_N = TT * DA_H, TT * SW_H, TT * MH
PAIR_MM, PAIR_T, PAIR_O = 8, 4, 8
MM, _mm_dense = _turns([
    ("ada", 13), ("da_v", TT), ("da_q", 4), ("da_k_rot", 12), ("da_s", 2 * DA_N),
    ("da_out", 16), ("mla_in", 10), ("kr_rot", 1), ("mla_v", KEY_TILES),
    ("mla_heads", MLA_N + 3 * MH), ("mla_out", 16), ("sw_kv_rot", 7),
    ("sw_s", SW_N), ("sw_out", 16), ("o", 8), ("norm2", 1), ("router", 1), ("gather_p", 2),
    ("pairs", 0)])
MM["combine_p"] = _mm_dense + PAIRS * PAIR_MM
MM_LAYER = MM["combine_p"] + 1
MM_USES = [(MM_LAYER + 1) // 2, MM_LAYER // 2]
T_BEFORE = TT
TR, _t_dense = _turns([
    ("cols", 1), ("ada", 1), ("da_ctx", 1), ("da_new", 1), ("da", DA_N + TT), ("mla_ctx", 1), ("mla_new", 1),
    ("mla", MLA_N + TT), ("sw_ctx", 1), ("sw_vt", 1), ("sw_new", 1), ("sw", SW_N + TT), ("lg", 1), ("aff", 1), ("h_tok", TT),
    ("pos", 1), ("hot_p", 1), ("pairs", 0)])
T_LAYER = _t_dense + PAIRS * PAIR_T
OO, _o_dense = _turns([("da", DA_N), ("mla", MLA_N), ("sw", SW_N), ("pairs", 0)])
O_LAYER = _o_dense + PAIRS * PAIR_O
O_USES = [O_LAYER // 2, O_LAYER // 2]
assert O_LAYER % 2 == 0 and _o_dense % 2 == 0


NORM1_AT = 7
MM["norm1"] = MM["ada"] + NORM1_AT


SW_Q = [MM["mla_in"] + n for n in (4, 6, 8, 9)]
MLA_NORM = [MM["mla_in"] + n for n in (5, 7)]


DA_K = [MM["da_k_rot"] + 2 * m + 1 for m in range(4)]
DA_ROT = [MM["da_k_rot"] + (2 * m if m < 4 else 4 + m) for m in range(8)]
SW_K, SW_V = MM["sw_kv_rot"] + 2, MM["sw_kv_rot"] + 5
SW_ROT = [MM["sw_kv_rot"] + n for n in (0, 1, 3, 4, 6)]

H_TILES, H_AT = [], {}


def _h_tiles(name, turns, chunks, cols):
    H_AT[name] = len(H_TILES)
    for t_, c_, (c0, width) in zip(turns, chunks, cols):
        H_TILES.append((t_, c_, c0, width))


_four = [(m * P, P) for m in range(4)]
_h_tiles("da_q", [MM["da_q"] + m for m in range(4)], [FIRST["in"] + 2] * 4, _four)
_h_tiles("da_k", DA_K, [FIRST["in"] + 4] * 4, _four)
_h_tiles("da_gate", [MM["da_out"] + 2 * m for m in range(KT)], [FIRST["br_da"] - 2 + 3 * (m // 4) for m in range(KT)],
         _four * 2)
_h_tiles("mla_in", [MM["mla_in"] + m for m in range(4)], [FIRST["qb"] - 4] * 4,
         _four[:3] + [(3 * P - MNOPE, MQ)])
_h_tiles("sw_q", SW_Q, [FIRST["qb"] - 2] * 4, _four)
_h_tiles("mla_gate", [MM["mla_out"] + 2 * m for m in range(KT)], [FIRST["br_mla"] - 2 + 3 * (m // 4) for m in range(KT)],
         _four * 2)
_h_tiles("sw_kv", [SW_K, SW_V], [FIRST["br_swa"] - 4] * 2, _four[:2])
_h_tiles("sw_gate", [MM["sw_out"] + 2 * m for m in range(KT)], [FIRST["br_swa"] - 2 + 3 * (m // 4) for m in range(KT)],
         _four * 2)
H_N = len(H_TILES)


def ada_turn(b):
    return MM["ada"] + b + (1 if b >= NORM1_AT else 0)


AF0, AF1, BF0, BF1, AO, BO = range(6)
UNITS = 2
SPLITS = 4
UK = HALF // UNITS
PAIR_UNITS = PAIR_CHUNKS * UNITS
JOB_UNITS = 4 * UNITS
USED_PAIR = PAIR_UNITS - 6
ADA_JOB = 2 * UNITS
ADA_UNITS = 12 * ADA_JOB
LAYER_UNITS = ADA_UNITS + PAIRS * PAIR_UNITS
LAYER_USED = ADA_UNITS - 12 + PAIRS * USED_PAIR
G0, G1 = 5, 6
COMBINE_AT = JOB_UNITS


def job_turn(q, last):
    return MM["pairs"] + 2 + (q if q < BO else (5 if last else 7))


def mla_s(i):
    h, t = divmod(i, TT)
    return MM["mla_heads"] + 3 + h * (TT + 3) + t + (min(t, 3) if h < MH - 1 else 0)


def mla_prep(h, piece):
    return MM["mla_heads"] + (piece if h == 0 else 3 + (h - 1) * (TT + 3) + 1 + 2 * piece)


def t_order(n, per_tile, every):
    p, o, at = {}, {}, 0
    for s in range(n + 2):
        if 1 <= s <= n:
            p[s - 1] = at
            at += 1
        if every and s >= per_tile + 3 and (s - 3) % per_tile == 0:
            o[(s - 3) // per_tile - 1] = at
            at += 1
    for t in range(TT):
        if t not in o:
            o[t] = at
            at += 1
    return p, o


DA_TP, DA_TO = t_order(DA_N, DA_H, False)
SW_TP, SW_TO = t_order(SW_N, SW_H, True)
MLA_TP, MLA_TO = t_order(MLA_N, MH, False)

NEW_STORES = 4
SMALL_LOADS = 15
NM_LAYER = 2 * DA_N + MLA_N + SW_N
PER_LAYER = {
    "sq_ready": 2 * KT + 3, "sq_used": 2 * (KT - 1) + 1, "var_ready": 4, "r0_ready": 4,
    "scaled": 2 * KT, "h_ready": 2 * KT,
}


def build(nc, a):
    ctx = ExitStack()
    with ctx:
        place = {}

        def sb(name, shape):
            cols_ = int(np.prod(shape[1:]))
            t = nc.alloc_sbuf_tensor_at(name, shape, FP32, offset=arena_at + place["end"])
            place[name] = arena_at + place["end"]
            place["end"] += (cols_ * 4 + 31) // 32 * 32
            assert place["end"] <= ARENA * 4, place["end"]
            return t

        def rounded(name, host, at, shape):
            return nc.alloc_sbuf_tensor_at(name, shape, FP32R, offset=place[host] + 4 * at)

        ARENA = 53184
        arena_at = (nc.sbuf_base + 31) // 32 * 32
        ctx.enter_context(nc.sbuf_tensor("arena", [P, ARENA], FP32))
        place["end"] = 0

        def sem(name):
            return ctx.enter_context(nc.semaphore(name))

        ring = [sb(f"ring{i}", [P, HALF, 512]) for i in range(RING)]
        x = sb("x", [P, KT, T])
        h = sb("h", [P, KT, T])
        merged = sb("merged", [P, KT, T])
        tok = merged[:, :, :].rearrange("p k t -> p (k t)").rearrange("p (t c) -> p t c", c=D)
        SCRATCH = 15872
        scratch = sb("scratch", [P, SCRATCH])
        pt = sb("pt", [P, 2, T])
        h_hi = rounded("h_hi", "x", 0, [P, KT, NLAT])
        h_lo = rounded("h_lo", "h", 0, [P, KT, T])
        dw_lo = [rounded(f"dw_lo{i}", "x", KT * NLAT + i * HALF * P, [P, HALF, P]) for i in range(2)]
        dw_hi = [rounded(f"dw_hi{i}", "pt", i * HALF * P, [P, HALF, P]) for i in range(2)]
        tmp = [sb(f"tmp{i}", [P, T]) for i in range(3)]
        rstd = tmp_r = sb("rstd", [P, T])
        const = sb("const", [P, CONST_COLS])
        rows = sb("rows", [NROWS, P])
        cols = sb("cols", [P, NROWS])
        mod = sb("mod", [P, 48, 2])
        gain = sb("gain", [P, 2, KT, 2])
        sb("silu_c", [P, 2, KT, 2])
        c_hi = nc.alloc_sbuf_tensor_at("c_hi", [P, KT, 2], FP32R, offset=place["silu_c"])
        c_lo = nc.alloc_sbuf_tensor_at("c_lo", [P, KT, 2], FP32R, offset=place["silu_c"] + 8 * KT)
        silu_t = sb("silu_t", [P, 2 * KT])
        bc = sb("bc", [P, 4 * DH + SW_H + 2])
        lam = sb("lam", [P, 8])
        ctx_in = sb("ctx_in", [P, 352])
        new_out = sb("new_out", [P, 512])
        stat = sb("stat", [P, 64])
        wr = sb("wr", [P, KT, NE])
        pos_t = sb("pos_t", [P, TT, NE])
        aff = sb("aff", [P, TT, NE])

        def c_(name, rows_=slice(0, P)):
            lo, hi = CONST[name]
            return const[rows_, lo:hi]

        def col(name, k=0):
            lo = ROWS[name][0]
            return cols[:, lo + k:lo + k + 1]

        def view(at, *shape):
            n = int(np.prod(shape))
            assert at + n <= SCRATCH, (at, shape)
            v = scratch[:, at:at + n]
            if len(shape) == 1:
                return v
            if len(shape) == 2:
                return v.rearrange("p (a b) -> p a b", b=shape[1])
            return v.rearrange("p (a b c) -> p a b c", b=shape[1], c=shape[2])

        ident = c_("ident")
        ones = c_("ones")

        da_q, da_k = view(0, 4, T), view(2560, 4, KEYS)
        da_v = view(5632, KEY_TILES, 512)
        da_o = view(12288, TT, 512)
        da_ss, da_r0 = view(14848, DA_N), view(14880, DA_N)
        da_p = [[view(9728 + (2 * i + m) * T, T) for m in range(2)] for i in range(2)]
        da_ctx = view(0, 512)
        cq, ckv = view(0, 2, T), view(1280, KEYS)
        ml_v = view(2048, KEY_TILES, 512)
        ml_q = [view(5120 + i * T, T) for i in range(2)]
        ml_k = [view(6400 + i * KEYS, KEYS) for i in range(2)]
        ml_otok = view(7936, TT, 512)
        ml_p = [view(10496 + i * T, T) for i in range(2)]
        ml_o = view(2048, 4, T)
        sw_q, sw_kraw = view(12288, 4, T), view(2560, KEYS)
        sw_k = view(3328, 2, KEYS)
        sw_v = view(4864, KEY_TILES, SW_KV * DH)
        sw_o = view(5632, 2, 512)
        sw_vraw = view(6656, T)
        sw_p = [view(6656 + i * 512, 512) for i in range(2)]
        ada_row = view(9728, 6 * D)
        xe_p = view(0, KT, SLOTS_P)
        ye_ptok = view(0, 2, D)
        w_lo = [rounded(f"w_lo{i}", "scratch", 2048 + i * UK * 512, [P, UK, 512]) for i in range(SPLITS)]
        w_hi = [rounded(f"w_hi{i}", "h", i * UK * 512, [P, UK, 512]) for i in range(SPLITS)]
        x_hi = [rounded("xa_hi", "scratch", 6144, [P, KT, CAP]), rounded("xb_hi", "scratch", 7424, [P, KT, P])]
        x_lo = [rounded("xa_lo", "scratch", 6784, [P, KT, CAP]), rounded("xb_lo", "scratch", 8448, [P, KT, P])]
        hid = view(9472, FF)
        hid_hi = rounded("hid_hi", "h", 2 * CHUNK, [P, KT, P])
        hid_lo = rounded("hid_lo", "scratch", 10496, [P, KT, P])
        ye_hi = rounded("ye_hi", "scratch", 11520, [P, D])
        ye_lo = rounded("ye_lo", "pt", 0, [P, D])
        ye_pr = view(12544, D)
        hot = view(13568, LT, 2, CAP_L)
        hotw = view(14080, LT, 2, CAP_L)
        hot_t = rounded("hot_t", "scratch", 14592, [P, NLAT])
        aff_slot = stat[:, 63:64]
        hot_p = view(15104, NE, CAP_P)
        hotw_p = view(15360, NE, CAP_P)
        hotw_pt = view(15616, 2, P)
        ROWS_OF = (CAP, P)
        LAT_OF = (slice(0, CAP_L), slice(P - CAP_L, P))
        PR_OF = (slice(CAP_L, CAP), slice(0, CAP_P))
        lgt_e, work_e, mask_e = view(9472, T), view(10112, T), view(10752, T)
        cum_e = view(11392, T)
        ones_e, top8 = view(12032, T), view(12672, 8)

        mm = [ctx.enter_context(nc.psum_tensor(f"mm{i}", [P, 1024], FP32)) for i in range(2)]
        tp = ctx.enter_context(nc.psum_tensor("tp", [P, 1024], FP32))
        oo = [ctx.enter_context(nc.psum_tensor(f"oo{i}", [P, 512], FP32)) for i in range(2)]

        slot_in = [sem(f"slot{i}_in") for i in range(RING)]
        chunks_free = sem("chunks_free")
        mm_full = [sem(f"mm{i}_full") for i in range(2)]
        mm_empty = [sem(f"mm{i}_empty") for i in range(2)]
        t_full, t_empty = sem("t_full"), sem("t_empty")
        o_full = [sem(f"o{i}_full") for i in range(2)]
        o_empty = [sem(f"o{i}_empty") for i in range(2)]
        const_in, x_in = sem("const_in"), sem("x_in")
        small_in, ctx_kin, ctx_vin, sw_vin, wr_in = (sem("small_in"), sem("ctx_kin"), sem("ctx_vin"),
                                                     sem("sw_vin"), sem("wr_in"))
        small_free, layer_free = sem("small_free"), sem("layer_free")
        cols_ready, silu_e, silu_ready, mod_ready = (sem("cols_ready"), sem("silu_e"), sem("silu_ready"),
                                                     sem("mod_ready"))
        lam_e, lam_e_done = sem("lam_e"), sem("lam_e_done")
        sq_ready, sq_used, var_ready, r0_ready = sem("sq_ready"), sem("sq_used"), sem("var_ready"), sem("r0_ready")
        scaled, h_ready = sem("scaled"), sem("h_ready")
        da_roped, da_kctx_sent, nm_ready, p_mixed = (sem("da_roped"), sem("da_ctx_done"), sem("nm_ready"),
                                                     sem("p_mixed"))
        new_ready, new_sent, v_sent = sem("new_ready"), sem("new_sent"), sem("v_sent")
        ss_ready, o_ready = sem("ss_ready"), sem("o_ready")
        rs_ln, rs_done = sem("rs_ln"), sem("rs_done")
        e_ready, merged_ready = sem("e_ready"), sem("merged_ready")
        c_normed, kr_ready, mq_roped = sem("c_normed"), sem("kr_ready"), sem("mq_roped")
        sw_kready, sw_roped = sem("sw_kready"), sem("sw_roped")
        sink_in, sink_e = sem("sink_in"), sem("sink_e")
        x_ready, sum_ready = sem("x_ready"), sem("sum_ready")
        x_spilled, x_back = sem("x_spilled"), [sem(f"x_back{i}") for i in range(2)]
        h_hi_ready, h_lo_ready = sem("h_hi_ready"), sem("h_lo_ready")
        dw_hi_ready, dw_ready, dw_used = sem("dw_hi_ready"), sem("dw_ready"), sem("dw_used")
        lg_ready, lg_e, aff_ready, pos_ready = sem("lg_ready"), sem("lg_e"), sem("aff_ready"), sem("pos_ready")
        hotp_ready, hot_ready, hotw_ready = sem("hotp_ready"), sem("hot_ready"), sem("hotw_ready")
        xhi_ready, xe_ready = sem("xhi_ready"), sem("xe_ready")
        w_hi_ready, w_ready, w_used = sem("w_hi_ready"), sem("w_ready"), sem("w_used")
        silu_out, hid_ready, hid_hi_ready = sem("silu_out"), sem("hid_ready"), sem("hid_hi_ready")
        ye_stored, ye_back, ye_done = sem("ye_stored"), sem("ye_back"), sem("ye_done")
        ye_hi_ready, aff_slot_ready = sem("ye_hi_ready"), sem("aff_slot_ready")
        y_ready, y_sent = sem("y_ready"), sem("y_sent")
        pe_waited = sem("pe_waited")

        def mm_count(l, j, e):
            n = l * MM_USES[j % 2] + j // 2 + 1
            return n if e is None else n + e * (PAIR_MM // 2)

        def t_count(l, j, e):
            n = l * T_LAYER + (T_BEFORE + j + 1)
            return n if e is None else n + e * PAIR_T

        def o_count(l, j, e):
            n = l * O_USES[j % 2] + j // 2 + 1
            return n if e is None else n + e * (PAIR_O // 2)

        def wait_mm_full(eng, l, j, e=None):
            eng.wait_ge(mm_full[j % 2], mm_count(l, j, e))

        def wait_mm_empty(eng, l, j, e=None):
            eng.wait_ge(mm_empty[j % 2], mm_count(l, j, e))

        def wait_mm_read(eng, l, j, e=None):
            eng.wait_ge(mm_empty[j % 2], mm_count(l, j, e) + 1)

        def wait_t_full(eng, l, j, e=None):
            eng.wait_ge(t_full, t_count(l, j, e))

        def wait_t_empty(eng, l, j, e=None):
            eng.wait_ge(t_empty, t_count(l, j, e))

        def wait_t_read(eng, l, j, e=None):
            eng.wait_ge(t_empty, t_count(l, j, e) + 1)

        def wait_o_full(eng, l, j, e=None):
            eng.wait_ge(o_full[j % 2], o_count(l, j, e))

        def wait_o_empty(eng, l, j, e=None):
            eng.wait_ge(o_empty[j % 2], o_count(l, j, e))

        def chunk_use(l, i, e=None):
            before = LAYER_CHUNKS // RING + (1 if i % RING < LAYER_CHUNKS % RING else 0)
            n = l * before + i // RING + 1
            return n if e is None else n + e * (PAIR_CHUNKS // RING)

        def pair_part(l, e, m):
            return l * LAYER_UNITS + e * PAIR_UNITS + (ADA_UNITS + m + 1)

        def pair_used(l, e, p):
            return l * LAYER_USED + e * USED_PAIR + (ADA_UNITS - 12 + p - p // JOB_UNITS + 1)

        def ada_part(l, m):
            return l * LAYER_UNITS + (m + 1)

        def ada_used(l, p):
            return l * LAYER_USED + (p - p // ADA_JOB + 1)

        block = ctx.enter_context(nc.Block())

        @block.sync
        def _(sp):
            sp.dma_start(const[:, :], a["const"]).then_inc(const_in, 16)
            sp.dma_start(tok[:, 0:LT, :], a["x_sample"][0].rearrange("(t p) c -> p t c", p=P)).then_inc(x_in, 16)
            sp.dma_start(tok[:, PRT, :], a["x_prompt"][0]).then_inc(x_in, 16)

            def chunk_source(l, kind, k0, c0, width):
                r0 = k0 * P
                if kind == "qb":
                    return a["mla_w_qb"][l].rearrange("(k p) c -> p k c", p=P)
                if kind == "kvb":
                    return a["mla_w_kvb"][l]
                w = {"ada": "w_ada", "in": "w_in", "gate": "w_gate", "br_da": "w_br_da",
                     "br_mla": "w_br_mla", "br_swa": "w_br_swa", "o": "w_o"}[kind]
                return a[w][l, r0:r0 + HALF * P, c0:c0 + width].rearrange("(k p) c -> p k c", p=P)

            def chunk_target(kind, slot, width):
                if kind == "qb":
                    return ring[slot][:, :, :].rearrange("p k c -> p (k c)")[:, 0:2 * MH * MQ].rearrange(
                        "p (k c) -> p k c", k=2)
                if kind == "kvb":
                    return ring[slot][:, :, :].rearrange("p k c -> p (k c)")[:, 0:MH * (MNOPE + MV)]
                return ring[slot][:, :, 0:width]

            with sp.Fori(0, DEPTH) as l:
                sp.wait_ge(small_free, l + 1)
                for name, key, per in (("b_ada", "b_ada", 48), ("norm1", "norm1", KT), ("norm2", "norm2", KT),
                                       ("q_norm", "mla_q_norm", 2), ("kv_norm", "mla_kv_norm", 1),
                                       ("subln", "da_subln", 1)):
                    lo, hi = ROWS[name]
                    sp.dma_start(rows[lo:hi, :], a[key][l].rearrange("(r c) -> r c", c=P)).then_inc(small_in, 16)
                for name, src in (("final", a["final_norm"]), ("c", a["c"][0]), ("c_ctx", a["c_ctx"])):
                    lo, hi = ROWS[name]
                    sp.dma_start(rows[lo:hi, :], src.rearrange("(r c) -> r c", c=P)).then_inc(small_in, 16)
                for i, key in enumerate(("da_lq1", "da_lk1", "da_lq2", "da_lk2")):
                    sp.dma_start(bc[:, i * DH:(i + 1) * DH], a[key][l].partition_broadcast(P)).then_inc(small_in, 16)
                sp.dma_start(bc[:, 4 * DH:4 * DH + SW_H], a["swa_sink"][l].partition_broadcast(P)).then_inc(small_in, 16)
                sp.dma_start(bc[:, 4 * DH + SW_H:], a["lam"][l].partition_broadcast(P)).then_inc(small_in, 16)

                def load(i):
                    kind, k0, c0, width = CHUNKS[i]
                    sp.wait_ge(chunks_free, l * LAYER_CHUNKS + (i + 1))
                    if i == FIRST["in"] + 2:
                        sp.dma_start(a["x_spill"], x[:, :, :]).then_inc(x_spilled, 16)
                    sp.dma_start(chunk_target(kind, i % RING, width),
                                 chunk_source(l, kind, k0, c0, width)).then_inc(slot_in[i % RING], 16)

                for i in range(FIRST["in"]):
                    load(i)
                sp.wait_ge(layer_free, l + 1)
                sp.dma_start(da_ctx, a["cache_da_k"][0, l].rearrange("t h d -> t (h d)")).then_inc(ctx_kin, 16)
                sp.dma_start(ctx_in[:, 0:KVR], a["cache_mla_ckv"][0, l]).then_inc(ctx_kin, 16)
                sp.dma_start(ctx_in[:, KVR + MNOPE:KVR + MQ], a["cache_mla_krope"][0, l]).then_inc(ctx_kin, 16)
                sp.dma_start(ctx_in[:, 224:352], a["cache_swa_k"][0, l].rearrange("t h d -> t (h d)")).then_inc(ctx_kin, 16)
                sp.dma_start(da_v[:, LT, :], a["cache_da_v"][0, l].rearrange("t h d -> t (h d)")).then_inc(ctx_vin, 16)
                sp.dma_start(wr[:, :, :], a["w_router"][l].rearrange("(k p) e -> p k e", p=P)).then_inc(wr_in, 16)
                for i in range(FIRST["in"], FIRST["qb"] + 2):
                    load(i)
                for i in range(FIRST["qb"] + 2, N_DENSE):
                    if i == N_DENSE - 1:
                        wait_mm_full(sp, l, MM["sw_out"] + 14)
                        for n, tiles in enumerate((slice(0, 2), slice(2, KT))):
                            sp.dma_start(x[:, tiles, :], a["x_spill"][:, tiles, :]).then_inc(x_back[n], 16)
                    if i == FIRST["br_swa"] - 4:
                        wait_mm_full(sp, l, MM["mla_out"] + 1)
                        sp.dma_start(sw_v[:, LT, :],
                                     a["cache_swa_v"][0, l].rearrange("t h d -> t (h d)")).then_inc(sw_vin, 16)
                    load(i)

                with sp.Fori(0, PAIRS) as e:
                    i = N_DENSE
                    hidden = [("w_ff1", 0), ("w_ff3", 0), ("w_ff1", 512), ("w_ff3", 512)]
                    out = [("w_ff2", 0), ("w_ff2", 512)]
                    for half, blocks in ((0, hidden), (1, hidden), (0, out), (1, out)):
                        for w, c0 in blocks:
                            for k0 in (0, HALF):
                                sp.wait_ge(chunks_free, l * LAYER_CHUNKS + e * PAIR_CHUNKS + (i + 1))
                                sp.dma_start(ring[i % RING][:, :, :],
                                             a[w][l, 2 * e + half, k0 * P:(k0 + HALF) * P, c0:c0 + 512]
                                             .rearrange("(k p) c -> p k c", p=P)).then_inc(slot_in[i % RING], 16)
                                i += 1
            sp.wait_ge(y_ready, 2)
            sp.dma_start(a["y_sample"][0].rearrange("(t p) c -> p t c", p=P), tok[:, 0:LT, :]).then_inc(y_sent, 16)
            sp.dma_start(a["y_prompt"][0], tok[:, PRT, :]).then_inc(y_sent, 16)
            sp.wait_ge(y_sent, 32)
            sp.wait_ge(new_sent, DEPTH * NEW_STORES * 16)
            sp.wait_ge(v_sent, DEPTH * 2 * 16)

        @block.gpsimd
        def _(pool):
            pool.sem_inc(chunks_free, RING)
            pool.sem_inc(small_free, 1)
            for s in (*mm_empty, t_empty, *o_empty):
                pool.sem_inc(s, 1)
            pool.sem_inc(ye_stored, 32)

            with pool.Fori(0, DEPTH) as l:
                def consumed(turn, n, e=None):
                    wait_mm_full(pool, l, turn, e)
                    pool.sem_inc(chunks_free, n)

                for n in range(24):
                    pool.wait_ge(w_ready, ada_part(l, n * UNITS + UNITS - 1))
                    pool.sem_inc(chunks_free, 1)
                consumed(MM["da_v"] + TT - 1, 2)
                consumed(MM["da_q"] + 3, 2)
                consumed(DA_K[3], 2)
                consumed(MM["da_out"] + 7, 3)
                consumed(MM["da_out"] + 15, 3)
                consumed(MM["mla_in"] + 3, 2)
                consumed(SW_Q[3], 2)
                consumed(mla_prep(MH - 1, 2), 2)
                consumed(MM["mla_out"] + 7, 3)
                consumed(MM["mla_out"] + 15, 3)
                consumed(SW_V, 2)
                consumed(MM["sw_out"] + 7, 3)
                consumed(MM["sw_out"] + 15, 3)
                consumed(MM["o"] + 3, 2)
                consumed(MM["o"] + 7, 2)
                with pool.Fori(0, PAIRS) as e:
                    for n in range(PAIR_CHUNKS):
                        pool.wait_ge(w_ready, pair_part(l, e, n * UNITS + UNITS - 1))
                        pool.sem_inc(chunks_free, 1)

        @block.tensor
        def _(pe):
            pe.wait_ge(const_in, 16)
            pe.wait_ge(x_in, 32)
            for t in range(TT):
                pe.wait_ge(t_empty, t + 1)
                for k in range(KT):
                    last = pe.transpose(tp[:, k * P:(k + 1) * P], tok[:, t, k * P:(k + 1) * P], ident)
                last.then_inc(t_full, 1)

            def product(out, lhs, rhs, terms, before=None):
                for n in range(terms):
                    if before is not None:
                        before(n)
                    for lo, hi in ((0, 512), (512, T)):
                        last = pe.matmul(out[:, lo:hi], lhs(n), rhs(n)[:, lo:hi],
                                         start=(n == 0), stop=(n == terms - 1))
                return last

            def norm_of_x(l, turn, n):
                pe.wait_ge(sum_ready, n)
                wait_mm_empty(pe, l, turn)
                for lo, hi in ((0, 512), (512, T)):
                    last = pe.matmul(mm[turn % 2][:, lo:hi], ones, tmp[2][:, lo:hi], start=True, stop=True)
                last.then_inc(mm_full[turn % 2], 1)

            def norm_sum(l, turn, sq0, used0, tiles):
                wait_mm_empty(pe, l, turn)
                for k in range(tiles):
                    pe.wait_ge(sq_ready, l * PER_LAYER["sq_ready"] + (sq0 + k + 1))
                    for lo, hi in ((0, 512), (512, T)):
                        last = pe.matmul(mm[turn % 2][:, lo:hi], ones, tmp[k % 2][:, lo:hi],
                                         start=(k == 0), stop=(k == tiles - 1))
                    last.then_inc(sq_used if k < tiles - 1 else mm_full[turn % 2], 1)

            def wait_chunks(l, i, n, e=None):
                for c in range(i, i + n):
                    pe.wait_ge(slot_in[c % RING], 16 * chunk_use(l, c, e))

            def weight(i, k, c0, c1):
                return ring[(i + k // HALF) % RING][:, k % HALF, c0:c1]

            def product_h(l, q, before=None):
                j, chunk, c0, width = H_TILES[q]
                out = mm[j % 2]
                wait_mm_empty(pe, l, j)
                for half in range(2):
                    u = 2 * q + half
                    pe.wait_ge(dw_ready, l * 2 * H_N + (u + 1))
                    for kk in range(HALF):
                        k = half * HALF + kk
                        if before is not None:
                            before(k)
                        for i, (w_, h_) in enumerate(((dw_lo, h_hi), (dw_hi, h_lo), (dw_hi, h_hi))):
                            pe.matmul(out[0:width, 0:NLAT], w_[u % 2][:, kk, 0:width], h_[:, k, 0:NLAT],
                                      start=(k == 0 and i == 0), stop=(k == KT - 1 and i == 2))
                        last = pe.matmul(out[0:width, NLAT:T], weight(chunk, k, c0, c0 + width), h[:, k, NLAT:T],
                                         start=(k == 0), stop=(k == KT - 1))
                    last.then_inc(mm_full[j % 2] if half else dw_used, 1)

            def branch_out(l, chunk, turn, o_t, turned, q0):
                for m in range(KT):
                    c = chunk + 3 * (m // 4)
                    if m % 4 == 0:
                        wait_chunks(l, c, 3)
                    m0 = (m % 4) * P
                    j = turn + 2 * m
                    product_h(l, q0 + m)
                    if m == 0:
                        turned()
                    wait_mm_empty(pe, l, j + 1)
                    product(mm[(j + 1) % 2], lambda k: weight(c + 2, k, m0, m0 + P), lambda k: o_t[:, k, :], 4)\
                        .then_inc(mm_full[(j + 1) % 2], 1)

            def values(l, chunk, turn, c0, width, before):
                for t in range(TT):
                    j = turn + t
                    wait_mm_empty(pe, l, j)
                    for k in range(KT):
                        if t == 0:
                            before(k)
                        last = pe.matmul(mm[j % 2][:, 0:width], h[:, k, t * P:(t + 1) * P],
                                         weight(chunk, k, c0, c0 + width), start=(k == 0), stop=(k == KT - 1))
                    last.then_inc(mm_full[j % 2], 1)

            def attention(l, n, score, tiles, p_ready, probs, v_of, width, tr, t_p, o_base, after):
                for s in range(n + 2):
                    if s < n:
                        score(s)
                    if 1 <= s <= n:
                        i = s - 1
                        p_ready(i)
                        j = tr + t_p[i]
                        wait_t_empty(pe, l, j)
                        for b in range(tiles(i)):
                            last = pe.transpose(tp[:, b * P:(b + 1) * P], probs(i)[:, b * P:(b + 1) * P], ident)
                        last.then_inc(t_full, 1)
                    if s >= 2:
                        i = s - 2
                        o = o_base + i
                        wait_t_read(pe, l, tr + t_p[i])
                        wait_o_empty(pe, l, o)
                        for b in range(tiles(i)):
                            last = pe.matmul(oo[o % 2][:, 0:width], pt[:, i % 2, b * P:(b + 1) * P], v_of(i, b),
                                             start=(b == 0), stop=(b == tiles(i) - 1))
                        last.then_inc(o_full[o % 2], 1)
                    after(s)

            def turn_outputs(l, j, o_tok, ready, n):
                pe.wait_ge(ready, n)
                wait_t_empty(pe, l, j)
                for k in range(4):
                    last = pe.transpose(tp[:, k * P:(k + 1) * P], o_tok[:, k * P:(k + 1) * P], ident)
                last.then_inc(t_full, 1)

            def latent_keys(t):
                return [(0, 512, 0), (512, T, 512)] if t < LT else [(T, KEYS, 0)]

            def window(t):
                lo, hi = max(t - 1, 0), min(t + 1, LT - 1)
                return lo, hi

            def window_tiles(t):
                if t == PRT:
                    return 1
                lo, hi = window(t)
                return hi - lo + 2

            with pe.Fori(0, DEPTH) as l:
                pe.wait_ge(small_in, l * SMALL_LOADS * 16 + SMALL_LOADS * 16)
                wait_t_empty(pe, l, TR["cols"])
                pe.transpose(tp[:, 0:NROWS], rows[:, :], ident[0:NROWS, 0:NROWS]).then_inc(t_full, 1)
                pe.wait_ge(silu_ready, l + 1)
                for b in range(12):
                    j = ada_turn(b)
                    wait_mm_empty(pe, l, j)
                    for c in range(ADA_JOB):
                        m = ADA_JOB * b + c
                        pe.wait_ge(w_ready, ada_part(l, m))
                        for kk in range(UK):
                            k = c * UK + kk
                            for i, (a_, b_) in enumerate(((c_hi, w_lo), (c_lo, w_hi), (c_hi, w_hi))):
                                last = pe.matmul(mm[j % 2][0:2, 0:512], a_[:, k, :], b_[m % SPLITS][:, kk, :],
                                                 start=(k == 0 and i == 0), stop=(k == KT - 1 and i == 2))
                        last.then_inc(mm_full[j % 2] if c == ADA_JOB - 1 else w_used, 1)
                    if b == NORM1_AT - 1:
                        norm_of_x(l, MM["norm1"], l * 2 + 1)
                wait_mm_read(pe, l, ada_turn(10))
                wait_mm_read(pe, l, ada_turn(11))
                wait_t_empty(pe, l, TR["ada"])
                pe.sem_inc(pe_waited, 1)
                for m in range(48):
                    last = pe.transpose(tp[:, 2 * m:2 * m + 2], ada_row[0:2, m * P:(m + 1) * P], ident[0:2, 0:2])
                last.then_inc(t_full, 1)

                pe.wait_ge(ctx_kin, l * 64 + 64)
                wait_t_empty(pe, l, TR["da_ctx"])
                for m in range(4):
                    last = pe.transpose(tp[:, m * P:(m + 1) * P], da_ctx[:, m * P:(m + 1) * P], ident)
                last.then_inc(t_full, 1)
                c = FIRST["in"]
                wait_chunks(l, c, 2)
                values(l, c, MM["da_v"], 0, 512, lambda k: pe.wait_ge(h_ready, l * 2 * KT + (k + 1)))
                def da_rotate(m):
                    src = da_q[:, m, 0:NLAT] if m < 4 else da_k[:, m - 4, 0:NLAT]
                    j = DA_ROT[m]
                    wait_mm_read(pe, l, MM["da_q"] + m if m < 4 else DA_K[m - 4])
                    wait_mm_empty(pe, l, j)
                    pe.matmul(mm[j % 2][:, 0:NLAT], c_("swap"), src, start=True, stop=True).then_inc(mm_full[j % 2], 1)

                for q in range(4):
                    product_h(l, q, (lambda k: pe.wait_ge(h_lo_ready, l * KT + (k + 1))) if q == 0 else None)
                for m in range(4):
                    da_rotate(m)
                    product_h(l, H_AT["da_k"] + m)
                for m in range(4, 8):
                    da_rotate(m)
                wait_t_empty(pe, l, TR["da_new"])
                for m in range(4):
                    last = pe.transpose(tp[:, m * P:(m + 1) * P], da_k[:, m, T:KEYS], ident)
                last.then_inc(t_full, 1)
                pe.wait_ge(da_roped, l + 1)
                wait_t_read(pe, l, TR["da_ctx"])
                pe.wait_ge(ctx_vin, l * 16 + 16)
                wait_mm_read(pe, l, MM["da_v"] + TT - 1)
                wait_mm_read(pe, l, MM["da_v"] + TT - 2)

                def da_score(i, m):
                    t, hd = divmod(i, DA_H)
                    j = MM["da_s"] + 2 * i + m
                    r = slice(m * DH, (m + 1) * DH)
                    wait_mm_empty(pe, l, j)
                    for lo, hi, at in latent_keys(t):
                        last = pe.matmul(mm[j % 2][:, at:at + hi - lo], da_q[r, hd, t * P:(t + 1) * P],
                                         da_k[r, hd, lo:hi], start=True, stop=True)
                    last.then_inc(mm_full[j % 2], 1)

                for s in range(DA_N + 2):
                    i = s - 2
                    if s < DA_N:
                        da_score(s, 0)
                    if i >= 0:
                        n_tiles = 5 if i // DA_H < LT else 1
                        pe.wait_ge(p_mixed, l * DA_N + (i + 1))
                        wait_t_empty(pe, l, TR["da"] + DA_TP[i])
                        for b in range(n_tiles):
                            last = pe.transpose(tp[:, b * P:(b + 1) * P], da_p[i % 2][0][:, b * P:(b + 1) * P], ident)
                        last.then_inc(t_full, 1)
                    if s < DA_N:
                        da_score(s, 1)
                    if i >= 0:
                        t, hd = divmod(i, DA_H)
                        o = OO["da"] + i
                        wait_t_read(pe, l, TR["da"] + DA_TP[i])
                        wait_o_empty(pe, l, o)
                        for b in range(n_tiles):
                            last = pe.matmul(oo[o % 2][:, 0:P], pt[:, i % 2, b * P:(b + 1) * P],
                                             da_v[:, b if t < LT else PRT + 1, hd * P:(hd + 1) * P],
                                             start=(b == 0), stop=(b == n_tiles - 1))
                        last.then_inc(o_full[o % 2], 1)

                def da_turned():
                    for t in range(TT):
                        turn_outputs(l, TR["da"] + DA_TO[t], da_o[:, t, :], o_ready, l * 3 * TT + (t + 1))
                    wait_t_read(pe, l, TR["da"] + DA_TO[PRT])

                branch_out(l, FIRST["br_da"] - 2, MM["da_out"], da_q, da_turned, H_AT["da_gate"])

                wait_t_empty(pe, l, TR["mla_ctx"])
                pe.transpose(tp[:, 0:P], ctx_in[:, 0:KVR], ident)
                pe.transpose(tp[0:MQ, P:2 * P], ctx_in[:, KVR:KVR + MQ], ident).then_inc(t_full, 1)
                c = FIRST["qb"] - 4
                wait_chunks(l, c, 2)
                for m in range(4):
                    product_h(l, H_AT["mla_in"] + m)
                wait_chunks(l, c + 2, 2)
                for m in range(4):
                    product_h(l, H_AT["sw_q"] + m)
                    if m == 0:
                        norm_sum(l, MLA_NORM[0], KT, KT - 1, 2)
                    if m == 1:
                        norm_sum(l, MLA_NORM[1], KT + 2, KT, 1)
                j = MM["kr_rot"]
                wait_mm_read(pe, l, MM["mla_in"] + 3)
                wait_mm_empty(pe, l, j)
                pe.sem_inc(pe_waited, 1)
                pe.matmul(mm[j % 2][MNOPE:MQ, 0:NLAT], c_("swap32", slice(MNOPE, MQ)), ml_k[0][MNOPE:MQ, 0:NLAT],
                          start=True, stop=True).then_inc(mm_full[j % 2], 1)
                pe.wait_ge(c_normed, l * 2 + 2)
                wait_t_read(pe, l, TR["mla_ctx"])
                wait_chunks(l, FIRST["qb"], 2)
                wqb = ring[FIRST["qb"] % RING][:, :, :].rearrange("p k c -> p (k c)")[:, 0:2 * MH * MQ].rearrange(
                    "p (k c) -> p k c", k=2)
                wkvb = ring[FIRST["kvb"] % RING][:, :, :].rearrange("p k c -> p (k c)")[:, 0:MH * (MNOPE + MV)].rearrange(
                    "p (h c) -> p h c", h=MH)
                for t in range(KEY_TILES):
                    j = MM["mla_v"] + t
                    wait_mm_empty(pe, l, j)
                    pe.matmul(mm[j % 2][:, 0:512], ckv[:, t * P:(t + 1) * P], wkvb[:, :, MNOPE:],
                              start=True, stop=True).then_inc(mm_full[j % 2], 1)

                def project_head(hd, piece):
                    j = mla_prep(hd, piece)
                    if piece == 2:
                        wait_mm_read(pe, l, mla_prep(hd, 0))
                    wait_mm_empty(pe, l, j)
                    if piece == 0:
                        product(mm[j % 2][0:MQ, :], lambda k: wqb[:, k, hd * MQ:(hd + 1) * MQ],
                                lambda k: cq[:, k, :], 2).then_inc(mm_full[j % 2], 1)
                    elif piece == 1:
                        for lo, hi in ((0, 512), (512, KEYS)):
                            last = pe.matmul(mm[j % 2][0:MNOPE, lo:hi], wkvb[:, hd, 0:MNOPE], ckv[:, lo:hi],
                                             start=True, stop=True)
                        last.then_inc(mm_full[j % 2], 1)
                    else:
                        pe.sem_inc(pe_waited, 1)
                        pe.matmul(mm[j % 2][MNOPE:MQ, 0:NLAT], c_("swap32", slice(MNOPE, MQ)),
                                  ml_q[hd % 2][MNOPE:MQ, 0:NLAT], start=True, stop=True).then_inc(mm_full[j % 2], 1)

                pe.wait_ge(kr_ready, l + 1)
                wait_t_empty(pe, l, TR["mla_new"])
                pe.transpose(tp[:, 0:P], ckv[:, T:KEYS], ident)
                pe.transpose(tp[:, P:P + MROPE], ml_k[0][MNOPE:MQ, T:KEYS],
                             ident[MNOPE:MQ, MNOPE:MQ]).then_inc(t_full, 1)
                for piece in range(3):
                    project_head(0, piece)
                wait_mm_read(pe, l, MM["mla_v"] + KEY_TILES - 1)
                wait_mm_read(pe, l, MM["mla_v"] + KEY_TILES - 2)

                def mla_score(i):
                    hd, t = divmod(i, TT)
                    if 1 <= t <= 3 and hd < MH - 1:
                        project_head(hd + 1, t - 1)
                    if t == 0:
                        wait_mm_read(pe, l, mla_prep(hd, 1))
                        pe.wait_ge(mq_roped, l * MH + (hd + 1))
                    j = mla_s(i)
                    wait_mm_empty(pe, l, j)
                    for lo, hi, at in latent_keys(t):
                        last = pe.matmul(mm[j % 2][:, at:at + hi - lo], ml_q[hd % 2][0:MQ, t * P:(t + 1) * P],
                                         ml_k[hd % 2][0:MQ, lo:hi], start=True, stop=True)
                    last.then_inc(mm_full[j % 2], 1)

                attention(l, MLA_N, mla_score, lambda i: 5 if i % TT < LT else 1,
                          lambda i: wait_mm_read(pe, l, mla_s(i)), lambda i: ml_p[i % 2],
                          lambda i, b: ml_v[:, b if i % TT < LT else PRT + 1, (i // TT) * MV:(i // TT + 1) * MV],
                          MV, TR["mla"], MLA_TP, OO["mla"], lambda s: None)

                def mla_turned():
                    for t in range(TT):
                        turn_outputs(l, TR["mla"] + MLA_TO[t], ml_otok[:, t, :], o_ready, l * 3 * TT + 2 * TT)
                    wait_t_read(pe, l, TR["mla"] + MLA_TO[TT - 1])

                branch_out(l, FIRST["br_mla"] - 2, MM["mla_out"], ml_o, mla_turned, H_AT["mla_gate"])

                wait_t_empty(pe, l, TR["sw_ctx"])
                pe.transpose(tp[:, 0:P], ctx_in[:, 224:352], ident).then_inc(t_full, 1)
                def sw_rotate(m):
                    src = sw_q[:, m, 0:NLAT] if m < 4 else sw_kraw[:, 0:NLAT]
                    j = SW_ROT[m]
                    wait_mm_read(pe, l, SW_Q[m] if m < 4 else SW_K)
                    wait_mm_empty(pe, l, j)
                    pe.matmul(mm[j % 2][:, 0:NLAT], c_("swap"), src, start=True, stop=True).then_inc(mm_full[j % 2], 1)

                for q in range(2):
                    sw_rotate(2 * q)
                    sw_rotate(2 * q + 1)
                    product_h(l, H_AT["sw_kv"] + q)
                sw_rotate(4)
                wait_mm_read(pe, l, SW_V)
                wait_t_empty(pe, l, TR["sw_vt"])
                for t in range(TT):
                    last = pe.transpose(tp[:, t * P:(t + 1) * P], sw_vraw[:, t * P:(t + 1) * P], ident)
                last.then_inc(t_full, 1)
                wait_t_empty(pe, l, TR["sw_new"])
                pe.transpose(tp[:, 0:P], sw_kraw[:, T:KEYS], ident).then_inc(t_full, 1)
                pe.wait_ge(sw_roped, l + 1)
                pe.wait_ge(sw_vin, l * 16 + 16)
                wait_t_read(pe, l, TR["sw_vt"])

                def sw_score(i):
                    t, hd = divmod(i, SW_H)
                    r = slice((hd % 2) * DH, (hd % 2 + 1) * DH)
                    g = hd // (SW_H // SW_KV)
                    j = MM["sw_s"] + i
                    out = mm[j % 2]
                    q = sw_q[r, hd // 2, t * P:(t + 1) * P]
                    wait_mm_empty(pe, l, j)
                    if t == PRT:
                        last = pe.matmul(out[:, 0:P], q, sw_k[r, g, T:KEYS], start=True, stop=True)
                    else:
                        lo, hi = window(t)
                        n = (hi - lo + 1) * P
                        pe.matmul(out[:, 0:n], q, sw_k[r, g, lo * P:(hi + 1) * P], start=True, stop=False)
                        masks = [(0, "mask_before")] * (t > 0) + [(n - P, "mask_after")] * (t < LT - 1)
                        for at, name in masks:
                            pe.matmul(out[:, at:at + P], ident, c_(name), start=False,
                                      stop=(name == masks[-1][1]))
                        last = pe.matmul(out[:, n:n + P], q, sw_k[r, g, NLAT:T], start=True, stop=True)
                    last.then_inc(mm_full[j % 2], 1)

                def sw_values(i, b):
                    t, hd = divmod(i, SW_H)
                    g = hd // (SW_H // SW_KV)
                    if t == PRT:
                        tile = PRT + 1
                    else:
                        lo, hi = window(t)
                        tile = lo + b if b <= hi - lo else LT
                    return sw_v[:, tile, g * DH:(g + 1) * DH]

                def sw_after(s):
                    for t in range(TT):
                        if s == SW_H * (t + 1) + 3:
                            turn_outputs(l, TR["sw"] + SW_TO[t], sw_o[:, t % 2, :], o_ready,
                                         l * 3 * TT + (2 * TT + t + 1))

                attention(l, SW_N, sw_score, lambda i: window_tiles(i // SW_H),
                          lambda i: wait_mm_read(pe, l, MM["sw_s"] + i), lambda i: sw_p[i % 2],
                          sw_values, DH, TR["sw"], SW_TP, OO["sw"], sw_after)

                def sw_turned():
                    turn_outputs(l, TR["sw"] + SW_TO[PRT], sw_o[:, PRT % 2, :], o_ready, l * 3 * TT + 3 * TT)
                    wait_t_read(pe, l, TR["sw"] + SW_TO[PRT])

                branch_out(l, FIRST["br_swa"] - 2, MM["sw_out"], sw_q, sw_turned, H_AT["sw_gate"])

                def merged_tile(k):
                    if k == 0:
                        wait_mm_read(pe, l, MM["sw_out"] + 2 * (KT - 2) + 1)
                    if k == KT - 1:
                        pe.wait_ge(merged_ready, l * 3 + 3)

                for m in range(KT):
                    c = FIRST["o"] + 2 * (m // 4)
                    if m % 4 == 0:
                        wait_chunks(l, c, 2)
                    j = MM["o"] + m
                    wait_mm_empty(pe, l, j)
                    product(mm[j % 2], lambda k: weight(c, k, (m % 4) * P, (m % 4 + 1) * P),
                            lambda k: merged[:, k, :], KT, merged_tile if m == 0 else None)\
                        .then_inc(mm_full[j % 2], 1)

                norm_of_x(l, MM["norm2"], l * 2 + 2)
                pe.wait_ge(wr_in, l * 16 + 16)
                j = MM["router"]
                wait_mm_empty(pe, l, j)
                for k in range(KT):
                    pe.wait_ge(h_ready, l * 2 * KT + (KT + k + 1))
                    pe.sem_inc(pe_waited, 1)
                    for lo, hi in ((0, 512), (512, T)):
                        last = pe.matmul(mm[j % 2][0:NE, lo:hi], wr[:, k, :], h[:, k, lo:hi],
                                         start=(k == 0), stop=(k == KT - 1))
                last.then_inc(mm_full[j % 2], 1)
                wait_mm_read(pe, l, j)
                wait_t_empty(pe, l, TR["lg"])
                pe.sem_inc(pe_waited, 1)
                for t in range(TT):
                    last = pe.transpose(tp[:, t * NE:(t + 1) * NE], lgt_e[0:NE, t * P:(t + 1) * P], ident[0:NE, 0:NE])
                last.then_inc(t_full, 1)
                pe.wait_ge(aff_ready, l + 1)
                wait_t_empty(pe, l, TR["aff"])
                for t in range(TT):
                    last = pe.transpose(tp[0:NE, t * P:(t + 1) * P], aff[:, t, :], ident)
                last.then_inc(t_full, 1)
                for t in range(TT):
                    wait_t_empty(pe, l, TR["h_tok"] + t)
                    for k in range(KT):
                        last = pe.transpose(tp[:, k * P:(k + 1) * P], h[:, k, t * P:(t + 1) * P], ident)
                    last.then_inc(t_full, 1)
                pe.wait_ge(pos_ready, l + 1)
                wait_t_empty(pe, l, TR["pos"])
                pe.sem_inc(pe_waited, 1)
                for t in range(TT):
                    last = pe.transpose(tp[:, t * NE:(t + 1) * NE], cum_e[0:NE, t * P:(t + 1) * P], ident[0:NE, 0:NE])
                last.then_inc(t_full, 1)
                pe.wait_ge(hotp_ready, l + 1)
                wait_t_read(pe, l, TR["h_tok"] + TT - 1)
                for g in range(2):
                    j = MM["gather_p"] + g
                    wait_mm_empty(pe, l, j)
                    for k in range(4):
                        last = pe.matmul(mm[j % 2][:, k * SLOTS_P:(k + 1) * SLOTS_P],
                                         tok[:, PRT, (4 * g + k) * P:(4 * g + k + 1) * P],
                                         hot_p.rearrange("p e s -> p (e s)"), start=True, stop=True)
                    last.then_inc(mm_full[j % 2], 1)
                wait_t_empty(pe, l, TR["hot_p"])
                for g in range(2):
                    last = pe.transpose(tp[:, g * P:(g + 1) * P],
                                        hotw_p.rearrange("p e s -> p (e s)")[:, g * P:(g + 1) * P], ident)
                last.then_inc(t_full, 1)

                def gather(turn, g, e, of):
                    if g == 0:
                        pe.wait_ge(hot_ready, l * PAIRS + of + 1)
                    wait_mm_empty(pe, l, turn, e)
                    for k in range(4):
                        for t in range(LT):
                            last = pe.matmul(mm[turn % 2][:, k * P:(k + 1) * P],
                                             tok[:, t, (4 * g + k) * P:(4 * g + k + 1) * P],
                                             hot[:, t, :, :].rearrange("p a s -> p (a s)"),
                                             start=(t == 0), stop=(t == LT - 1))
                    last.then_inc(mm_full[turn % 2], 1)

                def combine(k, of):
                    if k == 0:
                        pe.wait_ge(ye_done, l * PAIRS + of + 1)
                    j = OO["pairs"] + k
                    wait_o_empty(pe, l, j, of)
                    for i, y in enumerate((ye_lo, ye_hi)):
                        last = pe.matmul(oo[j % 2][:, :], y[:, k * P:(k + 1) * P], hot_t[:, :],
                                         start=(i == 0), stop=(i == 1))
                    last.then_inc(o_full[j % 2], 1)

                def job(q, e, last_pair, before=None):
                    half = q % 2 if q >= AO else q // 2
                    rows_ = ROWS_OF[half]
                    hi, lo = (hid_hi, hid_lo) if q >= AO else (x_hi[half], x_lo[half])
                    j = job_turn(q, last_pair)
                    out = mm[j % 2]
                    wait_mm_empty(pe, l, j, e)
                    for c in range(JOB_UNITS):
                        n = JOB_UNITS * q + c
                        if before is not None and COMBINE_AT <= n < COMBINE_AT + KT:
                            combine(n - COMBINE_AT, before)
                        pe.wait_ge(w_ready, pair_part(l, e, n))
                        bank = (c // (2 * UNITS)) * 512
                        for kk in range(UK):
                            k = (c % (2 * UNITS)) * UK + kk
                            for i, (a_, b_) in enumerate(((hi, w_lo), (lo, w_hi), (hi, w_hi))):
                                last = pe.matmul(out[0:rows_, bank:bank + 512], a_[:, k, 0:rows_],
                                                 b_[n % SPLITS][:, kk, :], start=(k == 0 and i == 0),
                                                 stop=(k == KT - 1 and i == 2))
                        last.then_inc(mm_full[j % 2] if c == JOB_UNITS - 1 else w_used, 1)

                def turn_hidden(q, turn, e):
                    half, n = q // 2, q % 2
                    rows_ = ROWS_OF[half]
                    pe.wait_ge(hid_ready, (l * PAIRS + e) * 4 + (q + 1))
                    wait_t_empty(pe, l, turn, e)
                    for k in range(4):
                        last = pe.transpose(tp[:, k * P:k * P + rows_],
                                            hid[0:rows_, (4 * n + k) * P:(4 * n + k + 1) * P],
                                            ident[0:rows_, 0:rows_])
                    if q == AF0:
                        pe.wait_ge(hotw_ready, l * PAIRS + e + 1)
                        for t in range(LT):
                            last = pe.transpose(tp[:, (LT + t) * P:(LT + t + 1) * P],
                                                hotw[:, t, :, :].rearrange("p a s -> p (a s)"), ident)
                    last.then_inc(t_full, 1)

                def pair(e, before=None, last_pair=False):
                    m0, t0 = MM["pairs"] + 2, TR["pairs"]
                    pe.wait_ge(xe_ready, l * PAIRS + e + 1)
                    job(AF0, e, last_pair, before)
                    job(AF1, e, last_pair, before)
                    turn_hidden(AF0, t0, e)
                    job(BF0, e, last_pair)
                    turn_hidden(AF1, t0 + 1, e)
                    job(BF1, e, last_pair)
                    wait_t_read(pe, l, t0 + 1, e)
                    job(AO, e, last_pair)
                    turn_hidden(BF0, t0 + 2, e)
                    if not last_pair:
                        gather(m0 + G0, 0, e, e + 1)
                    turn_hidden(BF1, t0 + 3, e)
                    if not last_pair:
                        gather(m0 + G1, 1, e, e + 1)
                    wait_t_read(pe, l, t0 + 3, e)
                    job(BO, e, last_pair)

                gather(MM["pairs"], 0, None, 0)
                gather(MM["pairs"] + 1, 1, None, 0)
                pair(0)
                with pe.Fori(1, PAIRS - 1) as e:
                    pair(e, e - 1)
                pair(PAIRS - 1, PAIRS - 2, True)
                for k in range(KT):
                    combine(k, PAIRS - 1)

                pe.wait_ge(ye_back, l * 16 + 16)
                j = MM["combine_p"]
                wait_mm_empty(pe, l, j)
                for k in range(KT):
                    for g in range(2):
                        last = pe.matmul(mm[j % 2][:, k * P:(k + 1) * P], ye_ptok[:, g, k * P:(k + 1) * P],
                                         hotw_pt[:, g, :], start=(g == 0), stop=(g == 1))
                last.then_inc(mm_full[j % 2], 1)

            norm_of_x(DEPTH, 0, DEPTH * 2 + 1)
            pe.wait_ge(h_ready, DEPTH * 2 * KT + 1)
            for t in range(TT):
                wait_t_empty(pe, DEPTH, t)
                for k in range(KT):
                    last = pe.transpose(tp[:, k * P:(k + 1) * P], h[:, k, t * P:(t + 1) * P], ident)
                last.then_inc(t_full, 1)

        @block.scalar
        def _(act):
            def copy(out, in_, scale=1.0):
                return act.activation(out, in_, ACT.Copy, scale=scale)

            def squares(l, tiles, sq0, used0, src):
                for k in range(tiles):
                    if k >= 2:
                        act.wait_ge(sq_used, l * PER_LAYER["sq_used"] + (used0 + k - 1))
                    act.activation(tmp[k % 2][:, :], src(k), ACT.Square).then_inc(sq_ready, 1)

            def squares_of_x(l, sq0, used0, tile_ready):
                for k in range(KT):
                    if k >= 3:
                        act.wait_ge(sq_used, l * PER_LAYER["sq_used"] + (used0 + k - 2))
                    tile_ready(k)
                    act.activation(tmp[k % 2 if k else 2][:, :], x[:, k, :], ACT.Square).then_inc(sq_ready, 1)

            def first_rstd(l, n):
                act.wait_ge(var_ready, l * PER_LAYER["var_ready"] + (n + 1))
                act.activation(rstd[:, :], tmp[2][:, :], ACT.Ln)
                act.drain()
                act.activation(rstd[:, :], rstd[:, :], ACT.Exp, scale=-0.5).then_inc(r0_ready, 1)

            def shifts(l, n, shift):
                for k in range(KT):
                    act.wait_ge(scaled, l * PER_LAYER["scaled"] + (n * KT + k + 1))
                    act.activation(h[:, k, 0:NLAT], h[:, k, 0:NLAT], ACT.Identity, bias=mod[:, shift + k, 0:1])
                    act.activation(h[:, k, NLAT:T], h[:, k, NLAT:T], ACT.Identity, bias=mod[:, shift + k, 1:2])\
                        .then_inc(h_ready, 1)

            def hi_of_tile(l, q):
                _, chunk, c0, width = H_TILES[q]
                for half in range(2):
                    u = 2 * q + half
                    if q > 0:
                        if half:
                            wait_mm_full(act, l, H_TILES[q - 1][0])
                        else:
                            act.wait_ge(dw_used, l * H_N + q)
                    i = chunk + half
                    act.wait_ge(slot_in[i % RING], 16 * chunk_use(l, i))
                    copy(dw_hi[u % 2][:, :, 0:width], ring[i % RING][:, :, c0:c0 + width]).then_inc(dw_hi_ready, 1)

            def gates(l, turn, turned, q0):
                for m in range(KT):
                    j = turn + 2 * m
                    if q0 + m + 1 < H_N:
                        hi_of_tile(l, q0 + m + 1)
                    wait_mm_full(act, l, j)
                    if m >= 2:
                        wait_mm_read(act, l, j - 3)
                    act.activation(tmp[m % 2][:, :], mm[j % 2][:, 0:T], ACT.Exp, scale=-1.0).then_inc(mm_empty[j % 2], 1)
                    if m == 0:
                        turned()

            def exps(l, i0, i, j, out, width, sum_at):
                act.wait_ge(nm_ready, l * NM_LAYER + (i0 + i + 1))
                wait_mm_full(act, l, j)
                act.activation(out, mm[j % 2][:, 0:width], ACT.Exp, bias=stat[:, sum_at:sum_at + 1],
                               accum_out=stat[:, sum_at + 16:sum_at + 17])

            with act.Fori(0, DEPTH) as l:
                act.wait_ge(cols_ready, l + 1)
                lo, hi = ROWS["c"][0], ROWS["c_ctx"][1]
                act.activation(silu_t[:, :], cols[:, lo:hi], ACT.Exp, scale=-1.0).then_inc(silu_e, 1)
                act.wait_ge(lam_e, l + 1)
                act.activation(lam[:, 2:4], lam[:, 0:2], ACT.Exp).then_inc(lam_e_done, 1)
                def hi_of_ada(b):
                    for m in range(ADA_JOB * b, ADA_JOB * (b + 1)):
                        p = m - SPLITS
                        if p >= 0:
                            if p % ADA_JOB == ADA_JOB - 1:
                                wait_mm_full(act, l, ada_turn(p // ADA_JOB))
                            else:
                                act.wait_ge(w_used, ada_used(l, p))
                        i, u = divmod(m, UNITS)
                        if u == 0:
                            act.wait_ge(slot_in[i % RING], 16 * chunk_use(l, i))
                        copy(w_hi[m % SPLITS][:, :, :], ring[i % RING][:, u * UK:(u + 1) * UK, :])\
                            .then_inc(w_hi_ready, 1)

                hi_of_ada(0)
                for b in range(12):
                    if b < 11:
                        hi_of_ada(b + 1)
                    if b == NORM1_AT - 4:
                        act.wait_ge(x_ready, l * 2 + 1)
                        squares_of_x(l, 0, 0, lambda k: None)
                    if b == NORM1_AT:
                        first_rstd(l, 0)
                    j = ada_turn(b)
                    wait_mm_full(act, l, j)
                    copy(ada_row[0:2, b * 512:(b + 1) * 512], mm[j % 2][0:2, 0:512]).then_inc(mm_empty[j % 2], 1)
                shifts(l, 0, 0)

                wait_t_full(act, l, TR["da_ctx"])
                copy(da_k[:, :, NLAT:T], tp[:, 0:512].rearrange("p (m t) -> p m t", m=4)).then_inc(t_empty, 1)
                hi_of_tile(l, 0)
                act.drain()
                act.wait_ge(x_spilled, l * 16 + 16)
                for k in range(KT):
                    copy(h_hi[:, k, :], h[:, k, 0:NLAT]).then_inc(h_hi_ready, 1)
                for t in range(TT):
                    j = MM["da_v"] + t
                    wait_mm_full(act, l, j)
                    copy(da_v[:, t if t < LT else PRT + 1, :], mm[j % 2][:, 0:512]).then_inc(mm_empty[j % 2], 1)
                for m in range(4):
                    j = MM["da_q"] + m
                    hi_of_tile(l, m + 1)
                    wait_mm_full(act, l, j)
                    copy(da_q[:, m, :], mm[j % 2][:, 0:T], DH ** -0.5).then_inc(mm_empty[j % 2], 1)
                for m in range(4):
                    j = DA_K[m]
                    if m < 3:
                        hi_of_tile(l, 4 + m + 1)
                    wait_mm_full(act, l, j)
                    copy(da_k[:, m, 0:NLAT], mm[j % 2][:, 0:NLAT])
                    copy(da_k[:, m, T:KEYS], mm[j % 2][:, NLAT:T]).then_inc(mm_empty[j % 2], 1)
                wait_mm_read(act, l, MM["da_v"] + TT - 1)
                act.dma_start(a["new_da_v"][0, l].rearrange("t h d -> t (h d)"), da_v[:, PRT + 1, :]).then_inc(v_sent, 16)
                wait_t_full(act, l, TR["da_new"])
                copy(new_out[:, :], tp[:, 0:512]).then_inc(t_empty, 1)
                wait_t_read(act, l, TR["da_new"])
                act.dma_start(a["new_da_k"][0, l].rearrange("t h d -> t (h d)"), new_out[:, :]).then_inc(new_sent, 16)

                def turn_probs(l, j, i, n):
                    wait_t_full(act, l, j)
                    copy(pt[:, i % 2, 0:n * P], tp[:, 0:n * P]).then_inc(t_empty, 1)

                def turn_out_da(t):
                    wait_t_full(act, l, TR["da"] + DA_TO[t])
                    copy(da_q[:, :, t * P:(t + 1) * P], tp[:, 0:512].rearrange("p (m t) -> p m t", m=4),
                         lam[:, 7:8]).then_inc(t_empty, 1)

                def keep_squares(i):
                    o = OO["da"] + i
                    wait_o_full(act, l, o)
                    act.activation(rstd[:, 0:P], oo[o % 2][:, 0:P], ACT.Square, accum_out=da_ss[:, i:i + 1])
                    act.drain()
                    act.sem_inc(ss_ready, 1)

                for s in range(DA_N + 3):
                    if 2 <= s < DA_N + 2:
                        turn_probs(l, TR["da"] + DA_TP[s - 2], s - 2, 5 if (s - 2) // DA_H < LT else 1)
                    if s >= 3:
                        keep_squares(s - 3)
                    if s < DA_N:
                        width = T if s // DA_H < LT else P
                        for m in range(2):
                            j = MM["da_s"] + 2 * s + m
                            exps(l, 0, 2 * s + m, j, da_p[s % 2][m][:, 0:width], width, 2 * (s % 4) + m)
                            act.drain()
                            act.sem_inc(mm_empty[j % 2], 1)
                hi_of_tile(l, H_AT["da_gate"])
                act.wait_ge(rs_ln, l + 1)
                act.activation(da_r0, da_ss, ACT.Ln)
                act.drain()
                act.activation(da_r0, da_r0, ACT.Exp, scale=-0.5).then_inc(rs_done, 1)
                gates(l, MM["da_out"], lambda: [turn_out_da(t) for t in range(TT)], H_AT["da_gate"])

                act.wait_ge(merged_ready, l * 3 + 1)
                act.wait_ge(v_sent, l * 32 + 16)
                wait_t_full(act, l, TR["mla_ctx"])
                copy(ckv[:, NLAT:T], tp[:, 0:P])
                copy(ml_k[0][MNOPE:MQ, NLAT:T], tp[MNOPE:MQ, P:2 * P]).then_inc(t_empty, 1)
                for m in range(2):
                    j = MM["mla_in"] + m
                    hi_of_tile(l, H_AT["mla_in"] + m + 1)
                    wait_mm_full(act, l, j)
                    copy(cq[:, m, :], mm[j % 2][:, 0:T]).then_inc(mm_empty[j % 2], 1)
                j = MM["mla_in"] + 2
                hi_of_tile(l, H_AT["mla_in"] + 3)
                wait_mm_full(act, l, j)
                copy(ckv[:, 0:NLAT], mm[j % 2][:, 0:NLAT])
                copy(ckv[:, T:KEYS], mm[j % 2][:, NLAT:T]).then_inc(mm_empty[j % 2], 1)
                j = MM["mla_in"] + 3
                hi_of_tile(l, H_AT["sw_q"])
                wait_mm_full(act, l, j)
                copy(ml_k[0][MNOPE:MQ, 0:NLAT], mm[j % 2][MNOPE:MQ, 0:NLAT])
                copy(ml_k[0][MNOPE:MQ, T:KEYS], mm[j % 2][MNOPE:MQ, NLAT:T]).then_inc(mm_empty[j % 2], 1)
                act.drain()
                squares(l, 2, KT, KT - 1, lambda k: cq[:, k, :])

                def sw_q_in(m):
                    j = SW_Q[m]
                    if m < 3:
                        hi_of_tile(l, H_AT["sw_q"] + m + 1)
                    wait_mm_full(act, l, j)
                    copy(sw_q[:, m, :], mm[j % 2][:, 0:T], DH ** -0.5).then_inc(mm_empty[j % 2], 1)

                sw_q_in(0)
                first_rstd(l, 1)
                act.wait_ge(c_normed, l * 2 + 1)
                act.activation(tmp[0][:, 0:NLAT], ckv[:, 0:NLAT], ACT.Square)
                act.activation(tmp[0][:, NLAT:T], ckv[:, T:KEYS], ACT.Square).then_inc(sq_ready, 1)
                sw_q_in(1)
                first_rstd(l, 2)
                sw_q_in(2)
                sw_q_in(3)
                for t in range(KEY_TILES):
                    j = MM["mla_v"] + t
                    wait_mm_full(act, l, j)
                    copy(ml_v[:, t, :], mm[j % 2][:, 0:512]).then_inc(mm_empty[j % 2], 1)
                wait_t_full(act, l, TR["mla_new"])
                act.wait_ge(new_sent, l * NEW_STORES * 16 + 16)
                copy(new_out[:, 0:P + MROPE], tp[:, 0:P + MROPE]).then_inc(t_empty, 1)
                wait_t_read(act, l, TR["mla_new"])
                act.dma_start(a["new_mla_ckv"][0, l], new_out[:, 0:P]).then_inc(new_sent, 16)
                act.dma_start(a["new_mla_krope"][0, l], new_out[:, P:P + MROPE]).then_inc(new_sent, 16)

                def head_in(hd, piece):
                    j = mla_prep(hd, piece)
                    wait_mm_full(act, l, j)
                    if piece == 0:
                        copy(ml_q[hd % 2][0:MQ, :], mm[j % 2][0:MQ, 0:T], MQ ** -0.5).then_inc(mm_empty[j % 2], 1)
                    else:
                        copy(ml_k[hd % 2][0:MNOPE, :], mm[j % 2][0:MNOPE, 0:KEYS]).then_inc(mm_empty[j % 2], 1)

                head_in(0, 0)
                head_in(0, 1)
                for s in range(MLA_N + 2):
                    if s < MLA_N:
                        hd, t = divmod(s, TT)
                        if 1 <= t <= 2 and hd < MH - 1:
                            head_in(hd + 1, t - 1)
                        width = T if t < LT else P
                        j = mla_s(s)
                        if 1 <= s and s % 2 == 0:
                            turn_probs(l, TR["mla"] + MLA_TP[s - 1], s - 1, 5 if (s - 1) % TT < LT else 1)
                        exps(l, 2 * DA_N, s, j, ml_p[s % 2][:, 0:width], width, s % 8)
                        act.drain()
                        act.sem_inc(mm_empty[j % 2], 1)
                    elif s % 2 == 0 and s <= MLA_N:
                        turn_probs(l, TR["mla"] + MLA_TP[s - 1], s - 1, 5 if (s - 1) % TT < LT else 1)

                def mla_turned():
                    for t in range(TT):
                        wait_t_full(act, l, TR["mla"] + MLA_TO[t])
                        copy(ml_o[:, :, t * P:(t + 1) * P],
                             tp[:, 0:512].rearrange("p (m t) -> p m t", m=4)).then_inc(t_empty, 1)

                wait_o_full(act, l, OO["mla"] + MLA_N - 1)
                hi_of_tile(l, H_AT["mla_gate"])
                gates(l, MM["mla_out"], mla_turned, H_AT["mla_gate"])

                act.wait_ge(merged_ready, l * 3 + 2)
                wait_t_full(act, l, TR["sw_ctx"])
                copy(sw_kraw[:, NLAT:T], tp[:, 0:P]).then_inc(t_empty, 1)
                j = SW_K
                hi_of_tile(l, H_AT["sw_kv"] + 1)
                wait_mm_full(act, l, j)
                copy(sw_kraw[:, 0:NLAT], mm[j % 2][:, 0:NLAT])
                copy(sw_kraw[:, T:KEYS], mm[j % 2][:, NLAT:T]).then_inc(mm_empty[j % 2], 1)
                j = SW_V
                wait_mm_full(act, l, j)
                copy(sw_vraw, mm[j % 2][:, 0:T]).then_inc(mm_empty[j % 2], 1)
                wait_t_full(act, l, TR["sw_vt"])
                copy(sw_v[:, 0:LT, :], tp[:, 0:NLAT].rearrange("p (t c) -> p t c", c=P))
                copy(sw_v[:, PRT + 1, :], tp[:, NLAT:T]).then_inc(t_empty, 1)
                wait_t_read(act, l, TR["sw_vt"])
                act.dma_start(a["new_swa_v"][0, l].rearrange("t h d -> t (h d)"), sw_v[:, PRT + 1, :]).then_inc(v_sent, 16)
                wait_t_full(act, l, TR["sw_new"])
                act.wait_ge(new_sent, l * NEW_STORES * 16 + 48)
                copy(new_out[:, 0:P], tp[:, 0:P]).then_inc(t_empty, 1)
                wait_t_read(act, l, TR["sw_new"])
                act.dma_start(a["new_swa_k"][0, l].rearrange("t h d -> t (h d)"), new_out[:, 0:P]).then_inc(new_sent, 16)

                def win_tiles(t):
                    return 1 if t == PRT else min(t + 1, LT - 1) - max(t - 1, 0) + 2

                for s in range(SW_N + 2):
                    if s < SW_N:
                        t, hd = divmod(s, SW_H)
                        width = win_tiles(t) * P
                        j = MM["sw_s"] + s
                        if 1 <= s and s % 2 == 0:
                            turn_probs(l, TR["sw"] + SW_TP[s - 1], s - 1, win_tiles((s - 1) // SW_H))
                        exps(l, 2 * DA_N + MLA_N, s, j, sw_p[s % 2][:, 0:width], width, hd)
                        act.drain()
                        act.sem_inc(mm_empty[j % 2], 1)
                        if hd == SW_H - 1:
                            act.wait_ge(sink_in, l * TT + (t + 1))
                            act.activation(stat[:, 40:48], stat[:, 32:40], ACT.Exp).then_inc(sink_e, 1)
                    elif s % 2 == 0 and s <= SW_N:
                        turn_probs(l, TR["sw"] + SW_TP[s - 1], s - 1, win_tiles((s - 1) // SW_H))
                    for t in range(TT):
                        if s == SW_H * (t + 1) + 3:
                            wait_t_full(act, l, TR["sw"] + SW_TO[t])
                            copy(sw_q[:, :, t * P:(t + 1) * P],
                                 tp[:, 0:512].rearrange("p (m t) -> p m t", m=4)).then_inc(t_empty, 1)

                def sw_turned():
                    wait_t_full(act, l, TR["sw"] + SW_TO[PRT])
                    copy(sw_q[:, :, PRT * P:T], tp[:, 0:512].rearrange("p (m t) -> p m t", m=4)).then_inc(t_empty, 1)

                wait_o_full(act, l, OO["sw"] + SW_N - 1)
                hi_of_tile(l, H_AT["sw_gate"])
                gates(l, MM["sw_out"], sw_turned, H_AT["sw_gate"])

                act.wait_ge(new_sent, l * NEW_STORES * 16 + NEW_STORES * 16)
                squares_of_x(l, KT + 3, KT, lambda k: wait_mm_read(act, l, MM["o"] + k))
                first_rstd(l, 3)
                shifts(l, 1, 24)
                act.wait_ge(lg_ready, l + 1)
                act.activation(aff[:, :, :], aff[:, :, :], ACT.Exp).then_inc(lg_e, 1)
                for t in range(TT):
                    wait_t_full(act, l, TR["h_tok"] + t)
                    copy(tok[:, t, :], tp[:, :]).then_inc(t_empty, 1)
                for g in range(2):
                    j = MM["gather_p"] + g
                    wait_mm_full(act, l, j)
                    copy(xe_p[:, 4 * g:4 * g + 4, :],
                         mm[j % 2][:, :].rearrange("p (k s) -> p k s", k=4)).then_inc(mm_empty[j % 2], 1)
                wait_t_full(act, l, TR["hot_p"])
                copy(hotw_pt.rearrange("p g s -> p (g s)"), tp[:, 0:2 * P]).then_inc(t_empty, 1)

                def hi_of_chunk(n, e, last_pair=False):
                    i = N_DENSE + n
                    for u in range(UNITS):
                        m = UNITS * n + u
                        p = m - SPLITS
                        if p >= 0:
                            if p % JOB_UNITS == JOB_UNITS - 1:
                                wait_mm_full(act, l, job_turn(p // JOB_UNITS, last_pair), e)
                            else:
                                act.wait_ge(w_used, pair_used(l, e, p))
                        if u == 0:
                            act.wait_ge(slot_in[i % RING], 16 * chunk_use(l, i, e))
                        copy(w_hi[m % SPLITS][:, :, :], ring[i % RING][:, u * UK:(u + 1) * UK, :])\
                            .then_inc(w_hi_ready, 1)

                def hi_of_tokens(turn, g, e):
                    wait_mm_full(act, l, turn, e)
                    v = mm[turn % 2][:, 0:512].rearrange("p (k s) -> p k s", k=4)
                    copy(x_hi[0][:, 4 * g:4 * g + 4, LAT_OF[0]], v[:, :, 0:CAP_L])
                    copy(x_hi[1][:, 4 * g:4 * g + 4, LAT_OF[1]], v[:, :, CAP_L:]).then_inc(xhi_ready, 1)

                def hi_of_prompt(of):
                    for half in range(2):
                        last = copy(x_hi[half][:, :, PR_OF[half]],
                                    xe_p[:, :, bass.ds(CAP_P * (2 * of + half), CAP_P)])
                    last.then_inc(xhi_ready, 1)

                def silu(q, e, last_pair):
                    j = job_turn(q, last_pair)
                    rows_ = ROWS_OF[q // 2]
                    wait_mm_full(act, l, j, e)
                    act.activation(tmp[q % 2][0:rows_, 0:512], mm[j % 2][0:rows_, 0:512], ACT.Silu)\
                        .then_inc(silu_out, 1)

                def hi_of_hidden(q, turn, e):
                    rows_ = ROWS_OF[q // 2]
                    n = q % 2
                    wait_t_full(act, l, turn, e)
                    copy(hid_hi[:, 4 * n:4 * n + 4, 0:rows_],
                         tp[:, 0:512].rearrange("p (k s) -> p k s", k=4)[:, :, 0:rows_]).then_inc(hid_hi_ready, 1)

                def outputs(q, e, last_pair):
                    half = q - AO
                    j = job_turn(q, last_pair)
                    wait_mm_full(act, l, j, e)
                    if half == 0:
                        act.wait_ge(ye_stored, 32 * (l * PAIRS + e) + 32)
                    copy(ye_pr[PR_OF[half], :], mm[j % 2][PR_OF[half], :])
                    copy(ye_hi[LAT_OF[half], :], mm[j % 2][LAT_OF[half], :], aff_slot[LAT_OF[half], :])\
                        .then_inc(ye_hi_ready, 1)
                    act.drain()
                    act.dma_start(a["ye_pr"][2 * e + half], ye_pr[PR_OF[half], :]).then_inc(ye_stored, 16)

                def pair(e, before=None, last_pair=False):
                    m0, t0 = MM["pairs"] + 2, TR["pairs"]
                    for n in range(2, PAIR_CHUNKS if last_pair else PAIR_CHUNKS + 2):
                        hi_of_chunk(n, e, last_pair)
                        if n == 2 and before is not None:
                            outputs(BO, before, False)
                        if n == 5:
                            silu(AF0, e, last_pair)
                        if n == 9:
                            silu(AF1, e, last_pair)
                            hi_of_hidden(AF0, t0, e)
                            act.activation(hotw[:, :, :, :].rearrange("p t a s -> p (t a s)"), tp[:, NLAT:2 * NLAT],
                                           ACT.Copy, accum_out=aff_slot).then_inc(aff_slot_ready, 1)
                        if n == 13:
                            silu(BF0, e, last_pair)
                            hi_of_hidden(AF1, t0 + 1, e)
                        if n == 17:
                            silu(BF1, e, last_pair)
                        if n == 21:
                            hi_of_hidden(BF0, t0 + 2, e)
                            outputs(AO, e, last_pair)
                            if not last_pair:
                                hi_of_tokens(m0 + G0, 0, e)
                            hi_of_hidden(BF1, t0 + 3, e)
                            if not last_pair:
                                hi_of_tokens(m0 + G1, 1, e)
                                hi_of_prompt(e + 1)

                hi_of_chunk(0, 0)
                hi_of_chunk(1, 0)
                hi_of_tokens(MM["pairs"], 0, None)
                hi_of_tokens(MM["pairs"] + 1, 1, None)
                hi_of_prompt(0)
                pair(0)
                with act.Fori(1, PAIRS - 1) as e:
                    act.activation(stat[0:1, 62:63], const[0:1, 0:1], ACT.Silu)
                    pair(e, e - 1)
                pair(PAIRS - 1, PAIRS - 2, True)
                outputs(BO, PAIRS - 1, True)
                act.wait_ge(ye_stored, 32 * PAIRS * l + (32 * PAIRS + 32))
                act.dma_start(ye_ptok, a["ye_pr"].rearrange("e s c -> (e s) c").rearrange("(g p) c -> p g c", p=P))\
                    .then_inc(ye_back, 16)

            act.wait_ge(x_ready, DEPTH * 2 + 1)
            squares_of_x(DEPTH, 0, 0, lambda k: None)
            first_rstd(DEPTH, 0)
            for t in range(TT):
                wait_t_full(act, DEPTH, t)
                copy(tok[:, t, :], tp[:, :]).then_inc(t_empty, 1)
            act.drain()
            act.sem_inc(y_ready, 2)

        @block.vector
        def _(dve):
            def tt(out, in0, in1, op):
                return dve.tensor_tensor(out, in0, in1, op)

            def ts(out, in0, s1, op0, s2=None, op1=None):
                if op1 is None:
                    return dve.tensor_scalar(out, in0, s1, None, op0)
                return dve.tensor_scalar(out, in0, s1, s2, op0, op1)

            def stt(out, in0, s, in1, op0, op1):
                return dve.scalar_tensor_tensor(out=out, in0=in0, scalar=s, in1=in1, op0=op0, op1=op1)

            groups = ((0, NLAT, 0), (NLAT, T, 1))

            def refine_rstd(l, turn, n, width):
                wait_mm_full(dve, l, turn)
                ts(tmp[2][:, :], mm[turn % 2][:, 0:T], 1.0 / width, ALU.mult, EPS, ALU.add).then_inc(var_ready, 1)
                dve.drain()
                dve.sem_inc(mm_empty[turn % 2], 1)
                dve.wait_ge(r0_ready, l * PER_LAYER["r0_ready"] + (n + 1))
                tt(tmp[2][:, :], tmp[2][:, :], rstd[:, :], ALU.mult)
                dve.drain()
                tt(tmp[2][:, :], tmp[2][:, :], rstd[:, :], ALU.mult)
                dve.drain()
                ts(tmp[2][:, :], tmp[2][:, :], -0.5, ALU.mult, 1.5, ALU.add)
                dve.drain()
                tt(rstd[:, :], rstd[:, :], tmp[2][:, :], ALU.mult)
                dve.drain()

            def add_squares(l, k, sq0):
                dve.wait_ge(sq_ready, l * PER_LAYER["sq_ready"] + (sq0 + k + 1))
                tt(tmp[2][:, :], tmp[2][:, :], tmp[k % 2][:, :], ALU.add).then_inc(sq_used, 1)
                dve.drain()
                if k == KT - 1:
                    dve.sem_inc(sum_ready, 1)

            def scale_h(n):
                for k in range(KT):
                    for lo, hi, g in groups:
                        last = stt(h[:, k, lo:hi], x[:, k, lo:hi], gain[:, n, k, g:g + 1], rstd[:, lo:hi],
                                   ALU.mult, ALU.mult)
                    last.then_inc(scaled, 1)

            def rope(l, j, dst, rows_, cos, sin, t_):
                wait_mm_full(dve, l, j)
                tt(t_[rows_, 0:NLAT], mm[j % 2][rows_, 0:NLAT], sin, ALU.mult).then_inc(mm_empty[j % 2], 1)
                tt(dst, dst, cos, ALU.mult)
                dve.drain()
                return tt(dst, dst, t_[rows_, 0:NLAT], ALU.add)

            def lo_of_tile(l, q):
                _, chunk, c0, width = H_TILES[q]
                for half in range(2):
                    u = 2 * q + half
                    dve.wait_ge(dw_hi_ready, l * 2 * H_N + (u + 1))
                    tt(dw_lo[u % 2][:, :, 0:width], ring[(chunk + half) % RING][:, :, c0:c0 + width],
                       dw_hi[u % 2][:, :, 0:width].bitcast(FP32), ALU.subtract).then_inc(dw_ready, 1)

            def merge(l, turn, first, q0):
                for m in range(KT):
                    t_ = tmp[m % 2]
                    if q0 + m + 1 < H_N:
                        lo_of_tile(l, q0 + m + 1)
                    wait_mm_read(dve, l, turn + 2 * m)
                    ts(t_[:, :], t_[:, :], 1.0, ALU.add)
                    dve.drain()
                    dve.reciprocal(t_[:, :], t_[:, :])
                    dve.drain()
                    j = turn + 2 * m + 1
                    wait_mm_full(dve, l, j)
                    if first:
                        tt(merged[:, m, :], mm[j % 2][:, 0:T], t_[:, :], ALU.mult)
                    else:
                        tt(t_[:, :], mm[j % 2][:, 0:T], t_[:, :], ALU.mult)
                        dve.drain()
                        tt(merged[:, m, :], merged[:, m, :], t_[:, :], ALU.add)
                    dve.drain()
                    dve.sem_inc(mm_empty[j % 2], 1)
                dve.sem_inc(merged_ready, 1)

            def neg_max(l, j, width, at):
                wait_mm_full(dve, l, j)
                return dve.tensor_reduce(stat[:, at:at + 1], mm[j % 2][:, 0:width], AX.X, ALU.max, negate=True)

            def turn_probs(l, j, i, n):
                wait_t_full(dve, l, j)
                dve.tensor_copy(pt[:, i % 2, 0:n * P], tp[:, 0:n * P]).then_inc(t_empty, 1)

            for t in range(TT):
                dve.wait_ge(t_full, t + 1)
                dve.tensor_copy(x[:, :, t * P:(t + 1) * P],
                                tp[:, :].rearrange("p (k t) -> p k t", k=KT)).then_inc(t_empty, 1)
            dve.memset(ctx_in[:, :], 0.0)
            dve.drain()
            dve.sem_inc(x_ready, 1)
            dve.sem_inc(layer_free, 1)

            with dve.Fori(0, DEPTH) as l:
                wait_t_full(dve, l, TR["cols"])
                dve.tensor_copy(cols[:, :], tp[:, 0:NROWS])
                dve.drain()
                dve.sem_inc(t_empty, 1)
                dve.sem_inc(cols_ready, 1)
                dve.wait_ge(silu_e, l + 1)
                ts(silu_t[:, :], silu_t[:, :], 1.0, ALU.add)
                dve.drain()
                dve.reciprocal(silu_t[:, :], silu_t[:, :])
                dve.drain()
                for g, name in enumerate(("c", "c_ctx")):
                    lo, hi = ROWS[name]
                    tt(silu_t[:, g * KT:(g + 1) * KT], silu_t[:, g * KT:(g + 1) * KT], cols[:, lo:hi], ALU.mult)
                dve.drain()
                silu_v = silu_t[:, :].rearrange("p (g k) -> p k g", g=2)
                dve.tensor_copy(c_hi[:, :, :], silu_v)
                dve.drain()
                tt(c_lo[:, :, :], silu_v, c_hi[:, :, :].bitcast(FP32), ALU.subtract).then_inc(silu_ready, 1)
                tt(bc[:, 0:DH], bc[:, 0:DH], bc[:, DH:2 * DH], ALU.mult)
                tt(bc[:, 2 * DH:3 * DH], bc[:, 2 * DH:3 * DH], bc[:, 3 * DH:4 * DH], ALU.mult)
                dve.drain()
                dve.tensor_reduce(lam[:, 0:2], bc[:, 0:4 * DH].rearrange("p (g d) -> p g d", g=2)[:, :, 0:DH],
                                  AX.X, ALU.add).then_inc(lam_e, 1)
                dve.wait_ge(lam_e_done, l + 1)
                tt(lam[:, 4:5], lam[:, 3:4], lam[:, 2:3], ALU.subtract)
                dve.drain()
                tt(lam[:, 5:6], lam[:, 4:5], bc[:, 4 * DH + SW_H:4 * DH + SW_H + 1], ALU.subtract)
                tt(lam[:, 7:8], col("subln"), bc[:, 4 * DH + SW_H + 1:4 * DH + SW_H + 2], ALU.mult)
                for m in range(ADA_UNITS):
                    if m == ADA_JOB * (NORM1_AT - 2):
                        for k in range(1, KT):
                            add_squares(l, k, 0)
                    if m == ADA_JOB * (NORM1_AT + 2):
                        refine_rstd(l, MM["norm1"], 0, D)
                    i, u = divmod(m, UNITS)
                    dve.wait_ge(w_hi_ready, ada_part(l, m))
                    tt(w_lo[m % SPLITS][:, :, :], ring[i % RING][:, u * UK:(u + 1) * UK, :],
                       w_hi[m % SPLITS][:, :, :].bitcast(FP32), ALU.subtract).then_inc(w_ready, 1)
                b0 = ROWS["b_ada"][0]
                wait_t_full(dve, l, TR["ada"])
                tt(mod[:, :, :], tp[:, 0:96].rearrange("p (m g) -> p m g", g=2),
                   cols[:, b0:b0 + 48].unsqueeze(2).to_broadcast([P, 48, 2]), ALU.add).then_inc(t_empty, 1)
                dve.drain()
                for n, name in enumerate(("norm1", "norm2")):
                    lo, hi = ROWS[name]
                    for g in range(2):
                        stt(gain[:, n, :, g], mod[:, 24 * n + 8:24 * n + 16, g], 1.0, cols[:, lo:hi],
                            ALU.add, ALU.mult)
                dve.drain()
                scale_h(0)
                dve.wait_ge(x_spilled, l * 16 + 16)
                lo_of_tile(l, 0)
                wait_mm_full(dve, l, MM["da_v"] + TT - 1)
                for k in range(KT):
                    dve.wait_ge(h_hi_ready, l * KT + (k + 1))
                    tt(h_lo[:, k, 0:NLAT], h[:, k, 0:NLAT], h_hi[:, k, :].bitcast(FP32), ALU.subtract)\
                        .then_inc(h_lo_ready, 1)
                for q in range(1, 5):
                    lo_of_tile(l, q)

                for m in range(8):
                    dst = da_q[:, m, 0:NLAT] if m < 4 else da_k[:, m - 4, 0:NLAT]
                    last = rope(l, DA_ROT[m], dst, slice(0, P), c_("cos64"), c_("sin64"), tmp[m % 2])
                    if m < 3:
                        lo_of_tile(l, H_AT["da_k"] + m + 1)
                last.then_inc(da_roped, 1)

                def mix(i):
                    width = T if i // DA_H < LT else P
                    s0 = 16 + 2 * (i % 4)
                    for m in range(2):
                        wait_mm_read(dve, l, MM["da_s"] + 2 * i + m)
                    dve.reciprocal(stat[:, s0:s0 + 2], stat[:, s0:s0 + 2])
                    dve.drain()
                    p1, p2 = da_p[i % 2][0][:, 0:width], da_p[i % 2][1][:, 0:width]
                    ts(p2, p2, stat[:, s0 + 1:s0 + 2], ALU.mult, lam[:, 5:6], ALU.mult)
                    dve.drain()
                    stt(p1, p1, stat[:, s0:s0 + 1], p2, ALU.mult, ALU.add).then_inc(p_mixed, 1)

                def da_keep(i):
                    t, hd = divmod(i, DA_H)
                    o = OO["da"] + i
                    dve.wait_ge(ss_ready, l * DA_N + (i + 1))
                    dve.tensor_copy(da_o[:, t, hd * P:(hd + 1) * P], oo[o % 2][:, 0:P]).then_inc(o_empty[o % 2], 1)

                for s in range(DA_N + 3):
                    if s < DA_N:
                        for m in range(2):
                            neg_max(l, MM["da_s"] + 2 * s + m, T if s // DA_H < LT else P, 2 * (s % 4) + m)\
                                .then_inc(nm_ready, 1)
                    if 1 <= s <= DA_N:
                        mix(s - 1)
                    if s >= 3:
                        da_keep(s - 3)
                lo_of_tile(l, H_AT["da_gate"])
                ts(da_ss, da_ss, 1.0 / P, ALU.mult, EPS, ALU.add).then_inc(rs_ln, 1)
                dve.drain()
                dve.wait_ge(rs_done, l + 1)
                tt(da_ss, da_ss, da_r0, ALU.mult)
                dve.drain()
                tt(da_ss, da_ss, da_r0, ALU.mult)
                dve.drain()
                ts(da_ss, da_ss, -0.5, ALU.mult, 1.5, ALU.add)
                dve.drain()
                tt(da_r0, da_r0, da_ss, ALU.mult)
                dve.drain()
                for t in range(TT):
                    o_ = da_o[:, t, :].rearrange("p (h d) -> p h d", h=DA_H)
                    r_ = da_r0[:, t * DA_H:(t + 1) * DA_H]
                    tt(o_, o_, r_.unsqueeze(2).to_broadcast([P, DA_H, P]), ALU.mult).then_inc(o_ready, 1)
                merge(l, MM["da_out"], True, H_AT["da_gate"])

                for q in range(1, 6):
                    lo_of_tile(l, H_AT["mla_in"] + q)
                refine_rstd(l, MLA_NORM[0], 1, QR)
                for m in range(2):
                    last = stt(cq[:, m, :], cq[:, m, :], col("q_norm", m), rstd[:, :], ALU.mult, ALU.mult)
                last.then_inc(c_normed, 1)
                dve.drain()
                lo_of_tile(l, H_AT["sw_q"] + 2)
                refine_rstd(l, MLA_NORM[1], 2, KVR)
                lo_of_tile(l, H_AT["sw_q"] + 3)
                stt(ckv[:, 0:NLAT], ckv[:, 0:NLAT], col("kv_norm"), rstd[:, 0:NLAT], ALU.mult, ALU.mult)
                stt(ckv[:, T:KEYS], ckv[:, T:KEYS], col("kv_norm"), rstd[:, NLAT:T], ALU.mult, ALU.mult)\
                    .then_inc(c_normed, 1)
                r32 = slice(MNOPE, MQ)
                wait_t_read(dve, l, TR["mla_ctx"])
                rope(l, MM["kr_rot"], ml_k[0][r32, 0:NLAT], r32, c_("cos32", r32), c_("sin32", r32),
                     tmp[MM["kr_rot"] % 2])
                dve.drain()
                dve.tensor_copy(ml_k[1][r32, :], ml_k[0][r32, :]).then_inc(kr_ready, 1)

                def rope_head(hd, part):
                    j = mla_prep(hd, 2)
                    t_, q_ = tmp[j % 2][r32, 0:NLAT], ml_q[hd % 2][r32, 0:NLAT]
                    if part == 0:
                        wait_mm_full(dve, l, j)
                        tt(t_, mm[j % 2][r32, 0:NLAT], c_("sin32", r32), ALU.mult).then_inc(mm_empty[j % 2], 1)
                    else:
                        tt(q_, q_, c_("cos32", r32), ALU.mult)
                        dve.drain()
                        tt(q_, q_, t_, ALU.add).then_inc(mq_roped, 1)

                def mla_keep(i):
                    hd, t = divmod(i, TT)
                    o = OO["mla"] + i
                    s0 = 16 + i % 8
                    dve.reciprocal(stat[:, s0:s0 + 1], stat[:, s0:s0 + 1])
                    dve.drain()
                    wait_o_full(dve, l, o)
                    ts(ml_otok[:, t, hd * MV:(hd + 1) * MV], oo[o % 2][:, 0:MV], stat[:, s0:s0 + 1], ALU.mult)\
                        .then_inc(o_empty[o % 2], 1)

                rope_head(0, 0)
                rope_head(0, 1)
                for s in range(MLA_N + 2):
                    if s < MLA_N:
                        hd, t = divmod(s, TT)
                        turned = t == 3 and hd < MH - 1
                        if turned:
                            rope_head(hd + 1, 0)
                        neg_max(l, mla_s(s), T if t < LT else P, s % 8).then_inc(nm_ready, 1)
                        if turned:
                            rope_head(hd + 1, 1)
                    if 1 <= s <= MLA_N and s % 2 == 1:
                        turn_probs(l, TR["mla"] + MLA_TP[s - 1], s - 1, 5 if (s - 1) % TT < LT else 1)
                    if s >= 2:
                        wait_mm_read(dve, l, mla_s(s - 2))
                        mla_keep(s - 2)
                dve.drain()
                dve.sem_inc(o_ready, TT)
                lo_of_tile(l, H_AT["mla_gate"])
                merge(l, MM["mla_out"], False, H_AT["mla_gate"])

                for m in range(5):
                    dst = sw_q[:, m, 0:NLAT] if m < 4 else sw_kraw[:, 0:NLAT]
                    rope(l, SW_ROT[m], dst, slice(0, P), c_("cos64"), c_("sin64"), tmp[m % 2])
                    if m == 1:
                        lo_of_tile(l, H_AT["sw_kv"] + 1)
                dve.drain()
                wait_t_read(dve, l, TR["sw_ctx"])
                for g in range(2):
                    for half in range(2):
                        last = dve.tensor_copy(sw_k[half * DH:(half + 1) * DH, g, :], sw_kraw[g * DH:(g + 1) * DH, :])
                last.then_inc(sw_roped, 1)
                sinks = bc[:, 4 * DH:4 * DH + SW_H]
                ts(stat[:, 48:56], sinks, -1.0, ALU.mult)
                dve.drain()

                def win_tiles(t):
                    return 1 if t == PRT else min(t + 1, LT - 1) - max(t - 1, 0) + 2

                def sw_keep(i):
                    t, hd = divmod(i, SW_H)
                    o = OO["sw"] + i
                    wait_o_full(dve, l, o)
                    dve.tensor_copy(sw_o[:, t % 2, hd * DH:(hd + 1) * DH], oo[o % 2][:, 0:DH])\
                        .then_inc(o_empty[o % 2], 1)
                    if hd == SW_H - 1:
                        dve.drain()
                        o_ = sw_o[:, t % 2, :].rearrange("p (h d) -> p h d", h=SW_H)
                        r = stat[:, 56:64]
                        tt(o_, o_, r.unsqueeze(2).to_broadcast([P, SW_H, DH]), ALU.mult).then_inc(o_ready, 1)

                for s in range(SW_N + 2):
                    if s < SW_N:
                        t, hd = divmod(s, SW_H)
                        if hd == 0 and t > 0:
                            wait_mm_read(dve, l, MM["sw_s"] + s - 1)
                            dve.wait_ge(sink_e, l * TT + t)
                            tt(stat[:, 56:64], stat[:, 16:24], stat[:, 40:48], ALU.add)
                            dve.drain()
                            dve.reciprocal(stat[:, 56:64], stat[:, 56:64])
                            dve.drain()
                        neg_max(l, MM["sw_s"] + s, win_tiles(t) * P, hd)
                        dve.drain()
                        tt(stat[:, hd:hd + 1], stat[:, hd:hd + 1], stat[:, 48 + hd:49 + hd], ALU.min)
                        dve.drain()
                        dve.sem_inc(nm_ready, 1)
                        if hd == SW_H - 1:
                            tt(stat[:, 32:40], sinks, stat[:, 0:8], ALU.add).then_inc(sink_in, 1)
                    if 1 <= s <= SW_N and s % 2 == 1:
                        turn_probs(l, TR["sw"] + SW_TP[s - 1], s - 1, win_tiles((s - 1) // SW_H))
                    if s == SW_N:
                        wait_mm_read(dve, l, MM["sw_s"] + SW_N - 1)
                        dve.wait_ge(sink_e, l * TT + TT)
                    if s >= 2:
                        if s == SW_N + 1:
                            tt(stat[:, 56:64], stat[:, 16:24], stat[:, 40:48], ALU.add)
                            dve.drain()
                            dve.reciprocal(stat[:, 56:64], stat[:, 56:64])
                        sw_keep(s - 2)
                dve.drain()
                dve.sem_inc(small_free, 1)
                lo_of_tile(l, H_AT["sw_gate"])
                merge(l, MM["sw_out"], False, H_AT["sw_gate"])

                for m in range(KT):
                    if m in (0, 2):
                        dve.wait_ge(x_back[m // 2], l * 16 + 16)
                    j = MM["o"] + m
                    wait_mm_full(dve, l, j)
                    for lo, hi, g in groups:
                        last = stt(x[:, m, lo:hi], mm[j % 2][:, lo:hi], mod[:, 16 + m, g:g + 1], x[:, m, lo:hi],
                                   ALU.mult, ALU.add)
                    last.then_inc(mm_empty[j % 2], 1)
                    if m >= 2:
                        add_squares(l, m - 1, KT + 3)
                add_squares(l, KT - 1, KT + 3)
                dve.sem_inc(x_ready, 1)

                refine_rstd(l, MM["norm2"], 3, D)
                scale_h(1)
                for v in (x_hi[1], x_lo[1]):
                    dve.memset(v[:, :, CAP_P:P - CAP_L].bitcast(FP32), 0.0)
                e16 = slice(0, NE)
                dve.memset(ones_e[e16, :], 1.0)
                j = MM["router"]
                wait_mm_full(dve, l, j)
                dve.tensor_copy(lgt_e[e16, :], mm[j % 2][e16, 0:T]).then_inc(mm_empty[j % 2], 1)
                wait_t_full(dve, l, TR["lg"])
                lg = tp[:, 0:TT * NE].rearrange("p (t e) -> p t e", e=NE)
                dve.tensor_reduce(stat[:, 0:TT], lg, AX.X, ALU.max)
                dve.drain()
                tt(aff[:, :, :], lg, stat[:, 0:TT].unsqueeze(2).to_broadcast([P, TT, NE]), ALU.subtract)\
                    .then_inc(t_empty, 1)
                dve.drain()
                dve.sem_inc(lg_ready, 1)
                dve.wait_ge(lg_e, l + 1)
                dve.tensor_reduce(stat[:, 0:TT], aff[:, :, :], AX.X, ALU.add)
                dve.drain()
                dve.reciprocal(stat[:, 0:TT], stat[:, 0:TT])
                dve.drain()
                tt(aff[:, :, :], aff[:, :, :], stat[:, 0:TT].unsqueeze(2).to_broadcast([P, TT, NE]), ALU.mult)\
                    .then_inc(aff_ready, 1)
                dve.wait_ge(v_sent, l * 32 + 32)
                wait_t_full(dve, l, TR["aff"])
                dve.tensor_copy(work_e[e16, :], tp[e16, 0:T]).then_inc(t_empty, 1)
                dve.drain()
                for lo, hi, rounds in ((0, NLAT, CAP_L // 8), (NLAT, T, CAP_P // 8)):
                    for _ in range(rounds):
                        dve.max(top8[e16, :], work_e[e16, lo:hi])
                        dve.drain()
                        dve.match_replace(work_e[e16, lo:hi], top8[e16, :], work_e[e16, lo:hi], -1.0)
                        dve.drain()
                ts(mask_e[e16, :], work_e[e16, :], 0.0, ALU.is_lt)
                dve.drain()
                for lo, hi, _ in groups:
                    dve.tensor_tensor_scan(cum_e[e16, lo:hi], ones_e[e16, lo:hi], mask_e[e16, lo:hi], 0.0,
                                           ALU.mult, ALU.add)
                dve.drain()
                tt(cum_e[e16, :], cum_e[e16, :], mask_e[e16, :], ALU.mult)
                dve.drain()
                ts(cum_e[e16, :], cum_e[e16, :], -1.0, ALU.add).then_inc(pos_ready, 1)
                wait_t_full(dve, l, TR["pos"])
                dve.tensor_copy(pos_t[:, :, :], tp[:, 0:TT * NE].rearrange("p (t e) -> p t e", e=NE)).then_inc(t_empty, 1)
                dve.drain()
                lo, _ = CONST["iota"]
                tt(hot_p, const[:, lo:lo + CAP_P].unsqueeze(1).to_broadcast([P, NE, CAP_P]),
                   pos_t[:, PRT, :].unsqueeze(2).to_broadcast([P, NE, CAP_P]), ALU.is_equal)
                dve.drain()
                tt(hotw_p, hot_p, aff[:, PRT, :].unsqueeze(2).to_broadcast([P, NE, CAP_P]), ALU.mult)\
                    .then_inc(hotp_ready, 1)

                def f(v):
                    return v.bitcast(FP32)

                def select(of):
                    for half in range(2):
                        last = tt(hot[:, :, half, :], c_("iota").unsqueeze(1).to_broadcast([P, LT, CAP_L]),
                                  pos_t[:, 0:LT, bass.ds(2 * of + half, 1)].to_broadcast([P, LT, CAP_L]),
                                  ALU.is_equal)
                    last.then_inc(hot_ready, 1)

                def weigh(of):
                    for half in range(2):
                        last = tt(hotw[:, :, half, :], hot[:, :, half, :],
                                  aff[:, 0:LT, bass.ds(2 * of + half, 1)].to_broadcast([P, LT, CAP_L]), ALU.mult)
                    last.then_inc(hotw_ready, 1)

                def spread(k, of):
                    j = OO["pairs"] + k
                    wait_o_full(dve, l, j, of)
                    stt(x[:, k, 0:NLAT], oo[j % 2][:, :], mod[:, 40 + k, 0:1], x[:, k, 0:NLAT], ALU.mult, ALU.add)\
                        .then_inc(o_empty[j % 2], 1)

                def outputs(q, e, last_pair):
                    half = q - AO
                    j = job_turn(q, last_pair)
                    rows_ = LAT_OF[half]
                    dve.wait_ge(ye_hi_ready, (l * PAIRS + e) * 2 + (half + 1))
                    stt(ye_lo[rows_, :], mm[j % 2][rows_, :], aff_slot[rows_, :], f(ye_hi[rows_, :]),
                        ALU.mult, ALU.subtract).then_inc(mm_empty[j % 2], 1)
                    if half == 1:
                        dve.drain()
                        dve.sem_inc(ye_done, 1)

                def lo_of_chunk(n, e, before=None):
                    i = N_DENSE + n
                    for u in range(UNITS):
                        m = UNITS * n + u
                        if before is not None and 0 <= m - SPLITS - COMBINE_AT < KT:
                            spread(m - SPLITS - COMBINE_AT, before)
                        dve.wait_ge(w_hi_ready, pair_part(l, e, m))
                        tt(w_lo[m % SPLITS][:, :, :], ring[i % RING][:, u * UK:(u + 1) * UK, :],
                           f(w_hi[m % SPLITS][:, :, :]), ALU.subtract).then_inc(w_ready, 1)

                def lo_of_tokens(turn, g, e, of):
                    dve.wait_ge(xhi_ready, (l * PAIRS + of) * 3 + (g + 1))
                    v = mm[turn % 2][:, 0:512].rearrange("p (k s) -> p k s", k=4)
                    for half in range(2):
                        cs = LAT_OF[half]
                        last = tt(x_lo[half][:, 4 * g:4 * g + 4, cs], v[:, :, half * CAP_L:(half + 1) * CAP_L],
                                  f(x_hi[half][:, 4 * g:4 * g + 4, cs]), ALU.subtract)
                    last.then_inc(mm_empty[turn % 2], 1)

                def lo_of_prompt(of):
                    dve.wait_ge(xhi_ready, (l * PAIRS + of) * 3 + 3)
                    for half in range(2):
                        cs = PR_OF[half]
                        last = tt(x_lo[half][:, :, cs], xe_p[:, :, bass.ds(CAP_P * (2 * of + half), CAP_P)],
                                  f(x_hi[half][:, :, cs]), ALU.subtract)
                    dve.drain()
                    dve.sem_inc(xe_ready, 1)

                def hidden(q, e, last_pair):
                    j = job_turn(q, last_pair)
                    rows_ = ROWS_OF[q // 2]
                    n = q % 2
                    dve.wait_ge(silu_out, (l * PAIRS + e) * 4 + (q + 1))
                    tt(hid[0:rows_, n * 512:(n + 1) * 512], mm[j % 2][0:rows_, 512:1024], tmp[n][0:rows_, 0:512],
                       ALU.mult).then_inc(mm_empty[j % 2], 1)
                    dve.drain()
                    dve.sem_inc(hid_ready, 1)

                def lo_of_hidden(q, e):
                    rows_ = ROWS_OF[q // 2]
                    n = q % 2
                    dve.wait_ge(hid_hi_ready, (l * PAIRS + e) * 4 + (q + 1))
                    tt(hid_lo[:, 4 * n:4 * n + 4, 0:rows_],
                       tp[:, 0:512].rearrange("p (k s) -> p k s", k=4)[:, :, 0:rows_],
                       f(hid_hi[:, 4 * n:4 * n + 4, 0:rows_]), ALU.subtract).then_inc(t_empty, 1)

                def pair(e, before=None, last_pair=False):
                    m0, t0 = MM["pairs"] + 2, TR["pairs"]
                    for n in range(2, PAIR_CHUNKS if last_pair else PAIR_CHUNKS + 2):
                        lo_of_chunk(n, e, before)
                        if n == 2 and before is not None:
                            outputs(BO, before, False)
                        if n == 5:
                            hidden(AF0, e, last_pair)
                        if n == 9:
                            hidden(AF1, e, last_pair)
                            dve.wait_ge(aff_slot_ready, l * PAIRS + e + 1)
                            ts(hot_t[:, :], tp[:, NLAT:2 * NLAT], 0.0, ALU.is_gt)
                            lo_of_hidden(AF0, e)
                        if n == 11 and not last_pair:
                            select(e + 1)
                        if n == 15 and not last_pair:
                            dve.drain()
                            weigh(e + 1)
                        if n == 13:
                            hidden(BF0, e, last_pair)
                            lo_of_hidden(AF1, e)
                        if n == 17:
                            hidden(BF1, e, last_pair)
                        if n == 21:
                            lo_of_hidden(BF0, e)
                            outputs(AO, e, last_pair)
                            if not last_pair:
                                lo_of_tokens(m0 + G0, 0, e, e + 1)
                            lo_of_hidden(BF1, e)
                            if not last_pair:
                                lo_of_tokens(m0 + G1, 1, e, e + 1)
                                lo_of_prompt(e + 1)

                select(0)
                dve.drain()
                weigh(0)
                lo_of_chunk(0, 0)
                lo_of_chunk(1, 0)
                lo_of_tokens(MM["pairs"], 0, None, 0)
                lo_of_tokens(MM["pairs"] + 1, 1, None, 0)
                lo_of_prompt(0)
                pair(0)
                with dve.Fori(1, PAIRS - 1) as e:
                    pair(e, e - 1)
                pair(PAIRS - 1, PAIRS - 2, True)
                outputs(BO, PAIRS - 1, True)
                for k in range(KT):
                    spread(k, PAIRS - 1)
                dve.drain()
                j = MM["combine_p"]
                wait_mm_full(dve, l, j)
                for k in range(KT):
                    stt(x[:, k, NLAT:T], mm[j % 2][:, k * P:(k + 1) * P], mod[:, 40 + k, 1:2], x[:, k, NLAT:T],
                        ALU.mult, ALU.add)
                dve.drain()
                for s in (mm_empty[j % 2], x_ready, layer_free):
                    dve.sem_inc(s, 1)

            for k in range(1, KT):
                add_squares(DEPTH, k, 0)
            refine_rstd(DEPTH, 0, 0, D)
            for k in range(KT):
                last = stt(h[:, k, :], x[:, k, :], col("final", k), rstd[:, :], ALU.mult, ALU.mult)
            last.then_inc(h_ready, 1)

        return nc


_INS = ["x_prompt", "x_sample", "cache_da_k", "cache_da_v", "cache_mla_ckv", "cache_mla_krope",
        "cache_swa_k", "cache_swa_v", "c", "c_ctx", "w_ada", "b_ada", "norm1", "norm2", "w_in",
        "da_lq1", "da_lk1", "da_lq2", "da_lk2", "da_subln", "mla_q_norm", "mla_w_qb", "mla_kv_norm",
        "mla_w_kvb", "swa_sink", "w_gate", "w_br_da", "w_br_mla", "w_br_swa", "w_o", "w_router",
        "w_ff1", "w_ff3", "w_ff2", "final_norm"]
_OUTS = [("y_prompt", (1, NPR, D)), ("y_sample", (1, NLAT, D)),
         ("new_da_k", (1, DEPTH, NPR, DA_H, 2 * DH)), ("new_da_v", (1, DEPTH, NPR, DA_H, 2 * DH)),
         ("new_mla_ckv", (1, DEPTH, NPR, KVR)), ("new_mla_krope", (1, DEPTH, NPR, MROPE)),
         ("new_swa_k", (1, DEPTH, NPR, SW_KV, DH)), ("new_swa_v", (1, DEPTH, NPR, SW_KV, DH))]


def kernel(**inputs):
    import concourse.bacc as _bacc
    from concourse.bass_utils import run_bass_kernel_spmd as _run

    nc = _bacc.Bacc("TRN2", target_bir_lowering=False, num_devices=1)
    table, lam = shape_constants()
    arrays, a = {}, {}
    for name, value in [(n, inputs[n]) for n in _INS] + [("const", table), ("lam", lam)]:
        v = np.ascontiguousarray(value)
        arrays[f"in_{name}"] = v
        a[name] = nc.dram_tensor(f"in_{name}", v.shape, mybir.dt.from_np(v.dtype), kind="ExternalInput").ap()
    for name, shape in _OUTS:
        a[name] = nc.dram_tensor(f"out_{name}", shape, FP32, kind="ExternalOutput").ap()
    a["x_spill"] = nc.dram_tensor("x_spill", (P, KT, T), FP32, kind="Internal").ap()
    a["ye_pr"] = nc.dram_tensor("ye_pr_rows", (NE, CAP_P, D), FP32, kind="Internal").ap()
    build(nc, a)
    r = _run(nc, [arrays], core_ids=[0])
    return tuple(r.results[0][f"out_{name}"] for name, _ in _OUTS)
```
